# Optimizing a Trainium2 kernel written in Bass

```python
import math
import jax
import jax.numpy as jnp
from jax import lax
import numpy as np

D_MODEL = 2048
BATCH = 1
SEQ = 256
DEPTH = 2
DEC_BATCH = 8
DEC_SEQ = 1
PAST_LEN = 2048
PAGE_SIZE = 128

RW_HD = 64
RW_W = D_MODEL // 4
RW_HEADS = RW_W // RW_HD
RW_LORA_W = 64
RW_LORA_A = 64
RW_LORA_V = 32
RW_LORA_G = 128
RW_P = 3 * RW_W + RW_LORA_W + RW_LORA_A + RW_LORA_G
RW_GN_EPS = 64e-5
RET_V = 128
RET_QK = 64
RET_W = 3 * D_MODEL // 8
RET_HEADS = RET_W // RET_V
RET_P = 2 * RET_HEADS * RET_QK + 2 * RET_W
ML_V = 128
ML_QK = 64
ML_W = D_MODEL - RW_W - RET_W
ML_HEADS = ML_W // ML_V
ML_P = 2 * ML_HEADS * ML_QK + 2 * ML_W + 2 * ML_HEADS
ML_GATE_CAP = 15.0
MIX_W = RW_W + RET_W + ML_W
P_TOTAL = RW_P + RET_P + ML_P
D_FF = ((8 * D_MODEL + 3 * 256 - 1) // (3 * 256)) * 256
CHUNK = 128
ROPE_BASE = 10000.0
LN_EPS = 1e-5
NORM_EPS = 1e-6
ALPHA = (2 * DEPTH) ** 0.25
BETA = (8 * DEPTH) ** -0.25

kernel_name = 'hymba_rwkv7_retnet_mlstm_step'

def _split(a, sizes):
    return jnp.split(a, [int(s) for s in np.cumsum(sizes)[:-1]], axis=-1)

def _heads(a, h):
    return a.reshape(a.shape[:-1] + (h, a.shape[-1] // h))

def _layernorm(x, g, b):
    xf = x.astype(jnp.float32)
    mu = jnp.mean(xf, -1, keepdims=True)
    var = jnp.mean(jnp.square(xf - mu), -1, keepdims=True)
    return ((xf - mu) * lax.rsqrt(var + LN_EPS) * g + b).astype(x.dtype)

def _rmsnorm_heads(y):
    return y * lax.rsqrt(jnp.mean(jnp.square(y), -1, keepdims=True) + NORM_EPS)

def _shift_prev(p, prev_row):
    return jnp.concatenate([prev_row[:, None, :].astype(p.dtype), p[:, :-1]], axis=1)

def _rotary(x, pos):
    half = x.shape[-1] // 2
    inv = ROPE_BASE ** (-jnp.arange(half, dtype=jnp.float32) / half)
    ang = pos.astype(jnp.float32)[:, None] * inv[None, :]
    cos = jnp.cos(ang)[None, :, None, :]
    sin = jnp.sin(ang)[None, :, None, :]
    x1, x2 = x[..., :half], x[..., half:]
    return jnp.concatenate([x1 * cos - x2 * sin, x1 * sin + x2 * cos], -1)

def _rwkv7_scan(r, lw, k, v, kk, a, s0):
    def step(s, inp):
        r_t, lw_t, k_t, v_t, kk_t, a_t = inp
        sa = jnp.einsum('bhk,bhkv->bhv', kk_t, s)
        s = (jnp.exp(lw_t)[..., None] * s
             - (kk_t * a_t)[..., None] * sa[..., None, :]
             + k_t[..., None] * v_t[..., None, :])
        return s, jnp.einsum('bhk,bhkv->bhv', r_t, s)
    xs = tuple(jnp.moveaxis(t, 1, 0) for t in (r, lw, k, v, kk, a))
    s_fin, ys = lax.scan(step, s0, xs)
    return jnp.moveaxis(ys, 0, 1), s_fin

def _retention_chunked(q, k, v, r0):
    bsz, t_len, h, dk = q.shape
    dv = v.shape[-1]
    L = math.gcd(t_len, CHUNK)
    nc = t_len // L
    lg = jnp.log1p(-jnp.exp2(-5.0 - jnp.arange(h, dtype=jnp.float32)))
    idx = jnp.arange(L, dtype=jnp.float32)
    rel = idx[:, None] - idx[None, :]
    dmask = jnp.where(rel[None] >= 0, jnp.exp(jnp.maximum(rel, 0.0)[None] * lg[:, None, None]), 0.0)
    qc = q.reshape(bsz, nc, L, h, dk)
    kc = k.reshape(bsz, nc, L, h, dk)
    vc = v.reshape(bsz, nc, L, h, dv)
    scores = jnp.einsum('bcihd,bcjhd->bchij', qc, kc) * dmask
    y = jnp.einsum('bchij,bcjhv->bcihv', scores, vc)
    k_end = kc * jnp.exp((L - 1.0 - idx)[:, None] * lg[None, :])[:, :, None]
    kv = jnp.einsum('bcjhd,bcjhv->bchdv', k_end, vc)
    chunk_decay = jnp.exp(L * lg)[None, :, None, None]

    def step(rs, kv_c):
        return chunk_decay * rs + kv_c, rs
    r_fin, r_before = lax.scan(step, r0, jnp.moveaxis(kv, 1, 0))
    r_before = jnp.moveaxis(r_before, 0, 1)
    q_dec = qc * jnp.exp((idx + 1.0)[:, None] * lg[None, :])[:, :, None]
    y = y + jnp.einsum('bcihd,bchdv->bcihv', q_dec, r_before)
    return y.reshape(bsz, t_len, h, dv), r_fin

def _mlstm_chunked(q, k, v, ig, lf, c0, n0, m0):
    bsz, t_len, h, dk = q.shape
    dv = v.shape[-1]
    L = math.gcd(t_len, CHUNK)
    nc = t_len // L
    qc = q.reshape(bsz, nc, L, h, dk)
    kc = k.reshape(bsz, nc, L, h, dk)
    vc = v.reshape(bsz, nc, L, h, dv)
    igc = ig.reshape(bsz, nc, L, h)
    b = jnp.cumsum(lf.reshape(bsz, nc, L, h), axis=2)
    causal = jnp.tril(jnp.ones((L, L), dtype=bool))
    dlog = b[:, :, :, None, :] - b[:, :, None, :, :] + igc[:, :, None, :, :]
    dlog = jnp.where(causal[None, None, :, :, None], dlog, -jnp.inf)
    a_end = b[:, :, -1:, :] - b + igc
    g_tot = b[:, :, -1, :]

    def step(carry, inp):
        c, n, m = carry
        a_c, g_c, k_c, v_c = inp
        m_new = jnp.maximum(g_c + m, jnp.max(a_c, axis=1))
        dec = jnp.exp(g_c + m - m_new)
        kw = k_c * jnp.exp(a_c - m_new[:, None, :])[..., None]
        c_new = dec[..., None, None] * c + jnp.einsum('blhd,blhv->bhdv', kw, v_c)
        n_new = dec[..., None] * n + jnp.sum(kw, axis=1)
        return (c_new, n_new, m_new), (c, n, m)
    to_t = lambda t: jnp.moveaxis(t, 1, 0)
    to_b = lambda t: jnp.moveaxis(t, 0, 1)
    (c_f, n_f, m_f), (c_b, n_b, m_b) = lax.scan(
        step, (c0, n0, m0), (to_t(a_end), to_t(g_tot), to_t(kc), to_t(vc)))
    c_b, n_b, m_b = to_b(c_b), to_b(n_b), to_b(m_b)
    inter = b + m_b[:, :, None, :]
    m_i = jnp.maximum(jnp.max(dlog, axis=3), inter)
    s = jnp.einsum('bcihd,bcjhd->bcijh', qc, kc) * jnp.exp(dlog - m_i[:, :, :, None, :])
    sc = jnp.exp(inter - m_i)
    num = (jnp.einsum('bcijh,bcjhv->bcihv', s, vc)
           + sc[..., None] * jnp.einsum('bcihd,bchdv->bcihv', qc, c_b))
    den = jnp.sum(s, axis=3) + sc * jnp.einsum('bcihd,bchd->bcih', qc, n_b)
    hid = num / jnp.maximum(jnp.abs(den), jnp.exp(-m_i))[..., None]
    return hid.reshape(bsz, t_len, h, dv), c_f, n_f, m_f

def _layer(x, pos, v_first, st, lp):
    f32 = jnp.float32
    bsz, t_len, _ = x.shape
    p = x @ lp['w_in']
    p_rw, p_ret, p_ml = _split(p, [RW_P, RET_P, ML_P])

    p_rw_prev = _shift_prev(p_rw, st['rw_shift'] @ lp['w_in'][:, :RW_P])
    mixed = (p_rw + (p_rw_prev - p_rw) * lp['rw_mu']).astype(f32)
    r, k, v, xw, xa, xg = _split(mixed, [RW_W, RW_W, RW_W, RW_LORA_W, RW_LORA_A, RW_LORA_G])
    w = -jax.nn.softplus(-(lp['rw_w0'] + jnp.tanh(xw) @ lp['rw_w2'])) - 0.5
    a = jax.nn.sigmoid(lp['rw_a0'] + xa @ lp['rw_a2'])
    g = jax.nn.sigmoid(xg) @ lp['rw_g2']
    if v_first is None:
        v_first = v
    else:
        pv = x @ lp['rw_v1']
        pv_prev = _shift_prev(pv, st['rw_shift'] @ lp['rw_v1'])
        xv = (pv + (pv_prev - pv) * lp['rw_vmu']).astype(f32)
        v = v + (v_first - v) * jax.nn.sigmoid(lp['rw_v0'] + xv @ lp['rw_v2'])
    kk = _heads(k * lp['rw_kk'], RW_HEADS)
    kk = kk * lax.rsqrt(jnp.maximum(jnp.sum(jnp.square(kk), -1, keepdims=True), 1e-24))
    k = k * (1.0 + (a - 1.0) * lp['rw_ka'])
    rh, kh, vh, ah = (_heads(t, RW_HEADS) for t in (r, k, v, a))
    y, s_new = _rwkv7_scan(rh, _heads(-jnp.exp(w), RW_HEADS), kh, vh, kk, ah,
                           st['rw_wkv'].astype(f32))
    y_mu = jnp.mean(y, -1, keepdims=True)
    y_var = jnp.mean(jnp.square(y - y_mu), -1, keepdims=True)
    y = ((y - y_mu) * lax.rsqrt(y_var + RW_GN_EPS)).reshape(bsz, t_len, RW_W)
    y = y * lp['rw_lnx_g'] + lp['rw_lnx_b']
    bonus = jnp.sum(rh * kh * _heads(lp['rw_rk'].astype(f32), RW_HEADS), -1, keepdims=True) * vh
    o_rw = (y + bonus.reshape(bsz, t_len, RW_W)) * g

    qr, kr, vr, gr = _split(p_ret.astype(f32), [RET_HEADS * RET_QK] * 2 + [RET_W] * 2)
    qh = _rotary(_heads(qr, RET_HEADS), pos)
    khr = _rotary(_heads(kr, RET_HEADS), pos) * (RET_QK ** -0.5)
    yr, r_new = _retention_chunked(qh, khr, _heads(vr, RET_HEADS), st['ret'].astype(f32))
    o_ret = jax.nn.silu(gr) * _rmsnorm_heads(yr).reshape(bsz, t_len, RET_W)

    qm, km, vm, om, im, fm = _split(p_ml.astype(f32), [ML_HEADS * ML_QK] * 2 + [ML_W] * 2 + [ML_HEADS] * 2)
    ig = ML_GATE_CAP * jnp.tanh((im + lp['ml_ib']) / ML_GATE_CAP)
    lf = jax.nn.log_sigmoid(ML_GATE_CAP * jnp.tanh((fm + lp['ml_fb']) / ML_GATE_CAP))
    hm, c_new, n_new, m_new = _mlstm_chunked(
        _heads(qm, ML_HEADS), _heads(km, ML_HEADS) * (ML_QK ** -0.5), _heads(vm, ML_HEADS), ig, lf,
        st['ml_c'].astype(f32), st['ml_n'].astype(f32), st['ml_m'].astype(f32))
    o_ml = jax.nn.sigmoid(om) * (_rmsnorm_heads(hm).reshape(bsz, t_len, ML_W) * lp['ml_norm'])

    mix = jnp.concatenate([o_rw, o_ret, o_ml], -1).astype(x.dtype) @ lp['w_out']
    x1 = _layernorm(ALPHA * x + mix, lp['ln1_g'], lp['ln1_b'])
    hdn = jax.nn.silu(x1 @ lp['w_gate']) * (x1 @ lp['w_up'])
    x2 = _layernorm(ALPHA * x1 + hdn @ lp['w_down'], lp['ln2_g'], lp['ln2_b'])
    new_st = {
        'rw_shift': x[:, -1].astype(st['rw_shift'].dtype),
        'rw_wkv': s_new.astype(st['rw_wkv'].dtype),
        'ret': r_new.astype(st['ret'].dtype),
        'ml_c': c_new.astype(st['ml_c'].dtype),
        'ml_n': n_new.astype(st['ml_n'].dtype),
        'ml_m': m_new.astype(st['ml_m'].dtype),
    }
    return x2, v_first, new_st

def _zero_state(b, dtype):
    return {
        'rw_shift': jnp.zeros((b, D_MODEL), dtype),
        'rw_wkv': jnp.zeros((b, RW_HEADS, RW_HD, RW_HD), dtype),
        'ret': jnp.zeros((b, RET_HEADS, RET_QK, RET_V), dtype),
        'ml_c': jnp.zeros((b, ML_HEADS, ML_QK, ML_V), dtype),
        'ml_n': jnp.zeros((b, ML_HEADS, ML_QK), dtype),
        'ml_m': jnp.zeros((b, ML_HEADS), dtype),
    }

def setup_inputs(seed: int = 0) -> dict:
    key = jax.random.key(seed)
    ks = iter(jax.random.split(key, 64))
    f32 = jnp.float32

    def nrm(shape, scale=1.0):
        return jax.random.normal(next(ks), shape, f32) * scale

    def uni(shape, lo, hi):
        return jax.random.uniform(next(ks), shape, f32, lo, hi)

    lv = DEPTH - 1
    col_scale = np.ones((P_TOTAL,), np.float32)
    col_scale[2 * RW_W:3 * RW_W] = BETA
    o = RW_P + 2 * RET_HEADS * RET_QK
    col_scale[o:o + RET_W] = BETA
    o = RW_P + RET_P + 2 * ML_HEADS * ML_QK
    col_scale[o:o + ML_W] = BETA
    lin = jnp.linspace(0.0, 1.0, RW_W, dtype=f32)
    return {
        'x_prompt': nrm((BATCH, SEQ, D_MODEL)),
        'x_sample': nrm((DEC_BATCH, DEC_SEQ, D_MODEL)),
        'state_rw_shift': nrm((DEPTH, DEC_BATCH, D_MODEL)),
        'state_rw_wkv': nrm((DEPTH, DEC_BATCH, RW_HEADS, RW_HD, RW_HD), 0.5),
        'state_ret': nrm((DEPTH, DEC_BATCH, RET_HEADS, RET_QK, RET_V)),
        'state_ml_c': nrm((DEPTH, DEC_BATCH, ML_HEADS, ML_QK, ML_V), 0.5),
        'state_ml_n': nrm((DEPTH, DEC_BATCH, ML_HEADS, ML_QK), 0.5),
        'state_ml_m': uni((DEPTH, DEC_BATCH, ML_HEADS), -2.0, 2.0),
        'ln0_g': 1.0 + nrm((D_MODEL,), 0.05),
        'ln0_b': nrm((D_MODEL,), 0.02),
        'w_in': nrm((DEPTH, D_MODEL, P_TOTAL), D_MODEL ** -0.5) * jnp.asarray(col_scale),
        'rw_mu': uni((DEPTH, RW_P), 0.1, 0.9),
        'rw_w0': (-6.5 + 5.0 * lin ** 0.9)[None, :] + nrm((DEPTH, RW_W), 0.1),
        'rw_w2': nrm((DEPTH, RW_LORA_W, RW_W), 0.1),
        'rw_a0': nrm((DEPTH, RW_W), 0.1),
        'rw_a2': nrm((DEPTH, RW_LORA_A, RW_W), 0.1),
        'rw_g2': nrm((DEPTH, RW_LORA_G, RW_W), RW_LORA_G ** -0.5),
        'rw_kk': 0.85 + nrm((DEPTH, RW_W), 0.02),
        'rw_ka': 1.0 + nrm((DEPTH, RW_W), 0.02),
        'rw_rk': -0.04 + nrm((DEPTH, RW_W), 0.02),
        'rw_lnx_g': 1.0 + nrm((DEPTH, RW_W), 0.05),
        'rw_lnx_b': nrm((DEPTH, RW_W), 0.02),
        'rw_v0': 1.0 + nrm((lv, RW_W), 0.1),
        'rw_v1': nrm((lv, D_MODEL, RW_LORA_V), D_MODEL ** -0.5),
        'rw_vmu': uni((lv, RW_LORA_V), 0.1, 0.9),
        'rw_v2': nrm((lv, RW_LORA_V, RW_W), 0.1),
        'ml_ib': -2.0 + nrm((DEPTH, ML_HEADS), 0.1),
        'ml_fb': jnp.linspace(3.0, 6.0, ML_HEADS, dtype=f32)[None, :] + nrm((DEPTH, ML_HEADS), 0.1),
        'ml_norm': 1.0 + nrm((DEPTH, ML_W), 0.05),
        'w_out': nrm((DEPTH, MIX_W, D_MODEL), BETA * MIX_W ** -0.5),
        'ln1_g': 1.0 + nrm((DEPTH, D_MODEL), 0.05),
        'ln1_b': nrm((DEPTH, D_MODEL), 0.02),
        'w_gate': nrm((DEPTH, D_MODEL, D_FF), D_MODEL ** -0.5),
        'w_up': nrm((DEPTH, D_MODEL, D_FF), BETA * D_MODEL ** -0.5),
        'w_down': nrm((DEPTH, D_FF, D_MODEL), BETA * D_FF ** -0.5),
        'ln2_g': 1.0 + nrm((DEPTH, D_MODEL), 0.05),
        'ln2_b': nrm((DEPTH, D_MODEL), 0.02),
    }

def reference(x_prompt, x_sample, state_rw_shift, state_rw_wkv, state_ret, state_ml_c, state_ml_n, state_ml_m,
              ln0_g, ln0_b, w_in, rw_mu, rw_w0, rw_w2, rw_a0, rw_a2, rw_g2, rw_kk, rw_ka, rw_rk,
              rw_lnx_g, rw_lnx_b, rw_v0, rw_v1, rw_vmu, rw_v2, ml_ib, ml_fb, ml_norm, w_out,
              ln1_g, ln1_b, w_gate, w_up, w_down, ln2_g, ln2_b):
    names = ('rw_shift', 'rw_wkv', 'ret', 'ml_c', 'ml_n', 'ml_m')
    layers = []
    for l in range(DEPTH):
        lp = {
            'w_in': w_in[l], 'rw_mu': rw_mu[l], 'rw_w0': rw_w0[l], 'rw_w2': rw_w2[l],
            'rw_a0': rw_a0[l], 'rw_a2': rw_a2[l], 'rw_g2': rw_g2[l], 'rw_kk': rw_kk[l],
            'rw_ka': rw_ka[l], 'rw_rk': rw_rk[l], 'rw_lnx_g': rw_lnx_g[l], 'rw_lnx_b': rw_lnx_b[l],
            'ml_ib': ml_ib[l], 'ml_fb': ml_fb[l], 'ml_norm': ml_norm[l], 'w_out': w_out[l],
            'ln1_g': ln1_g[l], 'ln1_b': ln1_b[l], 'w_gate': w_gate[l], 'w_up': w_up[l],
            'w_down': w_down[l], 'ln2_g': ln2_g[l], 'ln2_b': ln2_b[l],
        }
        if l > 0:
            lp.update(rw_v0=rw_v0[l - 1], rw_v1=rw_v1[l - 1], rw_vmu=rw_vmu[l - 1], rw_v2=rw_v2[l - 1])
        layers.append(lp)

    def run(x, pos, states):
        x = _layernorm(x, ln0_g, ln0_b)
        v_first = None
        new = []
        for l in range(DEPTH):
            x, v_first, st = _layer(x, pos, v_first, states[l], layers[l])
            new.append(st)
        return x, [jnp.stack([st[n] for st in new]) for n in names]

    st_in = (state_rw_shift, state_rw_wkv, state_ret, state_ml_c, state_ml_n, state_ml_m)
    sample_states = [{n: s[l] for n, s in zip(names, st_in)} for l in range(DEPTH)]
    prompt_states = [_zero_state(x_prompt.shape[0], x_prompt.dtype) for _ in range(DEPTH)]
    y_p, sp = run(x_prompt, jnp.arange(x_prompt.shape[1]), prompt_states)
    y_s, ss = run(x_sample, PAST_LEN + jnp.arange(x_sample.shape[1]), sample_states)
    return (y_p, y_s, sp[0], sp[1], sp[2], sp[3], sp[4], sp[5], ss[0], ss[1], ss[2], ss[3], ss[4], ss[5])


_drawn_inputs = setup_inputs


def setup_inputs(seed=0):
    import zlib

    import numpy as np

    out = dict(_drawn_inputs(seed))
    spreads = {}
    factors = {'rw_rk': 24.368, 'rw_lnx_g': 8.0, 'rw_lnx_b': 7.192, 'ml_norm': 6.54}
    for name, (base, spread) in spreads.items():
        noise = np.random.default_rng([zlib.crc32(name.encode()), seed]).standard_normal(out[name].shape)
        drawn = base * np.exp(spread * noise) if base else spread * noise
        out[name] = jnp.asarray(drawn.astype(out[name].dtype))
    for name, factor in factors.items():
        out[name] = (out[name] * factor).astype(out[name].dtype)
    return out
```

```python
import numpy as np
import concourse.bass as bass
from concourse import mybir

F32 = mybir.dt.float32
F32R = mybir.dt.float32r
ALU = mybir.AluOpType
ACT = mybir.ActivationFunctionType
AX = mybir.AxisListType

D = 2048
SEQ, NS = 256, 8
T = SEQ + NS
TW = T + NS
DEPTH = 2
KB = D // 128
CH = 128
NCH = SEQ // CH
RW_W, RW_HEADS, RW_HD = 512, 8, 64
RW_BLK = RW_W // 128
RW_P = 3 * RW_W + 64 + 64 + 128
RW_PB = RW_P // 128
AH, AP_, AV = 6, 3, 128
P_TOTAL = 6412
PAST = 2048
D_FF = 5632
FB = D_FF // 128
ALPHA = (2 * DEPTH) ** 0.25
LN_EPS, NORM_EPS, GN_EPS = 1e-5, 1e-6, 64e-5
CAP = 15.0
GC = 512
RING = 4

PRM = [('rw_mu', RW_PB), ('rw_w0', 4), ('rw_a0', 4), ('rw_kk', 4), ('rw_ka', 4), ('rw_rk', 4), ('rw_lnx_g', 4),
       ('rw_lnx_b', 4), ('ml_norm', AH), ('ln1_g', KB), ('ln1_b', KB), ('ln2_g', KB), ('ln2_b', KB), ('rw_v0', 4)]
PRM_AT, _n = {}, 0
for _name, _rows in PRM:
    PRM_AT[_name] = _n
    _n += _rows
PRM_ROWS = _n

TAIL_SLABS = KB // 2
GROUP_SLABS = KB // 2
IN_GROUPS = 12
DOWN_SLABS = FB // 2
FF_GROUPS = D_FF // GC
LAYER_SLABS = TAIL_SLABS + IN_GROUPS * GROUP_SLABS + 4 * GROUP_SLABS + 2 * FF_GROUPS * GROUP_SLABS + 4 * DOWN_SLABS
LAYER_GROUPS = 1 + IN_GROUPS + 4 + 2 * FF_GROUPS + 4
TOTAL_SLABS = DEPTH * LAYER_SLABS


def constants():
    f = np.float32
    p, q = np.arange(128)[:, None], np.arange(128)[None, :]
    ident = (p == q)
    half = (p // 64 == q // 64)
    swap = (q == (p ^ 32))
    base = np.concatenate([ident, half, swap, np.ones((128, 128))], 1).astype(f)
    ident2 = (p % 64 == np.arange(64)[None, :]).astype(f)
    strict, incl = (p < q), (p <= q)
    neg = np.where(incl, 0.0, -1e30)
    first = ((p // 2 == q // 2) & (p < q))
    levels = [((p // (2 * n) == q // (2 * n)) & (p % (2 * n) >= n) & (q % (2 * n) < n)) for n in (1, 2, 4, 8, 16, 32, 64)]
    masks = np.concatenate([strict, incl, first, incl, neg] + levels, 1).astype(f)
    inv = (f(10000.0) ** (-np.arange(32, dtype=f) / f(32))).astype(f)
    pos = np.concatenate([np.arange(SEQ), np.full(NS, PAST)]).astype(f)
    ang = (pos[None, :] * inv[:, None]).astype(f).astype(np.float64)
    cos = np.tile(np.cos(ang), (4, 1))
    sin = np.concatenate([-np.sin(ang), np.sin(ang)] * 2, 0)
    rot = np.concatenate([cos, sin], 1).astype(f)
    lg = np.log1p(-np.exp2(-5.0 - np.arange(AH)))
    idx = np.arange(CH)
    rel = idx[None, :] - idx[:, None]
    dmask = [np.where(rel >= 0, np.exp(np.maximum(rel, 0) * g), 0.0) for g in lg]
    ofhalf = lambda pr: lg[2 * pr + np.arange(128) // 64][:, None]
    qdec = [np.exp((idx + 1.0)[None, :] * ofhalf(pr)) for pr in range(AP_)]
    kend = [np.exp((CH - 1.0 - idx)[None, :] * ofhalf(pr)) for pr in range(AP_)]
    ret = np.concatenate(dmask + qdec + kend, 1).astype(f)
    gam = np.concatenate([np.exp(ofhalf(pr)) for pr in range(AP_)] + [np.exp(CH * ofhalf(pr)) for pr in range(AP_)], 1).astype(f)
    sel = np.zeros((AH, AH + AP_, 128), f)
    for h in range(AH):
        sel[h, h, :] = 1
        sel[h, AH + h // 2, 64 * (h % 2):64 * (h % 2) + 64] = 1
    return {'c_base': base, 'c_ident2': ident2, 'c_masks': masks, 'c_rot': rot, 'c_ret': ret, 'c_gam': gam,
            'c_sel': sel.reshape(AH, -1)}


def build(nc, a, o):
    mm, tr = nc.tensor.matmul, nc.tensor.transpose
    ds = bass.ds

    here = [-(-nc.sbuf_base // 32) * 32]

    def put(name, shape, dt=F32):
        n = int(np.prod(shape[1:])) * 4
        t = nc.alloc_sbuf_tensor_at(name, shape, dt, offset=here[0])
        here[0] += -(-n // 32) * 32
        return t

    xh = put("x_hi", [128, KB, TW], F32R)
    xl = put("x_lo", [128, KB, TW], F32R)
    raw = put("w_raw", [128, RING, 2, GC])
    wh = put("w_hi", [128, RING, 2, GC], F32R)
    wl = put("w_lo", [128, RING, 2, GC], F32R)
    vfirst = put("v_first", [128, RW_BLK, T])
    prm = put("params", [128, 128])
    prm0 = put("params_ln0", [128, 32])
    base = put("base_tables", [128, 4, 128])
    ident2 = put("ident2", [128, 64])
    masks = put("masks", [128, 12, 128])
    gam = put("gammas", [128, 2 * AP_])
    sel = put("selectors", [AH, AH + AP_, 128])
    eps = put("eps", [128, 4])
    ident, halves, swap, ones = (base[:, i, :] for i in range(4))

    arena = here[0]

    def at(name, off, shape, dt=F32):
        assert arena + off + int(np.prod(shape[1:])) * 4 <= nc.sbuf_usable_end, name
        return nc.alloc_sbuf_tensor_at(name, shape, dt, offset=arena + off)

    BLK, BLW = T * 4, TW * 4
    O_H, O_L = 0, KB * BLK
    P_RET = 2 * KB * BLK
    P_MX = P_RET + 18 * BLW
    P_RAW = P_MX + 22 * BLK
    P_T = P_RAW + 16 * BLW
    P_END = P_T + 24 * BLK
    oh = at("o_hi", O_H, [128, KB, T], F32R)
    ol = at("o_lo", O_L, [128, KB, T], F32R)
    pret = at("p_ret", P_RET, [128, 18, TW])
    mx = at("rw_mixed", P_MX, [128, 22, T])
    praw = at("p_rw", P_RAW, [128, 16, TW])
    gate = at("rw_gate", P_T, [128, 4, T])
    bonus = at("rw_bonus", P_T + 4 * BLK, [128, 4, T])
    lw = at("rw_logw", P_T + 8 * BLK, [128, 4, T])
    ep = at("rw_ep", P_T + 12 * BLK, [128, 4, T])
    em = at("rw_em", P_T + 16 * BLK, [128, 4, T])
    tmp = at("rw_tmp", P_T + 20 * BLK, [128, 4, T])
    hh = at("h_hi", 0, [128, FB, T], F32R)
    hl = at("h_lo", FB * BLK, [128, FB, T], F32R)
    R = at("resid", 2 * FB * BLK, [128, KB, T])
    sg = at("sig_gate", (2 * FB + KB) * BLK, [128, 4, T])
    gu = at("gate_up", (2 * FB + KB + 4) * BLK, [128, 4, T])
    SQ = at("ln_squares", 0, [128, KB, T])
    small = [P_END]

    def little(name, shape, dt=F32):
        t = at(name, small[0], shape, dt)
        small[0] += -(-int(np.prod(shape[1:])) * 4 // 32) * 32
        return t

    ln_s = little("ln_sum", [128, T])
    ln_m = little("ln_stat", [128, T])
    ptail = little("p_tail", [128, 3, TW])
    prm_tok = at("params_rows", P_RAW, [PRM_ROWS, 128])
    prm0_tok = at("params0_rows", P_RAW + 512, [32, 128])
    mlb = little("ml_bias", [AH, 2])
    vmu = little("v_mu", [96, 1])
    ka1 = little("one_minus_ka", [128, 4])
    amid = little("rw_amid", [128, 4, NCH])
    namid = little("rw_namid", [128, 4, NCH])
    eamid = little("rw_eamid", [128, 4, NCH])
    wsam = little("rw_wsam", [128, 4, NS])
    enam = little("rw_enamid", [128, 4, NCH])
    eend = little("rw_eend", [128, 4, NCH])
    mlb2 = little("ml_bias_scaled", [AH, 2])
    mfin = little("m_final", [AH, NS + 1])
    mcol = little("m_carried", [AH, 1])
    rows9 = at("shift_cols", P_RAW + 1024, [128, KB, 1 + NS])
    mq = at("rw_mq", P_RAW, [128, RW_HEADS, 2, CH])
    tok = at("rw_tok", P_RAW + 8192, [128, 3, RW_W])
    zst = at("rw_state", P_RAW + 8192 + 6144, [128, 4, 64])
    tm = at("rw_t", P_T + 8 * BLK, [128, RW_HEADS, CH])
    ym = at("rw_tT", P_T + 8 * BLK + 4096, [128, RW_HEADS, CH])
    xm = at("rw_x", P_T + 8 * BLK + 8192, [128, RW_HEADS, CH])
    lm = at("rw_l", P_T + 8 * BLK + 12288, [128, RW_HEADS, CH])
    qb = at("rw_qb", O_H + 4352, [128, RW_HEADS, CH])
    lmk = at("rw_lmask", O_H + 8448, [128, RW_HEADS, CH])
    wsb = at("rw_w", O_H + 12544, [128, RW_W])
    usb = at("rw_u", O_H + 14592, [128, RW_W])
    yt = at("rw_y", O_L + 4352, [128, 4, T])
    lora = at("rw_lora", O_L + 8576, [128, 3, RW_W])
    srw = at("rw_sample", O_L + 8576, [128, 4, NS, 64])
    s1t = at("rw_sample_t1", P_RAW, [128, 4, NS, 64])
    s2t = at("rw_sample_t2", P_T + 8 * BLK, [128, 4, NS, 64])
    shift_tok = at("shift_rows", P_RET, [NS, D])
    shift_out = at("shift_out", P_RET + 8192, [1 + NS, D])
    B0 = P_RAW
    kw = at("a_kw", B0, [128, AP_, T])
    qs = at("a_qs", B0 + 3168, [128, AP_, T])
    ktok = at("a_ktok", B0 + 6336, [128, NCH, AP_ * 128])
    vtok = at("a_vtok", B0 + 9408, [128, NCH, AH * 128])
    ssb = at("a_scores", B0 + 15552, [128, 2, AH, CH])
    st = at("a_state", B0 + 21696, [128, 2, AP_, 128])
    nst = at("a_nstate", B0 + 24768, [128, 2, AP_, 128])
    ay = at("a_y", B0 + 27840, [128, AH, T])
    ad = at("a_den", B0 + 34176, [128, AH, T])
    assert B0 + 34176 + 6336 <= P_END
    rtmp = at("r_tmp", P_MX, [128, AH, T])
    rsam = at("r_sample", P_MX + 6336, [128, AP_, NS, 128])
    rvd = at("r_vdiag", P_MX + 18624, [128, NS, 128])
    rdec = at("r_decays", O_H + 10 * BLK, [128, 12, 128])
    rrot = at("r_rotary", O_L + 10 * BLK, [128, 2, T])
    mgate = at("m_gate", B0, [128, AH, T])
    pml = at("p_ml", P_MX, [128, 16, TW])
    mexp = at("m_exp", P_RET, [128, AH, SEQ])
    mvd = at("m_vdiag", P_RET, [128, NS, 128])
    msam = at("m_sample", P_RET + 6144, [128, AP_, NS, 128])
    rows = at("m_rows", B0 + 27840, [AH, 6, T])
    mct = little("m_ct", [128, NCH, AH])
    msn = little("m_nsample", [128, AP_, NS])
    msk = little("m_scol", [128, AP_, NS])
    mpd = little("m_nprod", [128, AP_, NS])
    msk_abs = little("m_sample_absden", [128, AH * NS])
    mdc = little("m_cdecay", [128, AP_])
    x_tok = at("x_rows", 0, [128, 3, D])
    y_tok = at("y_rows", 0, [128, 3, D])

    ps = nc.alloc_psum_tensor("psum", [128, 8, 512], F32)

    made = {}

    class Names:
        def __getattr__(self, name):
            if name not in made:
                made[name] = nc.alloc_semaphore(name)
            return made[name]
    S = Names()
    raw_loaded = [nc.alloc_semaphore(f"raw_loaded{i}") for i in range(RING)]
    tail_loaded = [nc.alloc_semaphore(f"tail_loaded{i}") for i in range(RING)]

    class Own:
        def __init__(self, eng, sem):
            self.eng, self.sem, self.n = eng, sem, 0

        def __call__(self, ins):
            self.n += 1
            ins.then_inc(self.sem, 1)
            self.eng.wait_ge(self.sem, self.n)

    def col(name, i=0):
        return prm[:, PRM_AT[name] + i:PRM_AT[name] + i + 1]

    def cols(name, n):
        return prm[:, PRM_AT[name]:PRM_AT[name] + n]

    def over(ap, n):
        return ap.unsqueeze(2).to_broadcast([ap.shape[0], ap.shape[1], n])

    def each(ap, m):
        return ap.unsqueeze(1).to_broadcast([ap.shape[0], m, ap.shape[1]])

    def hb(h, b0, w):
        return b0 + h % 2, slice(w * (h // 2), w * (h // 2) + w)

    def halves_of(b0, w, n):
        return ps[:, b0:b0 + 2, 0:w * (n // 2)].rearrange("p e (q i) -> p q e i", i=w)

    def pairs(ap):
        return ap.rearrange("p (q e) i -> p q e i", e=2)

    def each2(ap, m):
        return ap.unsqueeze(1).unsqueeze(1).to_broadcast([ap.shape[0], m, 2, ap.shape[1]])

    def slab0(l, part):
        n = l * LAYER_SLABS
        for name, slabs in (('tail', TAIL_SLABS), ('in', IN_GROUPS * 8), ('out', 32), ('up', 16 * FF_GROUPS),
                            ('down', 4 * DOWN_SLABS)):
            if name == part:
                return n
            n += slabs

    def group0(l, part):
        n = 1 + l * LAYER_GROUPS
        for name, groups in (('tail', 1), ('in', IN_GROUPS), ('out', 4), ('up', 2 * FF_GROUPS), ('down', 4)):
            if name == part:
                return n
            n += groups

    block = nc.Block()
    with block:
        @block.sync
        def _(sp):
            def free(s):
                if not (isinstance(s, int) and s < RING):
                    sp.wait_ge(S.hi_ready, s - RING + 1)
                    sp.wait_ge(S.lo_ready, s - RING + 1)

            def load(s, j, src, k0, c0):
                free(s)
                sp.dma_start(raw[:, j % RING, :, :], src[:, k0:k0 + 2, ds(c0, GC)]).then_inc(raw_loaded[j % RING], 16)

            sp.wait_ge(S.raw_cleared, 1)
            for l in range(DEPTH):
                win = a['w_in'][l].rearrange("(k p) n -> p k n", p=128)
                c0 = IN_GROUPS * GC
                for j in range(TAIL_SLABS):
                    s = slab0(l, 'tail') + j
                    free(s)
                    rj = raw[:, j % RING]
                    sp.dma_start(rj[:, :, 0:262], win[:, 2 * j:2 * j + 2, c0:c0 + 262]).then_inc(raw_loaded[j % RING], 16)
                    sp.dma_start(rj[:, :, 288:294], win[:, 2 * j:2 * j + 2, c0 + 262:c0 + 268]).then_inc(tail_loaded[j % RING], 16)
                    if l:
                        v1 = a['rw_v1'][l - 1].rearrange("(k p) n -> p k n", p=128)
                        sp.dma_start(rj[:, :, 320:352], v1[:, 2 * j:2 * j + 2, :]).then_inc(tail_loaded[j % RING], 16)

                def stream(src, s0, bodies, kblocks):
                    slabs = kblocks // 2
                    with sp.Fori(0, bodies) as it:
                        for j in range(2 * slabs):
                            load(it * (2 * slabs) + (s0 + j), j, src, 2 * (j % slabs), it * (2 * GC) + GC * (j // slabs))
                stream(win, slab0(l, 'in'), IN_GROUPS // 2, KB)
                stream(a['w_out'][l].rearrange("(k p) n -> p k n", p=128), slab0(l, 'out'), 2, KB)
                wg = a['w_gate'][l].rearrange("(k p) n -> p k n", p=128)
                wu = a['w_up'][l].rearrange("(k p) n -> p k n", p=128)
                with sp.Fori(0, FF_GROUPS) as it:
                    for j in range(16):
                        load(it * 16 + (slab0(l, 'up') + j), j, wg if j < 8 else wu, 2 * (j % 8), it * GC)
                stream(a['w_down'][l].rearrange("(k p) n -> p k n", p=128), slab0(l, 'down'), 2, FB)

            for t in range(2):
                sp.wait_ge(S.y_rows, t + 1)
                sp.dma_start(o['y_prompt'][0, 128 * t:128 * t + 128, :], y_tok[:, t, :]).then_inc(S.y_stored, 16)
            sp.wait_ge(S.y_rows, 3)
            sp.dma_start(o['y_sample'][:, 0, :], y_tok[0:NS, 2, :]).then_inc(S.y_stored, 16)
            sp.wait_ge(S.y_stored, 48)
            sp.wait_ge(S.shift_stored, 32 * DEPTH)
            sp.wait_ge(S.rw_stored, 16 * 5 * DEPTH)
            sp.wait_ge(S.ret_stored, 16 * 4 * DEPTH)
            sp.wait_ge(S.ml_stored, 16 * 10 * DEPTH)

        @block.tensor
        def _(pe):
            def product(s, j, g, k0, last_k, bh, bl, nt, blocks=4):
                pe.wait_ge(S.lo_ready, s + 1)
                if k0 == 0 and g is not None:
                    pe.wait_ge(S.evacuated, g - 1)
                setat = 4 * ((j // ((last_k + 1) // 2)) % 2)
                for k in (k0, k0 + 1):
                    for n in range(blocks):
                        w0 = wh[:, j % RING, k - k0, 128 * n:128 * n + 128]
                        w1 = wl[:, j % RING, k - k0, 128 * n:128 * n + 128]
                        out = ps[:, setat + n, 0:nt]
                        mm(out, w1, bh[:, k, 0:nt], start=(k == 0), stop=False)
                        mm(out, w0, bl[:, k, 0:nt], start=False, stop=False)
                        last = mm(out, w0, bh[:, k, 0:nt], start=False, stop=(k == last_k))
                last.then_inc(S.slab_used, 1)

            def groups(s0, g0, bodies, kblocks, bh, bl, nt):
                slabs = kblocks // 2
                with pe.Fori(0, bodies) as it:
                    for j in range(2 * slabs):
                        product(it * (2 * slabs) + (s0 + j), j, it * 2 + (g0 + j // slabs), 2 * (j % slabs),
                                kblocks - 1, bh, bl, nt)

            def to_rows(src, n, w, bank0, sem):
                for b in range(n):
                    last = tr(ps[0:w, bank0 + b // 4, 128 * (b % 4):128 * (b % 4) + 128], src(b), ident)
                last.then_inc(sem, 1)

            def norm_sums(n):
                pe.wait_ge(S.ln_sum, n + 1)
                mm(ps[:, 0, 0:T], ones, ln_s[:, :], start=True, stop=True).then_inc(S.ln_sum_all, 1)
                pe.wait_ge(S.ln_sumsq, n + 1)
                mm(ps[:, 1, 0:T], ones, ln_s[:, :], start=True, stop=True).then_inc(S.ln_sumsq_all, 1)

            pe.wait_ge(S.tables_loaded, 16 * 5)
            pe.wait_ge(S.x_loaded, 32)
            for q in range(4):
                if q >= 2:
                    pe.wait_ge(S.x_taken, q - 1)
                for b in range(4):
                    bank = ps[:, 4 * (q % 2) + b]
                    f = 128 * (4 * q + b)
                    for t in range(2):
                        tr(bank[:, 128 * t:128 * t + 128], x_tok[:, t, f:f + 128], ident)
                    last = tr(bank[:, SEQ:T], x_tok[0:NS, 2, f:f + 128], ident[0:NS, 0:NS])
                last.then_inc(S.x_turned, 1)
            pe.wait_ge(S.prm0_loaded, 32)
            pe.wait_ge(S.x_taken, 4)
            tr(ps[:, 2, 0:32], prm0_tok[:, :], ident[0:32, 0:32]).then_inc(S.prm0_turned, 1)
            norm_sums(0)

            def attention(l, ml, n):
                src = pml if ml else pret
                qT = (lambda p: src[:, p, :])
                kT = (lambda p: src[:, AP_ + p, :])
                vT = (lambda h: src[:, 2 * AP_ + h, :])
                pe.wait_ge(S.a_prepared, n + 1)
                for c in range(NCH):
                    for p in range(AP_):
                        tr(ps[:, 4 * c, 128 * p:128 * p + 128], kw[:, p, CH * c:CH * c + CH], ident)
                    for h in range(AH):
                        last = tr(ps[:, 4 * c + 1 + h // 4, 128 * (h % 4):128 * (h % 4) + 128],
                                  vT(h)[:, CH * c:CH * c + CH], ident)
                last.then_inc(S.a_turned, 1)
                for c in range(NCH):
                    pe.wait_ge(S.a_tok, n + 1)
                    for h in range(AH):
                        r = slice(64 * (h % 2), 64 * (h % 2) + 64)
                        bank, hc = hb(h, 4 * c, 128)
                        last = mm(ps[:, bank, hc],
                                  kT(h // 2)[r, CH * c:CH * c + CH], qT(h // 2)[r, CH * c:CH * c + CH], start=True, stop=True)
                    last.then_inc(S.a_scored, 1)
                for c in range(NCH):
                    pe.wait_ge(S.a_weighted, 2 * n + 2)
                    if c:
                        pe.wait_ge(S.a_state_kept, 2 * n + 1)
                        pe.wait_ge(S.a_y_kept, 2 * n + 1)
                    for h in range(AH):
                        r = slice(64 * (h % 2), 64 * (h % 2) + 64)
                        bank, hc = hb(h, 0, 128)
                        mm(ps[:, bank, hc], vtok[:, c, 128 * h:128 * h + 128],
                           ssb[:, c, h, :], start=True, stop=(c == 0))
                        if c:
                            mm(ps[:, bank, hc], st[r, 0, h // 2, :],
                               qs[r, h // 2, CH * c:CH * c + CH], start=False, stop=True)
                        if ml:
                            mm(ps[:, bank + 2, hc], ones, ssb[:, c, h, :],
                               start=True, stop=(c == 0))
                            if c:
                                mm(ps[:, bank + 2, hc], nst[r, 0, h // 2, :],
                                   qs[r, h // 2, CH * c:CH * c + CH], start=False, stop=True)
                    for h in range(AH):
                        r = slice(64 * (h % 2), 64 * (h % 2) + 64)
                        last = mm(ps[r, 4, 128 * (h // 2):128 * (h // 2) + 128], ktok[:, c, 64 * h:64 * h + 64],
                                  vtok[:, c, 128 * h:128 * h + 128], start=True, stop=True)
                        if ml:
                            last = mm(ps[r, 5, 128 * (h // 2):128 * (h // 2) + 128], ktok[:, c, 64 * h:64 * h + 64],
                                      ones, start=True, stop=True)
                    last.then_inc(S.a_summed, 1)
                for p in range(AP_):
                    for e in range(2):
                        pe.wait_ge(S.a_vdiag, n * AH + 2 * p + e + 1)
                        if p and not e:
                            pe.wait_ge(S.a_pair_done, n * AP_ + p)
                        if p == 0 and not e:
                            pe.wait_ge(S.a_state_kept, 2 * n + 2)
                        vd = mvd if ml else rvd
                        for b in range(2):
                            last = mm(ps[64 * e:64 * e + 64, 6 + b, 0:512], ones[:, 0:64],
                                      vd[:, 4 * b:4 * b + 4, :].rearrange("p b v -> p (b v)"), start=True, stop=True)
                        last.then_inc(S.a_vspread, 1)
                pe.wait_ge(S.a_pair_done, n * AP_ + AP_)
                sam = msam if ml else rsam
                pe.wait_ge(S.a_y_kept, 2 * n + 2)
                for h in range(AH):
                    r = slice(64 * (h % 2), 64 * (h % 2) + 64)
                    for b in range(NS):
                        last = mm(ps[:, h % 2, 8 * (h // 2) + b:8 * (h // 2) + b + 1], sam[r, h // 2, b, :],
                                  qT(h // 2)[r, SEQ + b:SEQ + b + 1], start=True, stop=True)
                if ml:
                    pe.wait_ge(S.m_nprod, l + 1)
                    for h in range(AH):
                        r = slice(64 * (h % 2), 64 * (h % 2) + 64)
                        bank, hc = hb(h, 2, NS)
                        last = mm(ps[:, bank, hc], ones[r, :], mpd[r, h // 2, :], start=True, stop=True)
                last.then_inc(S.a_sample_y, 1)
                pe.wait_ge(S.a_squares, n + 1)
                for h in range(AH):
                    last = mm(ps[:, 2 + h, 0:T], ones, ad[:, h, :], start=True, stop=True)
                last.then_inc(S.a_sumsq, 1)

            for l in range(DEPTH):
                pe.wait_ge(S.x_ready, 2 * l + 1)
                pe.wait_ge(S.prm_loaded, 16 * (13 * (l + 1) + l))
                pr = PRM_ROWS if l else PRM_ROWS - 4
                tr(ps[:, 0, 0:pr], prm_tok[0:pr, :], ident[0:pr, 0:pr])
                pe.wait_ge(S.shift_loaded, 16 * (l + 1))
                for b in range(KB):
                    tr(ps[:, 1, 8 * b:8 * b + 8], shift_tok[:, 128 * b:128 * b + 128], ident[0:NS, 0:NS])
                pe.wait_ge(S.shift_cols, l + 1)
                to_rows(lambda b: rows9[:, b, :], KB, 1 + NS, 4, S.layer_turned)
                pe.wait_ge(S.layer_taken, l + 1)

                for j in range(TAIL_SLABS):
                    product(slab0(l, 'tail') + j, j, None, 2 * j, KB - 1, xh, xl, TW, blocks=3)
                pe.wait_ge(S.evacuated, group0(l, 'in'))
                groups(slab0(l, 'in'), group0(l, 'in'), 2, KB, xh, xl, TW)

                pe.wait_ge(S.rw_in, l + 1)
                for b in range(4):
                    c = slice(128 * b, 128 * b + 128)
                    mm(ps[:, b, 0:T], lora[0:64, 0, c], mx[0:64, 12, :], start=True, stop=True)
                for b in range(4):
                    c = slice(128 * b, 128 * b + 128)
                    last = mm(ps[:, 4 + b, 0:T], lora[64:128, 0, c], mx[64:128, 12, :], start=True, stop=True)
                last.then_inc(S.rw_wa, 1)
                pe.wait_ge(S.rw_wa_taken, l + 1)
                for b in range(4):
                    c = slice(128 * b, 128 * b + 128)
                    last = mm(ps[:, b, 0:T], lora[:, 1, c], mx[:, 13, :], start=True, stop=True)
                if l:
                    for b in range(4):
                        c = slice(128 * b, 128 * b + 128)
                        last = mm(ps[:, 4 + b, 0:T], lora[64:96, 2, c], ptail[64:96, 2, 0:T], start=True, stop=True)
                last.then_inc(S.rw_gv, 1)
                pe.wait_ge(S.rw_kk_sq, l + 1)
                for b in range(4):
                    last = mm(ps[:, b, 0:T], halves, tmp[:, b, :], start=True, stop=True)
                last.then_inc(S.rw_kk_sum, 1)
                pe.wait_ge(S.rw_bonus_in, l + 1)
                for b in range(4):
                    last = mm(ps[:, 4 + b, 0:T], halves, tmp[:, b, :], start=True, stop=True)
                last.then_inc(S.rw_bonus_sum, 1)

                for c in range(NCH):
                    n = NCH * l + c
                    cs = slice(CH * c, CH * c + CH)
                    pe.wait_ge(S.rw_scaled, l + 1)
                    if c:
                        pe.wait_ge(S.rw_chunk_done, n)
                    for i, b0 in enumerate((8, 4, 18)):
                        for b in range(4):
                            last = tr(ps[:, i, 128 * b:128 * b + 128], mx[:, b0 + b, cs], ident)
                    last.then_inc(S.rw_turned, 1)
                    for q in range(2):
                        for what, lhs0 in ((0, 18), (1, 4)):
                            if q:
                                pe.wait_ge(S.rw_pairs_taken, 4 * n + 1 + what)
                            for e in range(4):
                                h = 4 * q + e
                                r = slice(64 * (h % 2), 64 * (h % 2) + 64)
                                bank = 4 + 2 * what + e % 2
                                at_ = 256 * (e // 2)
                                mm(ps[:, bank, at_:at_ + 128], mx[r, lhs0 + h // 2, cs], mx[r, 14 + h // 2, cs],
                                   start=True, stop=True)
                                last = mm(ps[:, bank, at_ + 128:at_ + 256], mx[r, lhs0 + h // 2, cs], mx[r, h // 2, cs],
                                          start=True, stop=True)
                            last.then_inc(S.rw_pairs, 1)
                    pe.wait_ge(S.rw_tok, n + 1)
                    for h in range(RW_HEADS):
                        r = slice(64 * (h % 2), 64 * (h % 2) + 64)
                        bank, hc = hb(h, 0, 128)
                        last = mm(ps[:, bank, hc], mx[r, 14 + h // 2, cs],
                                  mx[r, 18 + h // 2, cs], start=True, stop=True)
                    last.then_inc(S.rw_l, 1)
                    for lev in range(6):
                        for q in range(2):
                            m = 12 * n + 2 * lev + q
                            pe.wait_ge(S.rw_masked, m + 1)
                            for e in range(4):
                                h = 4 * q + e
                                last = mm(ps[:, q, 128 * e:128 * e + 128], lmk[:, h, :], ym[:, h, :], start=True, stop=True)
                            last.then_inc(S.rw_x, 1)
                        for q in range(2):
                            m = 12 * n + 2 * lev + q
                            pe.wait_ge(S.rw_x_kept, m + 1)
                            for e in range(4 if lev < 5 else 0):
                                h = 4 * q + e
                                mm(ps[:, 2 + 2 * q, 128 * e:128 * e + 128], xm[:, h, :], tm[:, h, :], start=True, stop=True)
                            for e in range(4):
                                h = 4 * q + e
                                last = mm(ps[:, 3 + 2 * q, 128 * e:128 * e + 128], tm[:, h, :], xm[:, h, :],
                                          start=True, stop=True)
                            last.then_inc(S.rw_tx, 1)
                    pe.wait_ge(S.rw_inverted, 2 * n + 2)
                    for h in range(RW_HEADS):
                        r = slice(64 * (h % 2), 64 * (h % 2) + 64)
                        hc = slice(64 * h, 64 * h + 64)
                        bank, oc = hb(h, 6, 64)
                        last = mm(ps[:, bank, oc], mq[:, h, 0, :], tok[:, 0, hc], start=True, stop=(c == 0))
                        if c:
                            last = mm(ps[:, bank, oc], mx[r, 14 + h // 2, cs], zst[r, h // 2, :], start=False, stop=True)
                    last.then_inc(S.rw_w, 1)
                    pe.wait_ge(S.rw_w_kept, n + 1)
                    for h in range(RW_HEADS):
                        hc = slice(64 * h, 64 * h + 64)
                        last = mm(ps[:, 2, hc], ym[:, h, :], wsb[:, hc], start=True, stop=True)
                    last.then_inc(S.rw_u, 1)
                    pe.wait_ge(S.rw_u_kept, n + 1)
                    for h in range(RW_HEADS):
                        r = slice(64 * (h % 2), 64 * (h % 2) + 64)
                        hc = slice(64 * h, 64 * h + 64)
                        out = ps[r, 3 * (h % 2), 128 * (h // 2):128 * (h // 2) + 128]
                        if c:
                            mm(out, zst[r, h // 2, :], mx[r, h // 2, cs], start=True, stop=False)
                        mm(out, tok[:, 0, hc], mq[:, h, 1, :], start=(c == 0), stop=False)
                        mm(out, usb[:, hc], qb[:, h, :], start=False, stop=True)
                        out = ps[r, 1, 64 * (h // 2):64 * (h // 2) + 64]
                        mm(out, tok[:, 1, hc], tok[:, 0, hc], start=True, stop=False)
                        last = mm(out, tok[:, 2, hc], usb[:, hc], start=False, stop=True)
                    last.then_inc(S.rw_y, 1)
                for i, src in enumerate((s1t, s2t, s1t)):
                    pe.wait_ge(S.rw_sample_in, 3 * l + i + 1)
                    for b in range(4):
                        last = mm(ps[:, (4 * i) % 8 + b, :], halves, src[:, b, :, :].rearrange("p b v -> p (b v)"),
                                  start=True, stop=True)
                    last.then_inc(S.rw_sample_sum, 1)
                for i in range(2):
                    pe.wait_ge(S.rw_gn_in, 2 * l + i + 1)
                    for b in range(4):
                        last = mm(ps[:, 4 * (1 - i) + b, 0:T], halves, (yt if i == 0 else tmp)[:, b, :], start=True, stop=True)
                    last.then_inc(S.rw_gn_sum, 1)
                pe.wait_ge(S.rw_done, l + 1)

                groups(slab0(l, 'in') + 32, group0(l, 'in') + 4, 2, KB, xh, xl, TW)
                pe.wait_ge(S.ret_in, l + 1)
                for b in range(6):
                    last = mm(ps[:, b, 0:T], swap, pret[:, b, 0:T], start=True, stop=True)
                last.then_inc(S.ret_swapped, 1)
                attention(l, False, 2 * l)
                pe.wait_ge(S.a_done, 2 * l + 1)

                groups(slab0(l, 'in') + 64, group0(l, 'in') + 8, 2, KB, xh, xl, TW)
                pe.wait_ge(S.m_rows_c, l + 1)
                for c in range(NCH):
                    tr(ps[:, 6, 8 * c:8 * c + AH], rows[:, 0, CH * c:CH * c + CH], ident[0:AH, 0:AH])
                pe.wait_ge(S.m_rows_m, l + 1)
                for h in range(AH):
                    last = mm(ps[:, h, 0:T], sel[:, h, :], rows[:, 3, :], start=True, stop=True)
                last.then_inc(S.m_spread, 1)
                pe.wait_ge(S.m_exp_in, l + 1)
                pe.wait_ge(S.m_rows_e, l + 1)
                for h in range(AH):
                    last = mm(ps[:, h, 0:T], sel[:, h, :], rows[:, 5, :], start=True, stop=True)
                last.then_inc(S.m_spread, 1)
                pe.wait_ge(S.m_guard_taken, l + 1)
                for p in range(AP_):
                    mm(ps[:, p, 0:T], sel[:, AH + p, :], rows[:, 4, :], start=True, stop=True)
                    last = mm(ps[:, 3 + p, 0:T], sel[:, AH + p, :], rows[:, 1, :], start=True, stop=True)
                last.then_inc(S.m_spread, 1)
                attention(l, True, 2 * l + 1)
                pe.wait_ge(S.a_done, 2 * l + 2)

                groups(slab0(l, 'out'), group0(l, 'out'), 2, KB, oh, ol, T)
                norm_sums(2 * l + 1)
                pe.wait_ge(S.x_ready, 2 * l + 2)
                groups(slab0(l, 'up'), group0(l, 'up'), FF_GROUPS, KB, xh, xl, T)
                pe.wait_ge(S.hidden_ready, FF_GROUPS * (l + 1))
                groups(slab0(l, 'down'), group0(l, 'down'), 2, FB, hh, hl, T)
                norm_sums(2 * l + 2)

            pe.wait_ge(S.x_ready, 2 * DEPTH + 1)
            to_rows(lambda b: R[:, b, 0:128], KB, 128, 0, S.y_turned)
            to_rows(lambda b: R[:, b, 128:256], KB, 128, 4, S.y_turned)
            pe.wait_ge(S.y_rows, 1)
            to_rows(lambda b: R[:, b, SEQ:T], KB, NS, 0, S.y_turned)

        @block.scalar
        def _(act):
            own = Own(act, S.act_steps)
            A = nc.scalar.activation

            def hi4(s0, pieces=None):
                for j in range(RING):
                    act.wait_ge(raw_loaded[j], s0 * 4 + 16)
                    if pieces:
                        act.wait_ge(tail_loaded[j], pieces)
                    if not (isinstance(s0, int) and s0 < RING):
                        act.wait_ge(S.slab_used, s0 + (j - RING + 1))
                    A(wh[:, j, :, :], raw[:, j, :, :], ACT.Copy).then_inc(S.hi_ready, 1)

            def his(s0, n):
                with act.Fori(0, n // RING) as it:
                    hi4(it * RING + s0)

            def tail_pieces(l, turn):
                return 16 * (turn + 1) if l == 0 else 32 + 64 * (l - 1) + 32 * (turn + 1)

            act.dma_start(x_tok[:, 0:2, :], a['x_prompt'][0].rearrange("(t p) d -> p t d", p=128)).then_inc(S.x_loaded, 16)
            act.dma_start(x_tok[0:NS, 2, :], a['x_sample'][:, 0, :]).then_inc(S.x_loaded, 16)
            act.dma_start(base[:, :, :].rearrange("p a b -> p (a b)"), a['c_base']).then_inc(S.tables_loaded, 16)
            act.dma_start(ident2[:, :], a['c_ident2']).then_inc(S.tables_loaded, 16)
            act.dma_start(masks[:, :, :].rearrange("p a b -> p (a b)"), a['c_masks']).then_inc(S.tables_loaded, 16)
            act.dma_start(gam[:, :], a['c_gam']).then_inc(S.tables_loaded, 16)
            act.dma_start(sel[:, :, :].rearrange("p a b -> p (a b)"), a['c_sel']).then_inc(S.tables_loaded, 16)
            act.dma_start(prm0_tok[0:16, :], a['ln0_g'].rearrange("(b c) -> b c", c=128)).then_inc(S.prm0_loaded, 16)
            act.dma_start(prm0_tok[16:32, :], a['ln0_b'].rearrange("(b c) -> b c", c=128)).then_inc(S.prm0_loaded, 16)

            def norm_parts(n):
                act.wait_ge(S.ln_centered, n + 1)
                A(SQ[:, :, :], R[:, :, :], ACT.Square).then_inc(S.ln_squared, 1)
                act.wait_ge(S.ln_sumsq_all, n + 1)
                A(ln_m[:, :], ps[:, 1, 0:T], ACT.Sqrt, bias=eps[:, 0:1], scale=1.0 / D).then_inc(S.ln_std, 1)

            def layer_loads(l):
                act.wait_ge(S.x_ready, 2 * l + 1)
                for name, n in PRM:
                    if name == 'rw_v0' and l == 0:
                        continue
                    src = a[name][l - 1 if name == 'rw_v0' else l].rearrange("(b c) -> b c", c=128)
                    act.dma_start(prm_tok[PRM_AT[name]:PRM_AT[name] + n, :], src).then_inc(S.prm_loaded, 16)
                act.dma_start(shift_tok[:, :], a['state_rw_shift'][l]).then_inc(S.shift_loaded, 16)
                act.dma_start(mlb[:, 0:1], a['ml_ib'][l].rearrange("(h a) -> h a", a=1)).then_inc(S.mlb_loaded, 16)
                act.dma_start(mlb[:, 1:2], a['ml_fb'][l].rearrange("(h a) -> h a", a=1)).then_inc(S.mlb_loaded, 16)
                act.dma_start(lora[0:64, 0, :], a['rw_w2'][l]).then_inc(S.lora_loaded, 16)
                act.dma_start(lora[64:128, 0, :], a['rw_a2'][l]).then_inc(S.lora_loaded, 16)
                act.dma_start(lora[:, 1, :], a['rw_g2'][l]).then_inc(S.lora_loaded, 16)
                if l:
                    act.dma_start(lora[64:96, 2, :], a['rw_v2'][l - 1]).then_inc(S.lora_loaded, 16)
                    act.dma_start(vmu[64:96, :], a['rw_vmu'][l - 1].rearrange("(h a) -> h a", a=1)).then_inc(S.lora_loaded, 16)

            def attention(l, ml, n):
                act.wait_ge(S.a_turned, n + 1)
                for c in range(NCH):
                    A(ktok[:, c, :], ps[:, 4 * c, 0:384], ACT.Copy)
                    A(vtok[:, c, 0:512], ps[:, 4 * c + 1, :], ACT.Copy)
                    last = A(vtok[:, c, 512:768], ps[:, 4 * c + 2, 0:256], ACT.Copy)
                last.then_inc(S.a_tok, 1)
                if ml:
                    for c in range(NCH):
                        act.wait_ge(S.a_summed, 2 * n + c + 1)
                        A(pairs(ssb[:, c, :, :]), halves_of(2, CH, AH), ACT.Abs).then_inc(S.m_absden, 1)
                    act.wait_ge(S.a_sample_y, n + 1)
                    A(pairs(msk_abs[:, :].rearrange("p (h b) -> p h b", b=NS)), halves_of(2, NS, AH), ACT.Abs).then_inc(S.m_absden, 1)
                act.wait_ge(S.a_y_ready, n + 1)
                A(ad[:, :, :], ay[:, :, :], ACT.Square).then_inc(S.a_squares, 1)
                act.wait_ge(S.a_sumsq, n + 1)
                A(ad[:, :, :], ps[:, 2:8, 0:T], ACT.Sqrt, bias=eps[:, 1:2], scale=1.0 / AV).then_inc(S.a_std, 1)
                if ml:
                    A(mgate[:, 0:4, :], pml[:, 12:16, 0:T], ACT.Sigmoid)
                    A(mgate[:, 4:6, :], ptail[:, 0:2, 0:T], ACT.Sigmoid).then_inc(S.a_gate, 1)
                else:
                    A(rtmp[:, :, :], pret[:, 12:18, 0:T], ACT.Sigmoid).then_inc(S.a_gate, 1)
                a0 = 10 if ml else 4
                act.wait_ge(S.a_out, n + 1)
                A(oh[:, a0:a0 + AH, :], ay[:, :, :], ACT.Copy).then_inc(S.a_out_hi, 1)

            hi4(0, tail_pieces(0, 0))
            norm_parts(0)
            for l in range(DEPTH):
                layer_loads(l)
                act.wait_ge(S.layer_taken, l + 1)
                act.dma_start(o['p_shift'][l], shift_out[0:1, :]).then_inc(S.shift_stored, 16)
                act.dma_start(o['s_shift'][l], shift_out[1:1 + NS, :]).then_inc(S.shift_stored, 16)
                hi4(slab0(l, 'tail') + 4, tail_pieces(l, 1))
                his(slab0(l, 'in'), 36)

                act.wait_ge(S.rw_mix, l + 1)
                A(mx[0:64, 12, :], mx[0:64, 12, :], ACT.Tanh)
                A(mx[:, 13, :], mx[:, 13, :], ACT.Sigmoid).then_inc(S.rw_in, 1)
                act.wait_ge(S.rw_wa, l + 1)
                for b in range(4):
                    A(lw[:, b, :], ps[:, b, 0:T], ACT.Sigmoid, bias=col('rw_w0', b))
                for b in range(4):
                    last = A(mx[:, 18 + b, :], ps[:, 4 + b, 0:T], ACT.Sigmoid, bias=col('rw_a0', b))
                last.then_inc(S.rw_wa_taken, 1)
                act.wait_ge(S.rw_gv, l + 1)
                last = A(gate[:, :, :], ps[:, 0:4, 0:T], ACT.Copy)
                if l:
                    for b in range(4):
                        last = A(tmp[:, b, :], ps[:, 4 + b, 0:T], ACT.Sigmoid, bias=col('rw_v0', b))
                last.then_inc(S.rw_gv_taken, 1)
                act.wait_ge(S.rw_kk_raw, l + 1)
                A(tmp[:, :, :], mx[:, 14:18, :], ACT.Square).then_inc(S.rw_kk_sq, 1)
                act.wait_ge(S.rw_kk_ss, l + 1)
                A(tmp[:, :, :], tmp[:, :, :], ACT.Sqrt).then_inc(S.rw_kk_norm, 1)
                act.wait_ge(S.rw_cum, l + 1)
                for b in range(4):
                    for c in range(NCH):
                        cs = slice(CH * c, CH * c + CH)
                        A(ep[:, b, cs], lw[:, b, cs], ACT.Exp, bias=namid[:, b, c:c + 1])
                        A(em[:, b, cs], lw[:, b, cs], ACT.Exp, bias=amid[:, b, c:c + 1], scale=-1.0)
                A(wsam[:, :, :], lw[:, :, SEQ:T], ACT.Exp)
                A(eamid[:, :, :], amid[:, :, :], ACT.Exp)
                A(enam[:, :, :], namid[:, :, :], ACT.Exp).then_inc(S.rw_exps, 1)
                for c in range(NCH):
                    n = NCH * l + c
                    act.wait_ge(S.rw_turned, n + 1)
                    A(tok[:, :, :], ps[:, 0:3, :], ACT.Copy).then_inc(S.rw_tok, 1)
                    for m in range(12 * n, 12 * n + 12):
                        q = m % 2
                        act.wait_ge(S.rw_x, m + 1)
                        A(xm[:, 4 * q:4 * q + 4, :], ps[:, q, :].rearrange("p (h i) -> p h i", i=CH),
                          ACT.Copy).then_inc(S.rw_x_kept, 1)
                    act.wait_ge(S.rw_w, n + 1)
                    A(pairs(wsb[:, :].rearrange("p (h v) -> p h v", v=64)), halves_of(6, 64, RW_HEADS), ACT.Copy).then_inc(S.rw_w_kept, 1)
                    act.wait_ge(S.rw_u, n + 1)
                    A(usb[:, :], ps[:, 2, :], ACT.Copy, scale=-1.0).then_inc(S.rw_u_kept, 1)
                    if c == 0:
                        si = a['state_rw_wkv'][l].rearrange("b (p e) k v -> p (e k) b v", e=2)
                        so = o['s_wkv'][l].rearrange("b (p e) k v -> p (e k) b v", e=2)
                        for p in range(4):
                            act.dma_start(srw[:, p, :, :], si[p]).then_inc(S.rw_sample_loaded, 16)
                act.wait_ge(S.rw_chunk_done, NCH * (l + 1))
                act.dma_start(o['p_wkv'][l, 0].rearrange("(p e) k v -> (e k) p v", e=2), zst[:, :, :]).then_inc(S.rw_stored, 16)
                act.wait_ge(S.rw_sample_new, l + 1)
                for p in range(4):
                    act.dma_start(so[p], srw[:, p, :, :]).then_inc(S.rw_stored, 16)
                act.wait_ge(S.rw_gn_c, l + 1)
                A(tmp[:, :, :], yt[:, :, :], ACT.Square).then_inc(S.rw_gn_in, 1)
                act.wait_ge(S.rw_gn_sum, 2 * l + 2)
                A(tmp[:, :, :], ps[:, 0:4, 0:T], ACT.Sqrt, bias=eps[:, 2:3], scale=1.0 / RW_HD).then_inc(S.rw_gn_std, 1)
                act.wait_ge(S.rw_out, l + 1)
                A(oh[:, 0:4, :], yt[:, :, :], ACT.Copy).then_inc(S.rw_out_hi, 1)

                act.wait_ge(S.rw_done, l + 1)
                act.wait_ge(S.rw_stored, 80 * (l + 1))
                act.dma_start(rdec[:, :, :].rearrange("p a b -> p (a b)"), a['c_ret']).then_inc(S.rdec_loaded, 16)
                act.dma_start(rrot[:, :, :].rearrange("p a b -> p (a b)"), a['c_rot']).then_inc(S.rdec_loaded, 16)
                si = a['state_ret'][l].rearrange("b (p e) k v -> p (e k) b v", e=2)
                so = o['s_ret'][l].rearrange("b (p e) k v -> p (e k) b v", e=2)
                for p in range(AP_):
                    act.dma_start(rsam[:, p, :, :], si[p]).then_inc(S.a_sample_loaded, 16)
                his(slab0(l, 'in') + 36, 32)
                attention(l, False, 2 * l)
                act.dma_start(o['p_ret'][l, 0].rearrange("(p e) k v -> (e k) p v", e=2), st[:, 1, :, :]).then_inc(S.ret_stored, 16)
                for p in range(AP_):
                    act.dma_start(so[p], rsam[:, p, :, :]).then_inc(S.ret_stored, 16)

                act.wait_ge(S.a_done, 2 * l + 1)
                si = a['state_ml_c'][l].rearrange("b (p e) k v -> p (e k) b v", e=2)
                so = o['s_mlc'][l].rearrange("b (p e) k v -> p (e k) b v", e=2)
                ni = a['state_ml_n'][l].rearrange("b (p e) k -> p (e k) b", e=2)
                no = o['s_mln'][l].rearrange("b (p e) k -> p (e k) b", e=2)
                for p in range(AP_):
                    act.dma_start(msam[:, p, :, :], si[p]).then_inc(S.a_sample_loaded, 16)
                    act.dma_start(msn[:, p, :], ni[p], allow_slow_non_contiguous=True).then_inc(S.m_n_loaded, 16)
                act.dma_start(rows[:, 4, SEQ:T], a['state_ml_m'][l].rearrange("b h -> h b"), allow_slow_non_contiguous=True).then_inc(S.m_m_loaded, 16)
                his(slab0(l, 'in') + 68, 32)
                act.wait_ge(S.m_gates_in, l + 1)
                own(A(rows[:, 0, :], rows[:, 0, :], ACT.Tanh, bias=mlb2[:, 0:1], scale=1.0 / CAP))
                own(A(rows[:, 1, :], rows[:, 1, :], ACT.Tanh, bias=mlb2[:, 1:2], scale=1.0 / CAP))
                own(A(rows[:, 1, :], rows[:, 1, :], ACT.Sigmoid, scale=CAP))
                A(rows[:, 1, :], rows[:, 1, :], ACT.Ln).then_inc(S.m_logf, 1)
                act.wait_ge(S.m_rows_x, l + 1)
                A(rows[:, 1, :], rows[:, 1, :], ACT.Exp)
                A(rows[:, 4, :], rows[:, 4, :], ACT.Exp)
                A(rows[:, 5, :], rows[:, 2, :], ACT.Exp, scale=-1.0).then_inc(S.m_rows_e, 1)
                act.wait_ge(S.m_exp_in, l + 1)
                for h in range(AH):
                    for c in range(NCH):
                        last = A(mexp[:, h, CH * c:CH * c + CH], mexp[:, h, CH * c:CH * c + CH], ACT.Exp,
                                 bias=mct[:, c, h:h + 1])
                last.then_inc(S.m_exp, 1)
                act.wait_ge(S.m_spread, 3 * l + 2)
                A(ad[:, :, :], ps[:, 0:6, 0:T], ACT.Copy).then_inc(S.m_guard_taken, 1)
                attention(l, True, 2 * l + 1)
                act.dma_start(o['p_mlc'][l, 0].rearrange("(p e) k v -> (e k) p v", e=2), st[:, 1, :, :]).then_inc(S.ml_stored, 16)
                act.dma_start(o['p_mln'][l, 0].rearrange("(p e) k -> (e k) p", e=2), nst[:, 1, :, 0], allow_slow_non_contiguous=True).then_inc(S.ml_stored, 16)
                act.dma_start(o['p_mlm'][l, 0].rearrange("(h a) -> h a", a=1), mfin[:, NS:NS + 1]).then_inc(S.ml_stored, 16)
                act.dma_start(o['s_mlm'][l].rearrange("b h -> h b"), mfin[:, 0:NS], allow_slow_non_contiguous=True).then_inc(S.ml_stored, 16)
                for p in range(AP_):
                    act.dma_start(so[p], msam[:, p, :, :]).then_inc(S.ml_stored, 16)
                    act.dma_start(no[p], msn[:, p, :], allow_slow_non_contiguous=True).then_inc(S.ml_stored, 16)

                his(slab0(l, 'out') + 4, 32)
                norm_parts(2 * l + 1)
                with act.Fori(0, FF_GROUPS) as it:
                    s = it * 16 + (slab0(l, 'up') + 4)
                    hi4(s)
                    hi4(s + 4)
                    act.wait_ge(S.slab_used, s + 4)
                    act.wait_ge(S.gated, it + (l * FF_GROUPS + 1))
                    A(sg[:, :, :], ps[:, 0:4, 0:T], ACT.Sigmoid).then_inc(S.gate_sig, 1)
                    hi4(s + 8)
                    hi4(s + 12)
                his(slab0(l, 'down') + 4, 4 * DOWN_SLABS - RING)
                if l + 1 < DEPTH:
                    hi4(slab0(l + 1, 'tail'), tail_pieces(l + 1, 0))
                norm_parts(2 * l + 2)
            for t in range(2):
                act.wait_ge(S.y_turned, t + 1)
                A(y_tok[:, t, :].rearrange("p (a b) -> p a b", a=4), ps[:, 4 * t:4 * t + 4, :], ACT.Copy).then_inc(S.y_rows, 1)
            act.wait_ge(S.y_turned, 3)
            A(y_tok[0:NS, 2, :].rearrange("p (a b) -> p a b", a=4), ps[0:NS, 0:4, :], ACT.Copy).then_inc(S.y_rows, 1)

        @block.vector
        def _(dve):
            v = nc.vector
            own = Own(dve, S.dve_steps)
            TT, TS, STT = v.tensor_tensor, v.tensor_scalar, v.scalar_tensor_tensor
            own(v.memset(eps[:, 0:1], LN_EPS))
            own(v.memset(eps[:, 1:2], NORM_EPS))
            own(v.memset(eps[:, 2:3], GN_EPS))
            dve.sem_inc(S.evacuated, 1)
            dve.sem_inc(S.gated, 1)
            v.memset(raw[:, :, :, :], 0.0).then_inc(S.raw_cleared, 1)

            def lo4(s0):
                for j in range(RING):
                    dve.wait_ge(S.hi_ready, s0 + (j + 1))
                    TT(wl[:, j, :, :], raw[:, j, :, :], wh[:, j, :, :].bitcast(F32), ALU.subtract).then_inc(S.lo_ready, 1)

            def evacuate(used, what):
                dve.wait_ge(S.slab_used, used)
                what().then_inc(S.evacuated, 1)

            def in_groups(l, first, dst, d0):
                with dve.Fori(0, 2) as it:
                    s = it * 16 + (slab0(l, 'in') + 8 * first)
                    lo4(s + 4)
                    lo4(s + 8)
                    evacuate(s + 8, lambda: v.tensor_copy(dst[:, ds(it * 8 + d0, 4), :], ps[:, 0:4, 0:TW]))
                    lo4(s + 12)
                    lo4(s + 16)
                    evacuate(s + 16, lambda: v.tensor_copy(dst[:, ds(it * 8 + (d0 + 4), 4), :], ps[:, 4:8, 0:TW]))

            def residual(blk, set_):
                STT(R[:, ds(blk, 4), :], xh[:, ds(blk, 4), 0:T].bitcast(F32), ALPHA, ps[:, set_:set_ + 4, 0:T],
                    ALU.mult, ALU.add).then_inc(S.resid_part, 1)
                return lambda: STT(R[:, ds(blk, 4), :], xl[:, ds(blk, 4), 0:T].bitcast(F32), ALPHA, R[:, ds(blk, 4), :],
                                   ALU.mult, ALU.add)

            def residual_group(used, blk, set_, count):
                dve.wait_ge(S.slab_used, used)
                second = residual(blk, set_)
                dve.wait_ge(S.resid_part, count + 1)
                second().then_inc(S.evacuated, 1)

            def norm(n, gam_, bet_, last=False):
                v.tensor_reduce(ln_s[:, :], R[:, :, :].rearrange("p b t -> p t b"), AX.X, ALU.add).then_inc(S.ln_sum, 1)
                dve.wait_ge(S.ln_sum_all, n + 1)
                own(TS(ln_m[:, :], ps[:, 0, 0:T], 1.0 / D, None, ALU.mult))
                TT(R[:, :, :], R[:, :, :], each(ln_m[:, :], KB), ALU.subtract).then_inc(S.ln_centered, 1)
                dve.wait_ge(S.ln_squared, n + 1)
                v.tensor_reduce(ln_s[:, :], SQ[:, :, :].rearrange("p b t -> p t b"), AX.X, ALU.add).then_inc(S.ln_sumsq, 1)
                dve.wait_ge(S.ln_std, n + 1)
                own(v.reciprocal(ln_m[:, :], ln_m[:, :]))
                own(TT(R[:, :, :], R[:, :, :], each(ln_m[:, :], KB), ALU.mult))
                for b in range(KB):
                    ins = TS(R[:, b, :], R[:, b, :], gam_(b), bet_(b), ALU.mult, ALU.add)
                    if b < KB - 1:
                        continue
                    if last:
                        ins.then_inc(S.x_ready, 1)
                    else:
                        own(ins)
                if not last:
                    own(v.tensor_copy(xh[:, :, 0:T], R[:, :, :]))
                    TT(xl[:, :, 0:T], R[:, :, :], xh[:, :, 0:T].bitcast(F32), ALU.subtract).then_inc(S.x_ready, 1)

            def attention(l, ml, n):
                src = pml if ml else pret
                for c in range(NCH):
                    dve.wait_ge(S.a_scored, 2 * n + c + 1)
                    if ml:
                        dve.wait_ge(S.m_exp, l + 1)
                    w = mexp[:, :, CH * c:CH * c + CH] if ml else rdec[:, 0:AH, :]
                    TT(pairs(ssb[:, c, :, :]), halves_of(4 * c, CH, AH), pairs(w), ALU.mult).then_inc(S.a_weighted, 1)
                for c in range(NCH):
                    dve.wait_ge(S.a_summed, 2 * n + c + 1)
                    if c == 0:
                        own(v.tensor_copy(st[:, 0, :, :], ps[:, 4, 0:384].rearrange("p (a b) -> p a b", a=AP_)))
                        if ml:
                            own(v.tensor_copy(nst[:, 0, :, :], ps[:, 5, 0:384].rearrange("p (a b) -> p a b", a=AP_)))
                    else:
                        for p in range(AP_):
                            sc = mdc[:, p:p + 1] if ml else gam[:, AP_ + p:AP_ + p + 1]
                            own(STT(st[:, 1, p, :], st[:, 0, p, :], sc, ps[:, 4, 128 * p:128 * p + 128], ALU.mult, ALU.add))
                            if ml:
                                own(STT(nst[:, 1, p, :], nst[:, 0, p, :], sc, ps[:, 5, 128 * p:128 * p + 128], ALU.mult, ALU.add))
                    dve.sem_inc(S.a_state_kept, 1)
                    y = v.tensor_copy(pairs(ay[:, :, CH * c:CH * c + CH]), halves_of(0, CH, AH))
                    if ml:
                        own(y)
                        dve.wait_ge(S.m_absden, 3 * l + c + 1)
                        y = TT(ad[:, :, CH * c:CH * c + CH], ad[:, :, CH * c:CH * c + CH], ssb[:, c, :, :], ALU.max)
                    y.then_inc(S.a_y_kept, 1)
                dve.wait_ge(S.a_y_kept, 2 * n + 2)
                dve.wait_ge(S.a_sample_loaded, 48 * (n + 1))
                sam, vd = (msam, mvd) if ml else (rsam, rvd)
                kv = ssb[:, :, :, :].rearrange("p c h i -> p (c h i)")[:, 0:NS * 128].rearrange("p (b v) -> p b v", v=128)
                for p in range(AP_):
                    for e in range(2):
                        h = 2 * p + e
                        if h:
                            dve.wait_ge(S.a_vspread, n * AH + h)
                        TT(vd[:, :, :], over(src[:, 2 * AP_ + h, SEQ:T], 128), each(ident, NS), ALU.mult).then_inc(S.a_vdiag, 1)
                    dve.wait_ge(S.a_vspread, n * AH + 2 * p + 2)
                    k = kw[:, p, SEQ:T] if ml else src[:, AP_ + p, SEQ:T]
                    own(TT(kv, ps[:, 6:8, :].rearrange("p a (b v) -> p (a b) v", v=128), over(k, 128), ALU.mult))
                    if ml:
                        own(TT(sam[:, p, :, :], sam[:, p, :, :], over(msk[:, p, :], 128), ALU.mult))
                        TT(sam[:, p, :, :], sam[:, p, :, :], kv, ALU.add).then_inc(S.a_pair_done, 1)
                    else:
                        STT(sam[:, p, :, :], sam[:, p, :, :], gam[:, p:p + 1], kv, ALU.mult, ALU.add).then_inc(S.a_pair_done, 1)
                    dve.wait_ge(S.a_pair_done, n * AP_ + p + 1)
                if ml:
                    dve.wait_ge(S.m_n_loaded, 48 * (l + 1))
                    own(TT(msn[:, :, :], msn[:, :, :], msk[:, :, :], ALU.mult))
                    own(TT(msn[:, :, :], msn[:, :, :], kw[:, :, SEQ:T], ALU.add))
                    TT(mpd[:, :, :], msn[:, :, :], src[:, 0:AP_, SEQ:T], ALU.mult).then_inc(S.m_nprod, 1)
                dve.wait_ge(S.a_sample_y, n + 1)
                y = v.tensor_copy(pairs(ay[:, :, SEQ:T]), halves_of(0, NS, AH))
                if ml:
                    own(y)
                    dve.wait_ge(S.m_absden, 3 * l + 3)
                    own(TT(ad[:, :, SEQ:T], ad[:, :, SEQ:T], msk_abs[:, :].rearrange("p (h b) -> p h b", b=NS), ALU.max))
                    own(v.reciprocal(ad[:, :, :], ad[:, :, :]))
                    y = TT(ay[:, :, :], ay[:, :, :], ad[:, :, :], ALU.mult)
                y.then_inc(S.a_y_ready, 1)
                dve.wait_ge(S.a_std, n + 1)
                own(v.reciprocal(ad[:, :, :], ad[:, :, :]))
                own(TT(ay[:, :, :], ay[:, :, :], ad[:, :, :], ALU.mult))
                dve.wait_ge(S.a_gate, n + 1)
                if ml:
                    own(TT(ay[:, :, :], ay[:, :, :], over(cols('ml_norm', AH), T), ALU.mult))
                    TT(ay[:, :, :], ay[:, :, :], mgate[:, :, :], ALU.mult).then_inc(S.a_out, 1)
                else:
                    own(TT(ay[:, :, :], ay[:, :, :], rtmp[:, :, :], ALU.mult))
                    TT(ay[:, :, :], ay[:, :, :], pret[:, 12:18, 0:T], ALU.mult).then_inc(S.a_out, 1)
                a0 = 10 if ml else 4
                dve.wait_ge(S.a_out_hi, n + 1)
                TT(ol[:, a0:a0 + AH, :], ay[:, :, :], oh[:, a0:a0 + AH, :].bitcast(F32), ALU.subtract).then_inc(S.a_done, 1)

            for q in range(4):
                dve.wait_ge(S.x_turned, q + 1)
                v.tensor_copy(R[:, 4 * q:4 * q + 4, :], ps[:, 4 * (q % 2):4 * (q % 2) + 4, 0:T]).then_inc(S.x_taken, 1)
            dve.wait_ge(S.prm0_turned, 1)
            own(v.tensor_copy(prm0[:, :], ps[:, 2, 0:32]))
            dve.wait_ge(S.x_taken, 4)
            norm(0, lambda b: prm0[:, b:b + 1], lambda b: prm0[:, 16 + b:17 + b])
            lo4(0)

            for l in range(DEPTH):
                dve.wait_ge(S.x_ready, 2 * l + 1)
                TT(rows9[:, :, :], xh[:, :, SEQ - 1:T].bitcast(F32), xl[:, :, SEQ - 1:T].bitcast(F32), ALU.add).then_inc(S.shift_cols, 1)
                dve.wait_ge(S.layer_turned, l + 1)
                npr = PRM_ROWS if l else PRM_ROWS - 4
                own(v.tensor_copy(prm[:, 0:npr], ps[:, 0, 0:npr]))
                own(TS(ka1[:, :], cols('rw_ka', 4), -1.0, 1.0, ALU.mult, ALU.add))
                sh = ps[:, 1, 0:128].rearrange("p (b s) -> p b s", s=NS)
                own(v.tensor_copy(xh[:, :, T:TW], sh))
                own(TT(xl[:, :, T:TW], sh, xh[:, :, T:TW].bitcast(F32), ALU.subtract))
                v.tensor_copy(shift_out[:, :].rearrange("p (a b) -> p a b", a=4), ps[0:1 + NS, 4:8, :]).then_inc(S.layer_taken, 1)

                lo4(slab0(l, 'tail') + 4)
                lo4(slab0(l, 'in'))
                evacuate(slab0(l, 'in'), lambda: v.tensor_copy(ptail[:, :, :], ps[:, 0:3, 0:TW]))
                in_groups(l, 0, praw, 0)

                dve.wait_ge(S.evacuated, group0(l, 'in') + 4)
                dve.wait_ge(S.shift_stored, 32 * (l + 1))
                own(v.tensor_copy(pret[:, 0:2, :], praw[:, 14:16, :]))
                own(TT(mx[:, 0:RW_PB, 1:SEQ], praw[:, 0:RW_PB, 0:SEQ - 1], praw[:, 0:RW_PB, 1:SEQ], ALU.subtract))
                own(TS(mx[:, 0:RW_PB, 0:1], praw[:, 0:RW_PB, 0:1], -1.0, None, ALU.mult))
                own(TT(mx[:, 0:RW_PB, SEQ:T], praw[:, 0:RW_PB, T:TW], praw[:, 0:RW_PB, SEQ:T], ALU.subtract))
                own(TT(mx[:, 0:RW_PB, :], mx[:, 0:RW_PB, :], over(cols('rw_mu', RW_PB), T), ALU.mult))
                dve.wait_ge(S.lora_loaded, 48 if l == 0 else 48 + 80 * l)
                if l:
                    g = slice(64, 96)
                    own(TT(tmp[g, 0, 1:SEQ], ptail[g, 2, 0:SEQ - 1], ptail[g, 2, 1:SEQ], ALU.subtract))
                    own(TS(tmp[g, 0, 0:1], ptail[g, 2, 0:1], -1.0, None, ALU.mult))
                    own(TT(tmp[g, 0, SEQ:T], ptail[g, 2, T:TW], ptail[g, 2, SEQ:T], ALU.subtract))
                    own(STT(ptail[g, 2, 0:T], tmp[g, 0, :], vmu[g, :], ptail[g, 2, 0:T], ALU.mult, ALU.add))
                TT(mx[:, 0:RW_PB, :], mx[:, 0:RW_PB, :], praw[:, 0:RW_PB, 0:T], ALU.add).then_inc(S.rw_mix, 1)
                dve.wait_ge(S.rw_gv_taken, l + 1)
                if l == 0:
                    own(v.tensor_copy(vfirst[:, :, :], mx[:, 8:12, :]))
                else:
                    own(TT(ep[:, :, :], vfirst[:, :, :], mx[:, 8:12, :], ALU.subtract))
                    own(TT(ep[:, :, :], ep[:, :, :], tmp[:, :, :], ALU.mult))
                    own(TT(mx[:, 8:12, :], mx[:, 8:12, :], ep[:, :, :], ALU.add))
                TT(mx[:, 14:18, :], mx[:, 4:8, :], over(cols('rw_kk', 4), T), ALU.mult).then_inc(S.rw_kk_raw, 1)
                own(TS(lw[:, :, :], lw[:, :, :], -float(np.exp(-0.5)), None, ALU.mult))
                for b in range(4):
                    for c in range(NCH):
                        cs = slice(CH * c, CH * c + CH)
                        own(v.tensor_tensor_scan(lw[:, b, cs], ones, lw[:, b, cs], 0.0, ALU.mult, ALU.add))
                mid = lw[:, :, 0:SEQ].rearrange("p b (c i) -> p b c i", i=CH)[:, :, :, CH // 2 - 1]
                own(v.tensor_copy(amid[:, :, :], mid))
                TS(namid[:, :, :], mid, -1.0, None, ALU.mult).then_inc(S.rw_cum, 1)
                dve.wait_ge(S.rw_kk_sum, l + 1)
                dve.wait_ge(S.rw_kk_sq, l + 1)
                TS(tmp[:, :, :], ps[:, 0:4, 0:T], 1e-24, None, ALU.max).then_inc(S.rw_kk_ss, 1)
                dve.wait_ge(S.rw_kk_norm, l + 1)
                own(v.reciprocal(tmp[:, :, :], tmp[:, :, :]))
                dve.wait_ge(S.rw_kk_raw, l + 1)
                own(TT(mx[:, 14:18, :], mx[:, 14:18, :], tmp[:, :, :], ALU.mult))
                own(TT(tmp[:, :, :], mx[:, 18:22, :], over(cols('rw_ka', 4), T), ALU.mult))
                own(TT(tmp[:, :, :], tmp[:, :, :], over(ka1[:, :], T), ALU.add))
                own(TT(mx[:, 4:8, :], mx[:, 4:8, :], tmp[:, :, :], ALU.mult))
                own(TT(tmp[:, :, :], mx[:, 0:4, :], mx[:, 4:8, :], ALU.mult))
                TT(tmp[:, :, :], tmp[:, :, :], over(cols('rw_rk', 4), T), ALU.mult).then_inc(S.rw_bonus_in, 1)
                own(TT(mx[:, 18:22, :], mx[:, 18:22, :], mx[:, 14:18, :], ALU.mult))
                dve.wait_ge(S.rw_bonus_sum, l + 1)
                own(TT(bonus[:, :, :], ps[:, 4:8, 0:T], mx[:, 8:12, :], ALU.mult))
                dve.wait_ge(S.rw_exps, l + 1)
                own(TT(mx[:, 4:8, 0:SEQ], mx[:, 4:8, 0:SEQ], em[:, :, 0:SEQ], ALU.mult))
                own(TT(mx[:, 18:22, 0:SEQ], mx[:, 18:22, 0:SEQ], em[:, :, 0:SEQ], ALU.mult))
                own(TT(mx[:, 0:4, 0:SEQ], mx[:, 0:4, 0:SEQ], ep[:, :, 0:SEQ], ALU.mult))
                kkv = mx[:, 14:18, 0:SEQ].rearrange("p b (c i) -> p b c i", i=CH)
                epv = ep[:, :, 0:SEQ].rearrange("p b (c i) -> p b c i", i=CH)
                own(TT(kkv[:, :, :, 1:CH], kkv[:, :, :, 1:CH], epv[:, :, :, 0:CH - 1], ALU.mult))
                own(TT(kkv[:, :, :, 0], kkv[:, :, :, 0], enam[:, :, :], ALU.mult))
                v.tensor_copy(eend[:, :, :], epv[:, :, :, CH - 1]).then_inc(S.rw_scaled, 1)
                dve.wait_ge(S.rw_scaled, l + 1)

                for c in range(NCH):
                    n = NCH * l + c
                    for q in range(2):
                        hs = slice(4 * q, 4 * q + 4)
                        dve.wait_ge(S.rw_pairs, 4 * n + 2 * q + 1)
                        pv_ = halves_of(4, 2 * CH, 4)
                        own(TT(pairs(ym[:, hs, :]), pv_[:, :, :, 0:CH], each2(masks[:, 2, :], 2), ALU.mult))
                        TT(pairs(qb[:, hs, :]), pv_[:, :, :, CH:2 * CH], each2(masks[:, 3, :], 2), ALU.mult).then_inc(S.rw_pairs_taken, 1)
                        own(STT(ym[:, hs, :], ym[:, hs, :], -1.0, each(ident, 4), ALU.mult, ALU.add))
                        dve.wait_ge(S.rw_pairs, 4 * n + 2 * q + 2)
                        TT(pairs(mq[:, hs, :, :].rearrange("p h a i -> p h (a i)")), halves_of(6, 2 * CH, 4),
                           each2(masks[:, 0:2, :].rearrange("p a i -> p (a i)"), 2), ALU.mult).then_inc(S.rw_pairs_taken, 1)
                    dve.wait_ge(S.rw_l, n + 1)
                    own(v.tensor_copy(pairs(lm[:, :, :]), halves_of(0, CH, RW_HEADS)))
                    own(TT(tm[:, :, :], lm[:, :, :], each(masks[:, 5, :], RW_HEADS), ALU.mult))
                    own(STT(tm[:, :, :], tm[:, :, :], -1.0, each(ident, RW_HEADS), ALU.mult, ALU.add))
                    for q in range(2):
                        hs = slice(4 * q, 4 * q + 4)
                        TT(lmk[:, hs, :], lm[:, hs, :], each(masks[:, 6, :], 4), ALU.mult).then_inc(S.rw_masked, 1)
                    for lev in range(6):
                        for q in range(2):
                            m = 12 * n + 2 * lev + q
                            hs = slice(4 * q, 4 * q + 4)
                            dve.wait_ge(S.rw_tx, m + 1)
                            yx = ps[:, 3 + 2 * q, :].rearrange("p (h i) -> p h i", i=CH)
                            if lev == 5:
                                TT(ym[:, hs, :], ym[:, hs, :], yx, ALU.subtract).then_inc(S.rw_inverted, 1)
                                continue
                            own(TT(lmk[:, hs, :], lm[:, hs, :], each(masks[:, 7 + lev, :], 4), ALU.mult))
                            own(TT(tm[:, hs, :], tm[:, hs, :], ps[:, 2 + 2 * q, :].rearrange("p (h i) -> p h i", i=CH), ALU.subtract))
                            TT(ym[:, hs, :], ym[:, hs, :], yx, ALU.subtract).then_inc(S.rw_masked, 1)
                    dve.wait_ge(S.rw_y, n + 1)
                    for e in range(2):
                        r = slice(64 * e, 64 * e + 64)
                        own(v.tensor_copy(yt[r, :, CH * c:CH * c + CH], ps[r, 3 * e, :].rearrange("p (b i) -> p b i", i=CH)))
                    upd = ps[:, 1, 0:256].rearrange("p (b i) -> p b i", i=64)
                    if c:
                        own(TT(zst[:, :, :], zst[:, :, :], upd, ALU.add))
                        TT(zst[:, :, :], zst[:, :, :], over(eend[:, :, c], 64), ALU.mult).then_inc(S.rw_chunk_done, 1)
                    else:
                        own(TT(zst[:, :, :], upd, over(eend[:, :, c], 64), ALU.mult))
                        TT(zst[:, :, :], zst[:, :, :], over(eamid[:, :, c + 1], 64), ALU.mult).then_inc(S.rw_chunk_done, 1)
                dve.wait_ge(S.rw_sample_loaded, 64 * (l + 1))

                def sam(b0):
                    return mx[:, b0:b0 + 4, SEQ:T].unsqueeze(3).to_broadcast([128, 4, NS, 64])
                id4 = ident2[:, :].unsqueeze(1).unsqueeze(1).to_broadcast([128, 4, NS, 64])
                TT(s1t[:, :, :, :], srw[:, :, :, :], sam(14), ALU.mult).then_inc(S.rw_sample_in, 1)
                TT(s2t[:, :, :, :], sam(8), id4, ALU.mult).then_inc(S.rw_sample_in, 1)
                own(TT(srw[:, :, :, :], srw[:, :, :, :], wsam[:, :, :].unsqueeze(3).to_broadcast([128, 4, NS, 64]), ALU.mult))
                dve.wait_ge(S.rw_sample_sum, 3 * l + 1)
                spread = (lambda b: ps[:, b:b + 4, :].rearrange("p a (b v) -> p a b v", v=64))
                own(TT(s1t[:, :, :, :], spread(0), sam(18), ALU.mult))
                own(TT(srw[:, :, :, :], srw[:, :, :, :], s1t[:, :, :, :], ALU.subtract))
                dve.wait_ge(S.rw_sample_sum, 3 * l + 2)
                own(TT(s1t[:, :, :, :], spread(4), sam(4), ALU.mult))
                TT(srw[:, :, :, :], srw[:, :, :, :], s1t[:, :, :, :], ALU.add).then_inc(S.rw_sample_new, 1)
                dve.wait_ge(S.rw_sample_new, l + 1)
                TT(s1t[:, :, :, :], srw[:, :, :, :], sam(0), ALU.mult).then_inc(S.rw_sample_in, 1)
                dve.wait_ge(S.rw_sample_sum, 3 * l + 3)
                own(TT(s2t[:, :, :, :], spread(0), id4, ALU.mult))
                v.tensor_reduce(yt[:, :, SEQ:T], s2t[:, :, :, :], AX.X, ALU.add).then_inc(S.rw_gn_in, 1)
                dve.wait_ge(S.rw_gn_sum, 2 * l + 1)
                STT(yt[:, :, :], ps[:, 4:8, 0:T], -1.0 / RW_HD, yt[:, :, :], ALU.mult, ALU.add).then_inc(S.rw_gn_c, 1)
                dve.wait_ge(S.rw_gn_std, l + 1)
                own(v.reciprocal(tmp[:, :, :], tmp[:, :, :]))
                own(TT(yt[:, :, :], yt[:, :, :], tmp[:, :, :], ALU.mult))
                own(TT(yt[:, :, :], yt[:, :, :], over(cols('rw_lnx_g', 4), T), ALU.mult))
                own(TT(yt[:, :, :], yt[:, :, :], over(cols('rw_lnx_b', 4), T), ALU.add))
                own(TT(yt[:, :, :], yt[:, :, :], bonus[:, :, :], ALU.add))
                TT(yt[:, :, :], yt[:, :, :], gate[:, :, :], ALU.mult).then_inc(S.rw_out, 1)
                dve.wait_ge(S.rw_out_hi, l + 1)
                TT(ol[:, 0:4, :], yt[:, :, :], oh[:, 0:4, :].bitcast(F32), ALU.subtract).then_inc(S.rw_done, 1)

                in_groups(l, 4, pret, 2)
                dve.wait_ge(S.evacuated, group0(l, 'in') + 8)
                dve.wait_ge(S.rdec_loaded, 32 * (l + 1))
                TT(kw[:, :, SEQ:T], pret[:, 0:AP_, SEQ:T], pret[:, 0:AP_, SEQ:T], ALU.add).then_inc(S.ret_in, 1)
                dve.wait_ge(S.ret_swapped, l + 1)
                own(TT(rtmp[:, :, :], ps[:, 0:6, 0:T], each(rrot[:, 1, :], AH), ALU.mult))
                own(TT(pret[:, 0:6, 0:T], pret[:, 0:6, 0:T], each(rrot[:, 0, :], AH), ALU.mult))
                own(TT(pret[:, 0:6, 0:T], pret[:, 0:6, 0:T], rtmp[:, :, :], ALU.add))
                own(TS(pret[:, 3:6, 0:T], pret[:, 3:6, 0:T], 0.125, None, ALU.mult))
                for dst, b0, t0 in ((qs, 0, AH), (kw, AP_, AH + AP_)):
                    for c in range(NCH):
                        cs = slice(CH * c, CH * c + CH)
                        last = TT(dst[:, :, cs], pret[:, b0:b0 + AP_, cs], rdec[:, t0:t0 + AP_, :], ALU.mult)
                last.then_inc(S.a_prepared, 1)
                attention(l, False, 2 * l)

                dve.wait_ge(S.ret_stored, 64 * (l + 1))
                in_groups(l, 8, pml, 0)
                dve.wait_ge(S.evacuated, group0(l, 'in') + 12)
                dve.wait_ge(S.mlb_loaded, 32 * (l + 1))
                own(TS(mlb2[:, :], mlb[:, :], 1.0 / CAP, None, ALU.mult))
                own(v.tensor_copy(rows[:, 0, :], ptail[0:AH, 2, 0:T]))
                v.tensor_copy(rows[:, 1, :], ptail[32:32 + AH, 2, 0:T]).then_inc(S.m_gates_in, 1)
                own(TS(pml[:, AP_:2 * AP_, 0:T], pml[:, AP_:2 * AP_, 0:T], 0.125, None, ALU.mult))
                dve.wait_ge(S.m_logf, l + 1)
                for c in range(NCH):
                    cs = slice(CH * c, CH * c + CH)
                    own(v.tensor_tensor_scan(rows[:, 2, cs], ones[0:AH, :], rows[:, 1, cs], 0.0, ALU.mult, ALU.add))
                own(v.tensor_copy(rows[:, 2, SEQ:T], rows[:, 1, SEQ:T]))
                STT(rows[:, 0, :], rows[:, 0, :], CAP, rows[:, 2, :], ALU.mult, ALU.subtract).then_inc(S.m_rows_c, 1)
                dve.wait_ge(S.m_rows_c, l + 1)
                dve.wait_ge(S.m_m_loaded, 16 * (l + 1))
                own(v.memset(rows[:, 4, 0:CH], 0.0))
                for c in range(NCH):
                    cs = slice(CH * c, CH * c + CH)
                    own(v.tensor_tensor_scan(rows[:, 3, cs], rows[:, 0, cs], rows[:, 0, cs], mcol[:, :] if c else 0.0, ALU.max, ALU.max))
                    if c + 1 < NCH:
                        own(TT(mcol[:, :], rows[:, 2, CH * c + CH - 1:CH * c + CH], rows[:, 3, CH * c + CH - 1:CH * c + CH], ALU.add))
                        own(v.tensor_copy(rows[:, 4, CH * c + CH:CH * c + 2 * CH], mcol[:, :].to_broadcast([AH, CH])))
                TT(rows[:, 3, SEQ:T], rows[:, 0, SEQ:T], rows[:, 4, SEQ:T], ALU.max).then_inc(S.m_rows_m, 1)
                dve.wait_ge(S.m_rows_m, l + 1)
                own(TT(rows[:, 2, :], rows[:, 2, :], rows[:, 3, :], ALU.add))
                own(v.tensor_copy(mfin[:, 0:NS], rows[:, 2, SEQ:T]))
                own(v.tensor_copy(mfin[:, NS:NS + 1], rows[:, 2, SEQ - 1:SEQ]))
                for c in range(NCH):
                    cs = slice(CH * c, CH * c + CH)
                    own(TS(rows[:, 1, cs], rows[:, 0, cs], rows[:, 3, CH * c + CH - 1:CH * c + CH], None, ALU.subtract))
                own(TT(rows[:, 1, SEQ:T], rows[:, 0, SEQ:T], rows[:, 3, SEQ:T], ALU.subtract))
                TT(rows[:, 4, :], rows[:, 4, :], rows[:, 3, :], ALU.subtract).then_inc(S.m_rows_x, 1)
                dve.wait_ge(S.m_spread, 3 * l + 1)
                own(v.tensor_copy(mct[:, :, :], ps[:, 6, 0:16].rearrange("p (c h) -> p c h", h=8)[:, :, 0:AH]))
                negm = masks[:, 4, :].unsqueeze(1).unsqueeze(1).to_broadcast([128, AH, NCH, CH])
                TT(mexp[:, :, :].rearrange("p h (c i) -> p h c i", i=CH), negm,
                   ps[:, 0:AH, 0:SEQ].rearrange("p h (c i) -> p h c i", i=CH), ALU.subtract).then_inc(S.m_exp_in, 1)
                dve.wait_ge(S.m_spread, 3 * l + 3)
                own(TT(kw[:, :, :], pml[:, AP_:2 * AP_, 0:T], ps[:, 3:6, 0:T], ALU.mult))
                own(v.tensor_copy(msk[:, :, :], ps[:, 0:3, SEQ:T]))
                own(v.tensor_copy(mdc[:, :], ps[:, 0:3, SEQ - 1]))
                TT(qs[:, :, :], pml[:, 0:AP_, 0:T], ps[:, 0:3, 0:T], ALU.mult).then_inc(S.a_prepared, 1)
                attention(l, True, 2 * l + 1)

                dve.wait_ge(S.ml_stored, 160 * (l + 1))
                with dve.Fori(0, 2) as it:
                    s = it * 16 + slab0(l, 'out')
                    lo4(s + 4)
                    lo4(s + 8)
                    residual_group(s + 8, it * 8, 0, it * 2 + 8 * l)
                    lo4(s + 12)
                    lo4(s + 16)
                    residual_group(s + 16, it * 8 + 4, 4, it * 2 + (8 * l + 1))
                dve.wait_ge(S.evacuated, group0(l, 'out') + 4)
                norm(2 * l + 1, lambda b: col('ln1_g', b), lambda b: col('ln1_b', b))
                dve.wait_ge(S.x_ready, 2 * l + 2)

                with dve.Fori(0, FF_GROUPS) as it:
                    s = it * 16 + slab0(l, 'up')
                    lo4(s + 4)
                    lo4(s + 8)
                    dve.wait_ge(S.gate_sig, it + (l * FF_GROUPS + 1))
                    TT(gu[:, :, :], sg[:, :, :], ps[:, 0:4, 0:T], ALU.mult).then_inc(S.evacuated, 1)
                    dve.wait_ge(S.evacuated, it * 2 + (group0(l, 'up') + 1))
                    dve.sem_inc(S.gated, 1)
                    lo4(s + 12)
                    lo4(s + 16)
                    dve.wait_ge(S.slab_used, s + 16)
                    TT(gu[:, :, :], gu[:, :, :], ps[:, 4:8, 0:T], ALU.mult).then_inc(S.evacuated, 1)
                    dve.wait_ge(S.evacuated, it * 2 + (group0(l, 'up') + 2))
                    v.tensor_copy(hh[:, ds(it * 4, 4), :], gu[:, :, :]).then_inc(S.hidden_hi, 1)
                    dve.wait_ge(S.hidden_hi, it + (l * FF_GROUPS + 1))
                    TT(hl[:, ds(it * 4, 4), :], gu[:, :, :], hh[:, ds(it * 4, 4), :].bitcast(F32), ALU.subtract).then_inc(S.hidden_ready, 1)

                def down(s, blk, before, more):
                    for k in range(4, 24, 4):
                        lo4(s + k)
                    residual_group(s + DOWN_SLABS, blk, 0, before)
                    for k in range(24, 48 if more else 44, 4):
                        lo4(s + k)
                    residual_group(s + 2 * DOWN_SLABS, blk + 4, 4, before + 1)
                dve.wait_ge(S.hidden_ready, FF_GROUPS * (l + 1))
                if l + 1 < DEPTH:
                    with dve.Fori(0, 2) as it:
                        down(it * (2 * DOWN_SLABS) + slab0(l, 'down'), it * 8, it * 2 + (8 * l + 4), True)
                else:
                    down(slab0(l, 'down'), 0, 8 * l + 4, True)
                    down(slab0(l, 'down') + 2 * DOWN_SLABS, 8, 8 * l + 6, False)
                dve.wait_ge(S.evacuated, group0(l, 'down') + 4)
                norm(2 * l + 2, lambda b: col('ln2_g', b), lambda b: col('ln2_b', b), last=l + 1 == DEPTH)


_NAMES = ['x_prompt', 'x_sample', 'state_rw_shift', 'state_rw_wkv', 'state_ret', 'state_ml_c', 'state_ml_n', 'state_ml_m',
          'ln0_g', 'ln0_b', 'w_in', 'rw_mu', 'rw_w0', 'rw_w2', 'rw_a0', 'rw_a2', 'rw_g2', 'rw_kk', 'rw_ka', 'rw_rk',
          'rw_lnx_g', 'rw_lnx_b', 'rw_v0', 'rw_v1', 'rw_vmu', 'rw_v2', 'ml_ib', 'ml_fb', 'ml_norm', 'w_out',
          'ln1_g', 'ln1_b', 'w_gate', 'w_up', 'w_down', 'ln2_g', 'ln2_b']
_OUTS = [('y_prompt', (1, SEQ, D)), ('y_sample', (NS, 1, D)),
         ('p_shift', (DEPTH, 1, D)), ('p_wkv', (DEPTH, 1, RW_HEADS, RW_HD, RW_HD)), ('p_ret', (DEPTH, 1, AH, 64, AV)),
         ('p_mlc', (DEPTH, 1, AH, 64, AV)), ('p_mln', (DEPTH, 1, AH, 64)), ('p_mlm', (DEPTH, 1, AH)),
         ('s_shift', (DEPTH, NS, D)), ('s_wkv', (DEPTH, NS, RW_HEADS, RW_HD, RW_HD)), ('s_ret', (DEPTH, NS, AH, 64, AV)),
         ('s_mlc', (DEPTH, NS, AH, 64, AV)), ('s_mln', (DEPTH, NS, AH, 64)), ('s_mlm', (DEPTH, NS, AH))]


def kernel(**inputs):
    from concourse import bacc
    from concourse.bass_utils import run_bass_kernel_spmd

    nc = bacc.Bacc("TRN2", target_bir_lowering=False, num_devices=1, dynamic_dma_scratch_size=64)
    arrays, a = {}, {}
    for name in _NAMES:
        arrays["in_" + name] = np.ascontiguousarray(inputs[name])
    for name, table in constants().items():
        arrays["in_" + name] = table
    for name, x in arrays.items():
        a[name[3:]] = nc.dram_tensor(name, x.shape, mybir.dt.from_np(x.dtype), kind="ExternalInput").ap()
    o = {name: nc.dram_tensor("out_" + name, shape, F32, kind="ExternalOutput").ap() for name, shape in _OUTS}
    build(nc, a, o)
    r = run_bass_kernel_spmd(nc, [arrays], core_ids=[0])
    return tuple(r.results[0]["out_" + name] for name, _ in _OUTS)
```

```python
import numpy as np
import concourse.bass as bass
from concourse import mybir

F32 = mybir.dt.float32
F32R = mybir.dt.float32r
ALU = mybir.AluOpType
ACT = mybir.ActivationFunctionType
AX = mybir.AxisListType

D = 2048
SEQ, NS = 256, 8
T = SEQ + NS
TW = T + NS
DEPTH = 2
KB = D // 128
CH = 128
NCH = SEQ // CH
RW_W, RW_HEADS, RW_HD = 512, 8, 64
RW_BLK = RW_W // 128
RW_P = 3 * RW_W + 64 + 64 + 128
RW_PB = RW_P // 128
AH, AP_, AV = 6, 3, 128
P_TOTAL = 6412
PAST = 2048
D_FF = 5632
FB = D_FF // 128
ALPHA = (2 * DEPTH) ** 0.25
LN_EPS, NORM_EPS, GN_EPS = 1e-5, 1e-6, 64e-5
CAP = 15.0
GC = 512
RING = 4

PRM = [('rw_mu', RW_PB), ('rw_w0', 4), ('rw_a0', 4), ('rw_kk', 4), ('rw_ka', 4), ('rw_rk', 4), ('rw_lnx_g', 4),
       ('rw_lnx_b', 4), ('ml_norm', AH), ('ln1_g', KB), ('ln1_b', KB), ('ln2_g', KB), ('ln2_b', KB), ('rw_v0', 4)]
PRM_AT, _n = {}, 0
for _name, _rows in PRM:
    PRM_AT[_name] = _n
    _n += _rows
PRM_ROWS = _n

TAIL_SLABS = KB // 2
GROUP_SLABS = KB // 2
IN_GROUPS = 12
DOWN_SLABS = FB // 2
FF_GROUPS = D_FF // GC
LAYER_SLABS = TAIL_SLABS + IN_GROUPS * GROUP_SLABS + 4 * GROUP_SLABS + 2 * FF_GROUPS * GROUP_SLABS + 4 * DOWN_SLABS
LAYER_GROUPS = 1 + IN_GROUPS + 4 + 2 * FF_GROUPS + 4
TOTAL_SLABS = DEPTH * LAYER_SLABS


def constants():
    f = np.float32
    p, q = np.arange(128)[:, None], np.arange(128)[None, :]
    ident = (p == q)
    half = (p // 64 == q // 64)
    swap = (q == (p ^ 32))
    base = np.concatenate([ident, half, swap, np.ones((128, 128))], 1).astype(f)
    ident2 = (p % 64 == np.arange(64)[None, :]).astype(f)
    strict, incl = (p < q), (p <= q)
    neg = np.where(incl, 0.0, -1e30)
    first = ((p // 2 == q // 2) & (p < q))
    levels = [((p // (2 * n) == q // (2 * n)) & (p % (2 * n) >= n) & (q % (2 * n) < n)) for n in (1, 2, 4, 8, 16, 32, 64)]
    masks = np.concatenate([strict, incl, first, incl, neg] + levels, 1).astype(f)
    inv = (f(10000.0) ** (-np.arange(32, dtype=f) / f(32))).astype(f)
    pos = np.concatenate([np.arange(SEQ), np.full(NS, PAST)]).astype(f)
    ang = (pos[None, :] * inv[:, None]).astype(f).astype(np.float64)
    cos = np.tile(np.cos(ang), (4, 1))
    sin = np.concatenate([-np.sin(ang), np.sin(ang)] * 2, 0)
    rot = np.concatenate([cos, sin], 1).astype(f)
    lg = np.log1p(-np.exp2(-5.0 - np.arange(AH)))
    idx = np.arange(CH)
    rel = idx[None, :] - idx[:, None]
    dmask = [np.where(rel >= 0, np.exp(np.maximum(rel, 0) * g), 0.0) for g in lg]
    ofhalf = lambda pr: lg[2 * pr + np.arange(128) // 64][:, None]
    qdec = [np.exp((idx + 1.0)[None, :] * ofhalf(pr)) for pr in range(AP_)]
    kend = [np.exp((CH - 1.0 - idx)[None, :] * ofhalf(pr)) for pr in range(AP_)]
    ret = np.concatenate(dmask + qdec + kend, 1).astype(f)
    gam = np.concatenate([np.exp(ofhalf(pr)) for pr in range(AP_)] + [np.exp(CH * ofhalf(pr)) for pr in range(AP_)], 1).astype(f)
    sel = np.zeros((RW_HEADS, AH + 4, 128), f)
    for h in range(RW_HEADS):
        if h < AH:
            sel[h, h, :] = 1
        sel[h, AH + h // 2, 64 * (h % 2):64 * (h % 2) + 64] = 1
    head = np.arange(128) // 64
    whole = np.concatenate([np.tile(np.arange(AH) == h, (128, 1)) for h in range(AH)], 1)
    pair6 = np.concatenate([2 * p + head[:, None] == np.arange(AH)[None] for p in range(AP_)], 1)
    pair8 = np.concatenate([2 * p + head[:, None] == np.arange(RW_HEADS)[None] for p in range(4)], 1)
    sums = np.concatenate([whole, pair6, pair8], 1).astype(f)
    return {'c_base': base, 'c_ident2': ident2, 'c_masks': masks, 'c_rot': rot, 'c_ret': ret, 'c_gam': gam,
            'c_sel': sel.reshape(RW_HEADS, -1), 'c_sums': sums}


def build(nc, a, o):
    mm, tr = nc.tensor.matmul, nc.tensor.transpose
    ds = bass.ds

    here = [-(-nc.sbuf_base // 32) * 32]

    def put(name, shape, dt=F32):
        n = int(np.prod(shape[1:])) * 4
        t = nc.alloc_sbuf_tensor_at(name, shape, dt, offset=here[0])
        here[0] += -(-n // 32) * 32
        return t

    xh = put("x_hi", [128, KB, TW], F32R)
    xl = put("x_lo", [128, KB, TW], F32R)
    raw = put("w_raw", [128, RING, 2, GC])
    wh = put("w_hi", [128, RING, 2, GC], F32R)
    wl = put("w_lo", [128, RING, 2, GC], F32R)
    vfirst = put("v_first", [128, RW_BLK, T])
    prm2 = put("params", [128, 2, 128])
    prm0 = put("params_ln0", [128, 32])
    base = put("base_tables", [128, 4, 128])
    ident2 = put("ident2", [128, 64])
    masks = put("masks", [128, 12, 128])
    gam = put("gammas", [128, 2 * AP_])
    sel = put("selectors", [RW_HEADS, AH + 4, 128])
    sums = put("sum_selectors", [128, AH * AH + AP_ * AH + 4 * RW_HEADS])
    eps = put("eps", [128, 4])
    whole6 = lambda h: sums[:, AH * h:AH * h + AH]
    pair6 = lambda p: sums[:, AH * AH + AH * p:AH * AH + AH * p + AH]
    pair8 = lambda p: sums[:, AH * AH + AP_ * AH + 8 * p:AH * AH + AP_ * AH + 8 * p + 8]
    ident, halves, swap, ones = (base[:, i, :] for i in range(4))

    arena = here[0]

    def at(name, off, shape, dt=F32):
        assert arena + off + int(np.prod(shape[1:])) * 4 <= nc.sbuf_usable_end, name
        return nc.alloc_sbuf_tensor_at(name, shape, dt, offset=arena + off)

    BLK, BLW = T * 4, TW * 4
    O_H, O_L = 0, KB * BLK
    P_RET = 2 * KB * BLK
    P_MX = P_RET + 18 * BLW
    P_RAW = P_MX + 22 * BLK
    P_T = P_RAW + 16 * BLW
    P_END = P_T + 24 * BLK
    oh = at("o_hi", O_H, [128, KB, T], F32R)
    ol = at("o_lo", O_L, [128, KB, T], F32R)
    pret = at("p_ret", P_RET, [128, 18, TW])
    mx = at("rw_mixed", P_MX, [128, 22, T])
    praw = at("p_rw", P_RAW, [128, 16, TW])
    gate = at("rw_gate", P_T, [128, 4, T])
    bonus = at("rw_bonus", P_T + 4 * BLK, [128, 4, T])
    lw = at("rw_logw", P_T + 8 * BLK, [128, 4, T])
    ep = at("rw_ep", P_T + 12 * BLK, [128, 4, T])
    em = at("rw_em", P_T + 16 * BLK, [128, 4, T])
    tmp = at("rw_tmp", P_T + 20 * BLK, [128, 4, T])
    hh = at("h_hi", 0, [128, FB, T], F32R)
    hl = at("h_lo", FB * BLK, [128, FB, T], F32R)
    R = at("resid", 2 * FB * BLK, [128, KB, T])
    sg = at("sig_gate", (2 * FB + KB) * BLK, [128, 4, T])
    gu = at("gate_up", (2 * FB + KB + 4) * BLK, [128, 4, T])
    SQ = at("ln_squares", 0, [128, KB, T])
    small = [P_END]

    def little(name, shape, dt=F32):
        t = at(name, small[0], shape, dt)
        small[0] += -(-int(np.prod(shape[1:])) * 4 // 32) * 32
        return t

    ln_s = little("ln_sum", [128, T])
    ln_m = little("ln_stat", [128, T])
    ptail = little("p_tail", [128, 3, TW])
    prm_tok = at("params_rows", P_RAW, [PRM_ROWS, 128])
    prm0_tok = at("params0_rows", P_RAW + 512, [32, 128])
    mlb = little("ml_bias", [AH, 2])
    vmu = little("v_mu", [96, 1])
    ka1 = little("one_minus_ka", [128, 4])
    amid = little("rw_amid", [128, 4, NCH])
    namid = little("rw_namid", [128, 4, NCH])
    eamid = little("rw_eamid", [128, 4, NCH])
    wsam = little("rw_wsam", [128, 4, NS])
    enam = little("rw_enamid", [128, 4, NCH])
    eend = little("rw_eend", [128, 4, NCH])
    mlb2 = little("ml_bias_scaled", [AH, 2])
    mfin = little("m_final", [AH, NS + 1])
    mcol = little("m_carried", [AH, 1])
    rows9 = little("shift_cols", [128, KB, 1 + NS])
    mq = at("rw_mq", P_RAW, [128, RW_HEADS, 2, CH])
    tok = at("rw_tok", P_RAW + 8192, [128, 3, RW_W])
    zst = at("rw_state", P_RAW + 8192 + 6144, [128, 4, 64])
    tm = at("rw_t", P_T + 8 * BLK, [128, RW_HEADS, CH])
    ym = at("rw_tT", P_T + 8 * BLK + 4096, [128, RW_HEADS, CH])
    xm = at("rw_x", P_T + 8 * BLK + 8192, [128, RW_HEADS, CH])
    lm = at("rw_l", P_T + 8 * BLK + 12288, [128, RW_HEADS, CH])
    qb = at("rw_qb", O_H + 4352, [128, RW_HEADS, CH])
    lmk = at("rw_lmask", O_H + 8448, [128, RW_HEADS, CH])
    wsb = at("rw_w", O_H + 12544, [128, RW_W])
    usb = at("rw_u", O_H + 14592, [128, RW_W])
    yt = at("rw_y", O_L + 4352, [128, 4, T])
    lora = at("rw_lora", O_L + 8576, [128, 3, RW_W])
    srw = at("rw_sample", O_L + 8576, [128, 4, NS, 64])
    s1t = at("rw_sample_t1", P_RAW, [128, 4, NS, 64])
    s2t = at("rw_sample_t2", P_T + 8 * BLK, [128, 4, NS, 64])
    shift_tok = at("shift_rows", P_RET, [NS, D])
    shift_out = at("shift_out", P_RET + 8192, [1 + NS, D])
    B0 = P_MX + 16 * BLW + 12288
    kw = at("a_kw", B0, [128, AP_, T])
    qs = at("a_qs", B0 + 3168, [128, AP_, T])
    ktok = at("a_ktok", B0 + 6336, [128, NCH, AP_ * 128])
    vtok = at("a_vtok", B0 + 9408, [128, NCH, AH * 128])
    ssb = at("a_scores", B0 + 15552, [128, 2, AH, CH])
    st = at("a_state", B0 + 21696, [128, 2, AP_, 128])
    men = at("m_guard", B0 + 24768, [AH, T])
    mdn = at("m_den", B0 + 24768 + 1056, [AH, T])
    ay = at("a_y", B0 + 27840, [128, AH, T])
    sq = at("a_squares", B0, [128, AH, T])
    assert B0 + 34176 <= P_END
    rtmp = at("r_tmp", B0 + 6336, [128, AH, T])
    rsam = at("r_sample", P_MX + 16 * BLW, [128, AP_, NS, 128])
    rvd = at("r_vdiag", O_L + 10 * BLK + 2112, [128, NS, 128])
    rdec = at("r_decays", O_H + 10 * BLK, [128, 12, 128])
    rrot = at("r_rotary", O_L + 10 * BLK, [128, 2, T])
    mgate = at("m_gate", B0 + 6336, [128, AH, T])
    pml = at("p_ml", P_MX, [128, 16, TW])
    mexp = at("m_exp", P_RET, [128, AH, SEQ])
    mvd = at("m_vdiag", P_RET, [128, NS, 128])
    msam = at("m_sample", P_RET + 6144, [128, AP_, NS, 128])
    rows = at("m_rows", B0 + 27840, [AH, 6, T])
    mnq = at("m_nq", P_MX + 16 * BLW, [128, AP_, CH])
    mnt = at("m_ntmp", B0 + 26880, [128, AP_])
    mnc = at("m_ncols", B0 + 26912, [128, 2, AP_])
    mct = at("m_ct", B0 + 26944, [128, NCH, AH])
    msn = at("m_nsample", B0 + 27008, [128, AP_, NS])
    msk = at("m_scol", B0 + 27104, [128, AP_, NS])
    mpd = at("m_nprod", B0 + 27200, [128, AP_, NS])
    mdc = at("m_cdecay", B0 + 27296, [128, AP_])
    x_tok = at("x_rows", 0, [128, 3, D])
    y_tok = at("y_rows", 0, [128, 3, D])

    ps = nc.alloc_psum_tensor("psum", [128, 8, 512], F32)

    made = {}

    class Names:
        def __getattr__(self, name):
            if name not in made:
                made[name] = nc.alloc_semaphore(name)
            return made[name]
    S = Names()
    raw_loaded = [nc.alloc_semaphore(f"raw_loaded{i}") for i in range(RING)]
    tail_loaded = [nc.alloc_semaphore(f"tail_loaded{i}") for i in range(RING)]

    class Own:
        def __init__(self, eng, sem):
            self.eng, self.sem, self.n = eng, sem, 0

        def __call__(self, ins):
            self.n += 1
            ins.then_inc(self.sem, 1)
            self.eng.wait_ge(self.sem, self.n)

    def cols(l, name, n):
        return prm2[:, l % 2, PRM_AT[name]:PRM_AT[name] + n]

    def col(l, name, i):
        return prm2[:, l % 2, PRM_AT[name] + i:PRM_AT[name] + i + 1]

    def over(ap, n):
        return ap.unsqueeze(2).to_broadcast([ap.shape[0], ap.shape[1], n])

    def each(ap, m):
        return ap.unsqueeze(1).to_broadcast([ap.shape[0], m, ap.shape[1]])

    def hb(h, b0, w):
        return b0 + h % 2, slice(w * (h // 2), w * (h // 2) + w)

    def halves_of(b0, w, n):
        return ps[:, b0:b0 + 2, 0:w * (n // 2)].rearrange("p e (q i) -> p q e i", i=w)

    def pairs(ap):
        return ap.rearrange("p (q e) i -> p q e i", e=2)

    def each2(ap, m):
        return ap.unsqueeze(1).unsqueeze(1).to_broadcast([ap.shape[0], m, 2, ap.shape[1]])

    def slab0(l, part):
        n = l * LAYER_SLABS
        for name, slabs in (('tail', TAIL_SLABS), ('in', IN_GROUPS * 8), ('out', 32), ('up', 16 * FF_GROUPS),
                            ('down', 4 * DOWN_SLABS)):
            if name == part:
                return n
            n += slabs

    def group0(l, part):
        n = 1 + l * LAYER_GROUPS
        for name, groups in (('tail', 1), ('in', IN_GROUPS), ('out', 4), ('up', 2 * FF_GROUPS), ('down', 4)):
            if name == part:
                return n
            n += groups

    def plan(steps, blocks):
        at_, out = 0, {}
        for name, n in steps:
            at_ = min(at_ + n, blocks)
            out[name] = at_
        out['end'] = blocks
        return out

    rw_steps = [('in', 12), ('a', 1), ('g', 1), ('v', 1), ('kk', 3), ('kks', 1), ('bonus', 5)]
    for c in range(NCH):
        rw_steps += [(f'tok{c}', 2), (f'pairs{c}', 0), (f'more{c}', 1), (f'l{c}', 1)]
        for lev in range(6):
            rw_steps += [(f'x{c}.{lev}', 1), (f'y{c}.{lev}', 0)]
        rw_steps += [(f'w{c}', 1), (f'u{c}', 1), (f'out{c}', 1)]
    rw_steps += [('sa', 3), ('sv', 2), ('sy', 5), ('gn', 3), ('gnss', 2), ('gnsp', 1)]
    ret_steps = [('swap', 1), ('swap1', 2), ('turn0', 6), ('turn1', 1), ('score', 1), ('num0', 2), ('num1', 3)]
    ret_steps += [(f'v{p}', 5) for p in range(AP_)] + [('sy', 4), ('sumsq', 2), ('spread', 2), ('spread1', 1)]
    BEHIND = 32
    rw_plan, ret_plan = plan(rw_steps, 2 * BEHIND), plan(ret_steps, 2 * BEHIND)
    no_plan = None

    class Parts:
        def __init__(self, plan_, one):
            self.i, self.one, self.goals, before = 0, one, {}, 0
            for name, n in (plan_ or {}).items():
                self.goals[name] = max(before // 2, n // 2 - 2)
                before = n
            if plan_:
                self.goals['end'] = BEHIND
            self.names = list(self.goals)
            self.goal = self.goals[self.names[0]] if plan_ else 0

        def step(self):
            if self.i < self.goal:
                self.one(self.i)
                self.i += 1

        def to(self, name):
            if not self.goals:
                return
            self.goal = self.goals[name]
            while self.i < self.goal:
                self.step()
            following = self.names.index(name) + 1
            if following < len(self.names):
                self.goal = self.goals[self.names[following]]

    block = nc.Block()
    with block:
        @block.sync
        def _(sp):
            def free(s):
                if not (isinstance(s, int) and s < RING):
                    sp.wait_ge(S.hi_ready, s - RING + 1)
                    sp.wait_ge(S.lo_ready, s - RING + 1)

            def load(s, j, src, k0, c0):
                free(s)
                sp.dma_start(raw[:, j % RING, :, :], src[:, k0:k0 + 2, ds(c0, GC)]).then_inc(raw_loaded[j % RING], 16)

            sp.wait_ge(S.raw_cleared, 1)
            for l in range(DEPTH):
                win = a['w_in'][l].rearrange("(k p) n -> p k n", p=128)
                c0 = IN_GROUPS * GC
                for j in range(TAIL_SLABS):
                    s = slab0(l, 'tail') + j
                    free(s)
                    rj = raw[:, j % RING]
                    sp.dma_start(rj[:, :, 0:262], win[:, 2 * j:2 * j + 2, c0:c0 + 262]).then_inc(raw_loaded[j % RING], 16)
                    sp.dma_start(rj[:, :, 288:294], win[:, 2 * j:2 * j + 2, c0 + 262:c0 + 268]).then_inc(tail_loaded[j % RING], 16)
                    if l:
                        v1 = a['rw_v1'][l - 1].rearrange("(k p) n -> p k n", p=128)
                        sp.dma_start(rj[:, :, 320:352], v1[:, 2 * j:2 * j + 2, :]).then_inc(tail_loaded[j % RING], 16)

                def stream(src, s0, bodies, kblocks):
                    slabs = kblocks // 2
                    with sp.Fori(0, bodies) as it:
                        for j in range(2 * slabs):
                            load(it * (2 * slabs) + (s0 + j), j, src, 2 * (j % slabs), it * (2 * GC) + GC * (j // slabs))
                stream(win, slab0(l, 'in'), IN_GROUPS // 2, KB)
                stream(a['w_out'][l].rearrange("(k p) n -> p k n", p=128), slab0(l, 'out'), 2, KB)
                wg = a['w_gate'][l].rearrange("(k p) n -> p k n", p=128)
                wu = a['w_up'][l].rearrange("(k p) n -> p k n", p=128)
                with sp.Fori(0, FF_GROUPS) as it:
                    for j in range(16):
                        load(it * 16 + (slab0(l, 'up') + j), j, wg if j < 8 else wu, 2 * (j % 8), it * GC)
                stream(a['w_down'][l].rearrange("(k p) n -> p k n", p=128), slab0(l, 'down'), 2, FB)

            for t in range(2):
                sp.wait_ge(S.y_rows, t + 1)
                sp.dma_start(o['y_prompt'][0, 128 * t:128 * t + 128, :], y_tok[:, t, :]).then_inc(S.y_stored, 16)
            sp.wait_ge(S.y_rows, 3)
            sp.dma_start(o['y_sample'][:, 0, :], y_tok[0:NS, 2, :]).then_inc(S.y_stored, 16)
            sp.wait_ge(S.y_stored, 48)
            sp.wait_ge(S.shift_stored, 32 * DEPTH)
            sp.wait_ge(S.rw_stored, 16 * 5 * DEPTH)
            sp.wait_ge(S.ret_stored, 16 * 4 * DEPTH)
            sp.wait_ge(S.ml_stored, 16 * 10 * DEPTH)

        @block.tensor
        def _(pe):
            def product(s, j, g, k0, last_k, bh, bl, nt, blocks=4, ready=None):
                pe.wait_ge(S.lo_ready, s + 1)
                if k0 == 0 and g is not None:
                    pe.wait_ge(S.evacuated, g - 1)
                setat = 4 * ((j // ((last_k + 1) // 2)) % 2)
                if ready is not None:
                    pe.wait_ge(S.x_ready, ready + k0 // 4 + 1)
                for k in (k0, k0 + 1):
                    for n in range(blocks):
                        w0 = wh[:, j % RING, k - k0, 128 * n:128 * n + 128]
                        w1 = wl[:, j % RING, k - k0, 128 * n:128 * n + 128]
                        out = ps[:, setat + n, 0:nt]
                        mm(out, w1, bh[:, k, 0:nt], start=(k == 0), stop=False)
                        mm(out, w0, bl[:, k, 0:nt], start=False, stop=False)
                        last = mm(out, w0, bh[:, k, 0:nt], start=False, stop=(k == last_k))
                last.then_inc(S.slab_used, 1)

            def groups(s0, g0, bodies, kblocks, bh, bl, nt, ready=None):
                slabs = kblocks // 2
                with pe.Fori(0, bodies) as it:
                    for j in range(2 * slabs):
                        product(it * (2 * slabs) + (s0 + j), j, it * 2 + (g0 + j // slabs), 2 * (j % slabs),
                                kblocks - 1, bh, bl, nt, ready=ready if j < slabs else None)

            class Behind:
                def __init__(self, l, first, plan_):
                    self.l, self.first, self.plan, self.i = l, first, plan_, 0

                def to(self, name):
                    while self.plan and self.i < self.plan[name]:
                        s = slab0(self.l, 'in') + 8 * self.first + self.i // 2
                        k, half = self.i % KB, self.i % 2
                        if not half:
                            pe.wait_ge(S.lo_ready, s + 1)
                        if k == 0:
                            pe.wait_ge(S.evacuated, group0(self.l, 'in') + self.first + self.i // KB)
                        for n in range(4):
                            w0 = wh[:, s % RING, half, 128 * n:128 * n + 128]
                            w1 = wl[:, s % RING, half, 128 * n:128 * n + 128]
                            mm(ps[:, n, 0:T], w1, xh[:, k, 0:T], start=(k == 0), stop=False)
                            mm(ps[:, n, 0:T], w0, xl[:, k, 0:T], start=False, stop=False)
                            last = mm(ps[:, n, 0:T], w0, xh[:, k, 0:T], start=False, stop=(k == KB - 1))
                        if half:
                            last.then_inc(S.slab_used, 1)
                        self.i += 1

            def to_rows(src, n, w, bank0, sem):
                for b in range(n):
                    last = tr(ps[0:w, bank0 + b // 4, 128 * (b % 4):128 * (b % 4) + 128], src(b), ident)
                last.then_inc(sem, 1)

            def norm_sums(n, nxt=None):
                pe.wait_ge(S.ln_sum, n + 1)
                mm(ps[:, 0, 0:T], ones, ln_s[:, :], start=True, stop=True).then_inc(S.ln_sum_all, 1)
                if nxt is not None:
                    pe.wait_ge(S.prm_loaded, 16 * (13 * (nxt + 1) + nxt))
                    pr = PRM_ROWS if nxt else PRM_ROWS - 4
                    tr(ps[:, 2, 0:pr], prm_tok[0:pr, :], ident[0:pr, 0:pr])
                    pe.wait_ge(S.shift_loaded, 16 * (nxt + 1))
                    for b in range(KB):
                        last = tr(ps[:, 3, 8 * b:8 * b + 8], shift_tok[:, 128 * b:128 * b + 128], ident[0:NS, 0:NS])
                    last.then_inc(S.layer_turned, 1)
                for q in range(4):
                    pe.wait_ge(S.ln_squared, 4 * n + q + 1)
                    for b in range(4 * q, 4 * q + 4):
                        last = mm(ps[:, 1, 0:T], ones, SQ[:, b, :], start=(b == 0), stop=(b == KB - 1))
                last.then_inc(S.ln_sumsq_all, 1)

            pe.wait_ge(S.tables_loaded, 16 * 6)
            pe.wait_ge(S.x_loaded, 32)
            for q in range(4):
                if q >= 2:
                    pe.wait_ge(S.x_taken, q - 1)
                for b in range(4):
                    bank = ps[:, 4 * (q % 2) + b]
                    f = 128 * (4 * q + b)
                    for t in range(2):
                        tr(bank[:, 128 * t:128 * t + 128], x_tok[:, t, f:f + 128], ident)
                    last = tr(bank[:, SEQ:T], x_tok[0:NS, 2, f:f + 128], ident[0:NS, 0:NS])
                last.then_inc(S.x_turned, 1)
            pe.wait_ge(S.prm0_loaded, 32)
            pe.wait_ge(S.x_taken, 4)
            tr(ps[:, 4, 0:32], prm0_tok[:, :], ident[0:32, 0:32]).then_inc(S.prm0_turned, 1)
            norm_sums(0, 0)

            def attention(l, ml, n, bg):
                src = pml if ml else pret
                qT = (lambda p: src[:, p, :])
                kT = (lambda p: src[:, AP_ + p, :])
                vT = (lambda h: src[:, 2 * AP_ + h, :])
                for c in range(NCH):
                    bg.to(f'turn{c}')
                    if c:
                        pe.wait_ge(S.a_tok, 2 * n + 1)
                    else:
                        pe.wait_ge(S.a_prepared, n + 1)
                    for p in range(AP_):
                        tr(ps[:, 4, 128 * p:128 * p + 128], kw[:, p, CH * c:CH * c + CH], ident)
                    for h in range(AH):
                        last = tr(ps[:, 5 + h // 4, 128 * (h % 4):128 * (h % 4) + 128],
                                  vT(h)[:, CH * c:CH * c + CH], ident)
                    last.then_inc(S.a_turned, 1)
                bg.to('score')
                pe.wait_ge(S.a_tok, 2 * n + 2)
                for c in range(NCH):
                    for h in range(AH):
                        r = slice(64 * (h % 2), 64 * (h % 2) + 64)
                        bank, hc = hb(h, 4 + 2 * c, 128)
                        last = mm(ps[:, bank, hc],
                                  kT(h // 2)[r, CH * c:CH * c + CH], qT(h // 2)[r, CH * c:CH * c + CH], start=True, stop=True)
                    last.then_inc(S.a_scored, 1)
                for c in range(NCH):
                    bg.to(f'num{c}')
                    pe.wait_ge(S.a_weighted, 2 * n + 2)
                    if c:
                        pe.wait_ge(S.a_state_kept, 2 * n + 1)
                        pe.wait_ge(S.a_y_kept, 2 * n + 1)
                    for h in range(AH):
                        r = slice(64 * (h % 2), 64 * (h % 2) + 64)
                        bank, hc = hb(h, 4, 128)
                        mm(ps[:, bank, hc], vtok[:, c, 128 * h:128 * h + 128],
                           ssb[:, c, h, :], start=True, stop=(c == 0))
                        if c:
                            mm(ps[:, bank, hc], st[r, 0, h // 2, :],
                               qs[r, h // 2, CH * c:CH * c + CH], start=False, stop=True)
                    if ml:
                        dc = slice(CH * c, CH * c + CH)
                        for h in range(AH):
                            mm(ps[0:AH, 6, dc], whole6(h), ssb[:, c, h, :], start=(h == 0), stop=(c == 0 and h == AH - 1))
                        if c:
                            pe.wait_ge(S.m_nq, l + 1)
                            for p in range(AP_):
                                mm(ps[0:AH, 6, dc], pair6(p), mnq[:, p, :], start=False, stop=(p == AP_ - 1))
                    for h in range(AH):
                        r = slice(64 * (h % 2), 64 * (h % 2) + 64)
                        last = mm(ps[r, 7, 128 * (h // 2):128 * (h // 2) + 128], ktok[:, c, 64 * h:64 * h + 64],
                                  vtok[:, c, 128 * h:128 * h + 128], start=True, stop=True)
                    last.then_inc(S.a_summed, 1)
                for p in range(AP_):
                    bg.to(f'v{p}')
                    for e in range(2):
                        pe.wait_ge(S.a_vdiag, n * AH + 2 * p + e + 1)
                        if p and not e:
                            pe.wait_ge(S.a_pair_done, n * AP_ + p)
                        if p == 0 and not e:
                            pe.wait_ge(S.a_y_kept, 2 * n + 2)
                        vd = mvd if ml else rvd
                        for b in range(2):
                            last = mm(ps[64 * e:64 * e + 64, 4 + b, 0:512], ones[:, 0:64],
                                      vd[:, 4 * b:4 * b + 4, :].rearrange("p b v -> p (b v)"), start=True, stop=True)
                        last.then_inc(S.a_vspread, 1)
                bg.to('sy')
                pe.wait_ge(S.a_pair_done, n * AP_ + AP_)
                sam = msam if ml else rsam
                for h in range(AH):
                    r = slice(64 * (h % 2), 64 * (h % 2) + 64)
                    for b in range(NS):
                        last = mm(ps[:, 4 + h % 2, 8 * (h // 2) + b:8 * (h // 2) + b + 1], sam[r, h // 2, b, :],
                                  qT(h // 2)[r, SEQ + b:SEQ + b + 1], start=True, stop=True)
                if ml:
                    pe.wait_ge(S.m_nprod, l + 1)
                    for p in range(AP_):
                        last = mm(ps[0:AH, 6, SEQ:T], pair6(p), mpd[:, p, :], start=(p == 0), stop=(p == AP_ - 1))
                last.then_inc(S.a_sample_y, 1)
                bg.to('sumsq')
                pe.wait_ge(S.a_squares, n + 1)
                pe.wait_ge(S.a_state_kept, 2 * n + 2)
                for h in range(AH):
                    last = mm(ps[0:AH, 7, 0:T], whole6(h), sq[:, h, :], start=(h == 0), stop=(h == AH - 1))
                last.then_inc(S.a_sumsq, 1)
                bg.to('spread')
                pe.wait_ge(S.a_inv, n + 1)
                for h in range(4):
                    last = mm(ps[:, 4 + h, 0:T], sel[0:AH, h, :], ln_s[0:AH, :], start=True, stop=True)
                last.then_inc(S.a_spread, 1)
                bg.to('spread1')
                pe.wait_ge(S.a_normed, n + 1)
                for h in range(4, AH):
                    last = mm(ps[:, h, 0:T], sel[0:AH, h, :], ln_s[0:AH, :], start=True, stop=True)
                last.then_inc(S.a_spread, 1)
                bg.to('end')

            for l in range(DEPTH):
                pe.wait_ge(S.layer_taken, l + 1)
                for j in range(TAIL_SLABS):
                    product(slab0(l, 'tail') + j, j, None, 2 * j, KB - 1, xh, xl, TW, blocks=3, ready=8 * l)
                pe.wait_ge(S.evacuated, group0(l, 'in'))
                groups(slab0(l, 'in'), group0(l, 'in'), 2, KB, xh, xl, TW)

                pe.wait_ge(S.evacuated, group0(l, 'in') + 4)
                pe.wait_ge(S.shift_cols, l + 1)
                to_rows(lambda b: rows9[:, b, :], KB, 1 + NS, 4, S.shift_turned)
                bg = Behind(l, 4, rw_plan)
                bg.to('in')
                pe.wait_ge(S.shift_rows, l + 1)

                pe.wait_ge(S.rw_in, l + 1)

                def four(lhs, rhs):
                    for b in range(4):
                        last = mm(ps[:, 4 + b, 0:T], lhs(slice(128 * b, 128 * b + 128)), rhs, start=True, stop=True)
                    return last
                four(lambda c: lora[0:64, 0, c], mx[0:64, 12, :]).then_inc(S.rw_wa, 1)
                bg.to('a')
                pe.wait_ge(S.rw_wa_taken, 2 * l + 1)
                four(lambda c: lora[64:128, 0, c], mx[64:128, 12, :]).then_inc(S.rw_wa, 1)
                bg.to('g')
                pe.wait_ge(S.rw_wa_taken, 2 * l + 2)
                four(lambda c: lora[:, 1, c], mx[:, 13, :]).then_inc(S.rw_g, 1)
                bg.to('v')
                pe.wait_ge(S.rw_g_taken, l + 1)
                if l:
                    four(lambda c: lora[64:96, 2, c], ptail[64:96, 2, 0:T]).then_inc(S.rw_v, 1)
                bg.to('kk')
                if l:
                    pe.wait_ge(S.rw_v_taken, l)
                pe.wait_ge(S.rw_kk_sq, l + 1)
                for b in range(4):
                    last = mm(ps[0:RW_HEADS, 4, 0:T], pair8(b), tmp[:, b, :], start=(b == 0), stop=(b == 3))
                last.then_inc(S.rw_kk_sum, 1)
                bg.to('kks')
                pe.wait_ge(S.rw_kk_inv, l + 1)
                for b in range(4):
                    last = mm(ps[:, 4 + b, 0:T], sel[:, AH + b, :], ln_s[0:RW_HEADS, :], start=True, stop=True)
                last.then_inc(S.rw_kk_spread, 1)
                bg.to('bonus')
                pe.wait_ge(S.rw_bonus_in, l + 1)
                for b in range(4):
                    last = mm(ps[:, 4 + b, 0:T], halves, tmp[:, b, :], start=True, stop=True)
                last.then_inc(S.rw_bonus_sum, 1)

                for c in range(NCH):
                    n = NCH * l + c
                    cs = slice(CH * c, CH * c + CH)
                    bg.to(f'tok{c}')
                    pe.wait_ge(S.rw_scaled, l + 1)
                    if c:
                        pe.wait_ge(S.rw_chunk_done, n)
                    for i, b0 in enumerate((8, 4, 18)):
                        for b in range(4):
                            last = tr(ps[:, 4 + i, 128 * b:128 * b + 128], mx[:, b0 + b, cs], ident)
                    last.then_inc(S.rw_turned, 1)
                    for q in range(2):
                        bg.to(f'more{c}' if q else f'pairs{c}')
                        if not q:
                            pe.wait_ge(S.rw_tok, n + 1)
                        for what, lhs0 in ((0, 18), (1, 4)):
                            if q:
                                pe.wait_ge(S.rw_pairs_taken, 4 * n + 1 + what)
                            for e in range(4):
                                h = 4 * q + e
                                r = slice(64 * (h % 2), 64 * (h % 2) + 64)
                                bank = 4 + 2 * what + e % 2
                                at_ = 256 * (e // 2)
                                mm(ps[:, bank, at_:at_ + 128], mx[r, lhs0 + h // 2, cs], mx[r, 14 + h // 2, cs],
                                   start=True, stop=True)
                                last = mm(ps[:, bank, at_ + 128:at_ + 256], mx[r, lhs0 + h // 2, cs], mx[r, h // 2, cs],
                                          start=True, stop=True)
                            last.then_inc(S.rw_pairs, 1)
                    bg.to(f'l{c}')
                    pe.wait_ge(S.rw_pairs_taken, 4 * n + 3)
                    for h in range(RW_HEADS):
                        r = slice(64 * (h % 2), 64 * (h % 2) + 64)
                        bank, hc = hb(h, 4, 128)
                        last = mm(ps[:, bank, hc], mx[r, 14 + h // 2, cs],
                                  mx[r, 18 + h // 2, cs], start=True, stop=True)
                    last.then_inc(S.rw_l, 1)
                    for lev in range(6):
                        bg.to(f'x{c}.{lev}')
                        for q in range(2):
                            m = 12 * n + 2 * lev + q
                            pe.wait_ge(S.rw_masked, m + 1)
                            for e in range(4):
                                h = 4 * q + e
                                last = mm(ps[:, 4 + q, 128 * e:128 * e + 128], lmk[:, h, :], ym[:, h, :], start=True, stop=True)
                            for e in range(4 if lev else 0):
                                last = tr(ps[:, 6 + q, 128 * e:128 * e + 128], ym[:, 4 * q + e, :], ident)
                            last.then_inc(S.rw_x, 1)
                        bg.to(f'y{c}.{lev}')
                        for q in range(2):
                            m = 12 * n + 2 * lev + q
                            pe.wait_ge(S.rw_x_kept, m + 1)
                            for e in range(4):
                                h = 4 * q + e
                                last = mm(ps[:, 6 + q, 128 * e:128 * e + 128], tm[:, h, :], xm[:, h, :],
                                          start=True, stop=True)
                            last.then_inc(S.rw_tx, 1)
                    bg.to(f'w{c}')
                    pe.wait_ge(S.rw_inverted, 2 * n + 2)
                    for h in range(RW_HEADS):
                        r = slice(64 * (h % 2), 64 * (h % 2) + 64)
                        hc = slice(64 * h, 64 * h + 64)
                        bank, oc = hb(h, 6, 64)
                        last = mm(ps[:, bank, oc], mq[:, h, 0, :], tok[:, 0, hc], start=True, stop=(c == 0))
                        if c:
                            last = mm(ps[:, bank, oc], mx[r, 14 + h // 2, cs], zst[r, h // 2, :], start=False, stop=True)
                    last.then_inc(S.rw_w, 1)
                    bg.to(f'u{c}')
                    pe.wait_ge(S.rw_w_kept, n + 1)
                    for h in range(RW_HEADS):
                        hc = slice(64 * h, 64 * h + 64)
                        last = mm(ps[:, 4, hc], ym[:, h, :], wsb[:, hc], start=True, stop=True)
                    last.then_inc(S.rw_u, 1)
                    bg.to(f'out{c}')
                    pe.wait_ge(S.rw_u_kept, n + 1)
                    for h in range(RW_HEADS):
                        r = slice(64 * (h % 2), 64 * (h % 2) + 64)
                        hc = slice(64 * h, 64 * h + 64)
                        out = ps[r, 5 + 2 * (h % 2), 128 * (h // 2):128 * (h // 2) + 128]
                        if c:
                            mm(out, zst[r, h // 2, :], mx[r, h // 2, cs], start=True, stop=False)
                        mm(out, tok[:, 0, hc], mq[:, h, 1, :], start=(c == 0), stop=False)
                        mm(out, usb[:, hc], qb[:, h, :], start=False, stop=True)
                        out = ps[r, 6, 64 * (h // 2):64 * (h // 2) + 64]
                        mm(out, tok[:, 1, hc], tok[:, 0, hc], start=True, stop=False)
                        last = mm(out, tok[:, 2, hc], usb[:, hc], start=False, stop=True)
                    last.then_inc(S.rw_y, 1)
                for i, (src, name) in enumerate(((s1t, 'sa'), (s2t, 'sv'), (s1t, 'sy'))):
                    bg.to(name)
                    pe.wait_ge(S.rw_sample_in, 3 * l + i + 1)
                    if i == 0:
                        pe.wait_ge(S.rw_chunk_done, NCH * (l + 1))
                    if i == 1:
                        pe.wait_ge(S.rw_sample_taken, l + 1)
                    for b in range(4):
                        last = mm(ps[:, 4 + b, :], halves, src[:, b, :, :].rearrange("p b v -> p (b v)"),
                                  start=True, stop=True)
                    last.then_inc(S.rw_sample_sum, 1)
                bg.to('gn')
                pe.wait_ge(S.rw_gn_in, 2 * l + 1)
                for b in range(4):
                    last = mm(ps[:, 4 + b, 0:T], halves, yt[:, b, :], start=True, stop=True)
                last.then_inc(S.rw_gn_sum, 1)
                bg.to('gnss')
                pe.wait_ge(S.rw_gn_in, 2 * l + 2)
                for b in range(4):
                    last = mm(ps[0:RW_HEADS, 4, 0:T], pair8(b), tmp[:, b, :], start=(b == 0), stop=(b == 3))
                last.then_inc(S.rw_gn_sum, 1)
                bg.to('gnsp')
                pe.wait_ge(S.rw_gn_inv, l + 1)
                for b in range(4):
                    last = mm(ps[:, 4 + b, 0:T], sel[:, AH + b, :], ln_s[0:RW_HEADS, :], start=True, stop=True)
                last.then_inc(S.rw_gn_spread, 1)
                bg.to('end')

                bg = Behind(l, 8, ret_plan)
                bg.to('swap')
                pe.wait_ge(S.rw_done, l + 1)
                pe.wait_ge(S.ret_in, l + 1)
                for b in range(4):
                    last = mm(ps[:, 4 + b, 0:T], swap, pret[:, b, 0:T], start=True, stop=True)
                last.then_inc(S.ret_swapped, 1)
                bg.to('swap1')
                pe.wait_ge(S.ret_swap_taken, l + 1)
                for b in range(4, 6):
                    last = mm(ps[:, b, 0:T], swap, pret[:, b, 0:T], start=True, stop=True)
                last.then_inc(S.ret_swapped, 1)
                attention(l, False, 2 * l, bg)
                pe.wait_ge(S.a_done, 2 * l + 1)

                pe.wait_ge(S.evacuated, group0(l, 'in') + 12)
                pe.wait_ge(S.m_rows_c, l + 1)
                for c in range(NCH):
                    tr(ps[:, 6, 8 * c:8 * c + AH], rows[:, 0, CH * c:CH * c + CH], ident[0:AH, 0:AH])
                pe.wait_ge(S.m_rows_m, l + 1)
                for h in range(AH):
                    last = mm(ps[:, h, 0:T], sel[0:AH, h, :], rows[:, 3, :], start=True, stop=True)
                last.then_inc(S.m_spread, 1)
                pe.wait_ge(S.m_exp_in, l + 1)
                pe.wait_ge(S.m_rows_e, l + 1)
                for p in range(AP_):
                    mm(ps[:, p, 0:T], sel[0:AH, AH + p, :], rows[:, 4, :], start=True, stop=True)
                    last = mm(ps[:, 3 + p, 0:T], sel[0:AH, AH + p, :], rows[:, 1, :], start=True, stop=True)
                last.then_inc(S.m_spread, 1)
                attention(l, True, 2 * l + 1, Behind(l, 0, no_plan))
                pe.wait_ge(S.a_done, 2 * l + 2)

                groups(slab0(l, 'out'), group0(l, 'out'), 2, KB, oh, ol, T)
                norm_sums(2 * l + 1, l + 1 if l + 1 < DEPTH else None)
                groups(slab0(l, 'up'), group0(l, 'up'), FF_GROUPS, KB, xh, xl, T, ready=8 * l + 4)
                pe.wait_ge(S.hidden_ready, FF_GROUPS * (l + 1))
                groups(slab0(l, 'down'), group0(l, 'down'), 2, FB, hh, hl, T)
                norm_sums(2 * l + 2)

            pe.wait_ge(S.x_ready, 8 * DEPTH + 4)
            to_rows(lambda b: R[:, b, 0:128], KB, 128, 0, S.y_turned)
            to_rows(lambda b: R[:, b, 128:256], KB, 128, 4, S.y_turned)
            pe.wait_ge(S.y_rows, 1)
            to_rows(lambda b: R[:, b, SEQ:T], KB, NS, 0, S.y_turned)

        @block.scalar
        def _(act):
            own = Own(act, S.act_steps)
            A = nc.scalar.activation

            def hi4(s0, pieces=None):
                for j in range(RING):
                    act.wait_ge(raw_loaded[j], s0 * 4 + 16)
                    if pieces:
                        act.wait_ge(tail_loaded[j], pieces)
                    if not (isinstance(s0, int) and s0 < RING):
                        act.wait_ge(S.slab_used, s0 + (j - RING + 1))
                    A(wh[:, j, :, :], raw[:, j, :, :], ACT.Copy).then_inc(S.hi_ready, 1)

            def his(s0, n):
                with act.Fori(0, n // RING) as it:
                    hi4(it * RING + s0)

            def behind(l, first, dst, d0, plan_):
                base_ = slab0(l, 'in') + 8 * first

                def one(i):
                    if i % 8 == 7:
                        act.wait_ge(S.slab_used, base_ + i + 1)
                        if first == 4 and i == 7:
                            act.wait_ge(S.shift_stored, 32 * (l + 1))
                        b = 4 * (i // 8) + d0
                        A(dst[:, b:b + 4, 0:T], ps[:, 0:4, 0:T], ACT.Copy).then_inc(S.evacuated, 1)
                    s = base_ + RING + i
                    act.wait_ge(raw_loaded[s % RING], 16 * (s // RING + 1))
                    act.wait_ge(S.slab_used, s - RING + 1)
                    A(wh[:, s % RING, :, :], raw[:, s % RING, :, :], ACT.Copy).then_inc(S.hi_ready, 1)
                return Parts(plan_, one)

            def tail_pieces(l, turn):
                return 16 * (turn + 1) if l == 0 else 32 + 64 * (l - 1) + 32 * (turn + 1)

            act.dma_start(x_tok[:, 0:2, :], a['x_prompt'][0].rearrange("(t p) d -> p t d", p=128)).then_inc(S.x_loaded, 16)
            act.dma_start(x_tok[0:NS, 2, :], a['x_sample'][:, 0, :]).then_inc(S.x_loaded, 16)
            act.dma_start(base[:, :, :].rearrange("p a b -> p (a b)"), a['c_base']).then_inc(S.tables_loaded, 16)
            act.dma_start(ident2[:, :], a['c_ident2']).then_inc(S.tables_loaded, 16)
            act.dma_start(masks[:, :, :].rearrange("p a b -> p (a b)"), a['c_masks']).then_inc(S.tables_loaded, 16)
            act.dma_start(gam[:, :], a['c_gam']).then_inc(S.tables_loaded, 16)
            act.dma_start(sel[:, :, :].rearrange("p a b -> p (a b)"), a['c_sel']).then_inc(S.tables_loaded, 16)
            act.dma_start(sums[:, :], a['c_sums']).then_inc(S.tables_loaded, 16)
            act.dma_start(prm0_tok[0:16, :], a['ln0_g'].rearrange("(b c) -> b c", c=128)).then_inc(S.prm0_loaded, 16)
            act.dma_start(prm0_tok[16:32, :], a['ln0_b'].rearrange("(b c) -> b c", c=128)).then_inc(S.prm0_loaded, 16)

            def norm_parts(n, gam_, bet_, last=False):
                for q in range(4):
                    qs_ = slice(4 * q, 4 * q + 4)
                    act.wait_ge(S.ln_centered, 4 * n + q + 1)
                    A(SQ[:, qs_, :], R[:, qs_, :], ACT.Square).then_inc(S.ln_squared, 1)
                act.wait_ge(S.ln_sumsq_all, n + 1)
                A(ln_m[:, :], ps[:, 1, 0:T], ACT.Sqrt, bias=eps[:, 0:1], scale=1.0 / D).then_inc(S.ln_std, 1)
                for q in range(4):
                    act.wait_ge(S.ln_scaled, 4 * n + q + 1)
                    for b in range(4 * q, 4 * q + 4):
                        ins = A(R[:, b, :], R[:, b, :], ACT.Identity, scale=gam_(b), bias=bet_(b))
                    if last:
                        ins.then_inc(S.x_ready, 1)
                    else:
                        own(ins)
                        A(xh[:, 4 * q:4 * q + 4, 0:T], R[:, 4 * q:4 * q + 4, :], ACT.Copy).then_inc(S.x_hi_ready, 1)

            def early_loads(l):
                for name, n in PRM:
                    if name == 'rw_v0' and l == 0:
                        continue
                    src = a[name][l - 1 if name == 'rw_v0' else l].rearrange("(b c) -> b c", c=128)
                    act.dma_start(prm_tok[PRM_AT[name]:PRM_AT[name] + n, :], src).then_inc(S.prm_loaded, 16)
                act.dma_start(shift_tok[:, :], a['state_rw_shift'][l]).then_inc(S.shift_loaded, 16)

            def layer_loads(l):
                act.wait_ge(S.x_ready, 8 * l + 4)
                act.dma_start(mlb[:, 0:1], a['ml_ib'][l].rearrange("(h a) -> h a", a=1)).then_inc(S.mlb_loaded, 16)
                act.dma_start(mlb[:, 1:2], a['ml_fb'][l].rearrange("(h a) -> h a", a=1)).then_inc(S.mlb_loaded, 16)
                act.dma_start(lora[0:64, 0, :], a['rw_w2'][l]).then_inc(S.lora_loaded, 16)
                act.dma_start(lora[64:128, 0, :], a['rw_a2'][l]).then_inc(S.lora_loaded, 16)
                act.dma_start(lora[:, 1, :], a['rw_g2'][l]).then_inc(S.lora_loaded, 16)
                if l:
                    act.dma_start(lora[64:96, 2, :], a['rw_v2'][l - 1]).then_inc(S.lora_loaded, 16)
                    act.dma_start(vmu[64:96, :], a['rw_vmu'][l - 1].rearrange("(h a) -> h a", a=1)).then_inc(S.lora_loaded, 16)

            def attention(l, ml, n, bg):
                for c in range(NCH):
                    bg.to(f'turn{c}')
                    act.wait_ge(S.a_turned, 2 * n + c + 1)
                    A(ktok[:, c, :], ps[:, 4, 0:384], ACT.Copy)
                    A(vtok[:, c, 0:512], ps[:, 5, :], ACT.Copy)
                    A(vtok[:, c, 512:768], ps[:, 6, 0:256], ACT.Copy).then_inc(S.a_tok, 1)
                for name in ('score', 'num0', 'num1') + tuple(f'v{p}' for p in range(AP_)) + ('sy', 'sumsq'):
                    bg.to(name)
                act.wait_ge(S.a_y_ready, n + 1)
                if ml:
                    A(sq[:, :, :], ay[:, :, :], ACT.Square).then_inc(S.a_squares, 1)
                    own(A(mdn[:, :], ps[0:AH, 6, 0:T], ACT.Abs))
                    act.sem_inc(S.m_absden, 1)
                    act.wait_ge(S.m_guarded, l + 1)
                    A(mdn[:, :], mdn[:, :], ACT.Square, scale=float(np.sqrt(NORM_EPS))).then_inc(S.m_eps, 1)
                    act.wait_ge(S.m_var, l + 1)
                    A(ln_s[0:AH, :], mdn[:, :], ACT.Sqrt).then_inc(S.a_std, 1)
                else:
                    A(sq[:, :, :], ay[:, :, :], ACT.Square).then_inc(S.a_squares, 1)
                    act.wait_ge(S.a_sumsq, n + 1)
                    A(ln_s[0:AH, :], ps[0:AH, 7, 0:T], ACT.Sqrt, bias=eps[0:AH, 1:2], scale=1.0 / AV).then_inc(S.a_std, 1)
                if ml:
                    A(mgate[:, 0:4, :], pml[:, 12:16, 0:T], ACT.Sigmoid)
                    A(mgate[:, 4:6, :], ptail[:, 0:2, 0:T], ACT.Sigmoid).then_inc(S.a_gate, 1)
                else:
                    A(rtmp[:, :, :], pret[:, 12:18, 0:T], ACT.Sigmoid).then_inc(S.a_gate, 1)
                bg.to('end')
                a0 = 10 if ml else 4
                act.wait_ge(S.a_out, n + 1)
                A(oh[:, a0:a0 + AH, :], ay[:, :, :], ACT.Copy).then_inc(S.a_out_hi, 1)

            early_loads(0)
            hi4(0, tail_pieces(0, 0))
            norm_parts(0, lambda b: prm0[:, b:b + 1], lambda b: prm0[:, 16 + b:17 + b])
            for l in range(DEPTH):
                layer_loads(l)
                hi4(slab0(l, 'tail') + 4, tail_pieces(l, 1))
                his(slab0(l, 'in'), 36)
                act.wait_ge(S.shift_turned, l + 1)
                A(shift_out[:, :].rearrange("p (a b) -> p a b", a=4), ps[0:1 + NS, 4:8, :], ACT.Copy).then_inc(S.shift_rows, 1)
                act.wait_ge(S.shift_rows, l + 1)
                act.dma_start(o['p_shift'][l], shift_out[0:1, :]).then_inc(S.shift_stored, 16)
                act.dma_start(o['s_shift'][l], shift_out[1:1 + NS, :]).then_inc(S.shift_stored, 16)

                bg = behind(l, 4, pret, 2, rw_plan)
                bg.to('in')
                act.wait_ge(S.rw_mix, l + 1)
                A(mx[0:64, 12, :], mx[0:64, 12, :], ACT.Tanh)
                A(mx[:, 13, :], mx[:, 13, :], ACT.Sigmoid).then_inc(S.rw_in, 1)
                act.wait_ge(S.rw_wa, 2 * l + 1)
                for b in range(4):
                    last = A(lw[:, b, :], ps[:, 4 + b, 0:T], ACT.Sigmoid, bias=col(l, 'rw_w0', b))
                last.then_inc(S.rw_wa_taken, 1)
                bg.to('a')
                act.wait_ge(S.rw_wa, 2 * l + 2)
                for b in range(4):
                    last = A(mx[:, 18 + b, :], ps[:, 4 + b, 0:T], ACT.Sigmoid, bias=col(l, 'rw_a0', b))
                last.then_inc(S.rw_wa_taken, 1)
                bg.to('g')
                act.wait_ge(S.rw_g, l + 1)
                A(gate[:, :, :], ps[:, 4:8, 0:T], ACT.Copy).then_inc(S.rw_g_taken, 1)
                if l:
                    bg.to('v')
                    act.wait_ge(S.rw_v, l)
                    for b in range(4):
                        last = A(tmp[:, b, :], ps[:, 4 + b, 0:T], ACT.Sigmoid, bias=col(l, 'rw_v0', b))
                    last.then_inc(S.rw_v_taken, 1)
                bg.to('kk')
                act.wait_ge(S.rw_kk_raw, l + 1)
                if l:
                    act.wait_ge(S.rw_v_used, l)
                A(tmp[:, :, :], mx[:, 14:18, :], ACT.Square).then_inc(S.rw_kk_sq, 1)
                bg.to('kks')
                act.wait_ge(S.rw_kk_ss, l + 1)
                A(ln_s[0:RW_HEADS, :], ln_m[0:RW_HEADS, :], ACT.Sqrt).then_inc(S.rw_kk_norm, 1)
                bg.to('bonus')
                act.wait_ge(S.rw_cum, l + 1)
                for b in range(4):
                    for c in range(NCH):
                        cs = slice(CH * c, CH * c + CH)
                        A(ep[:, b, cs], lw[:, b, cs], ACT.Exp, bias=namid[:, b, c:c + 1])
                        A(em[:, b, cs], lw[:, b, cs], ACT.Exp, bias=amid[:, b, c:c + 1], scale=-1.0)
                A(wsam[:, :, :], lw[:, :, SEQ:T], ACT.Exp)
                A(eamid[:, :, :], amid[:, :, :], ACT.Exp)
                A(enam[:, :, :], namid[:, :, :], ACT.Exp).then_inc(S.rw_exps, 1)
                for c in range(NCH):
                    n = NCH * l + c
                    bg.to(f'tok{c}')
                    act.wait_ge(S.rw_turned, n + 1)
                    A(tok[:, :, :], ps[:, 4:7, :], ACT.Copy).then_inc(S.rw_tok, 1)
                    for name in ('pairs', 'more', 'l'):
                        bg.to(f'{name}{c}')
                    for lev in range(6):
                        bg.to(f'x{c}.{lev}')
                        for q in range(2):
                            m = 12 * n + 2 * lev + q
                            hs = slice(4 * q, 4 * q + 4)
                            act.wait_ge(S.rw_x, m + 1)
                            last = A(xm[:, hs, :], ps[:, 4 + q, :].rearrange("p (h i) -> p h i", i=CH), ACT.Copy)
                            if lev:
                                last = A(tm[:, hs, :], ps[:, 6 + q, :].rearrange("p (h i) -> p h i", i=CH), ACT.Copy)
                            last.then_inc(S.rw_x_kept, 1)
                        bg.to(f'y{c}.{lev}')
                    bg.to(f'w{c}')
                    act.wait_ge(S.rw_w, n + 1)
                    A(pairs(wsb[:, :].rearrange("p (h v) -> p h v", v=64)), halves_of(6, 64, RW_HEADS), ACT.Copy).then_inc(S.rw_w_kept, 1)
                    bg.to(f'u{c}')
                    act.wait_ge(S.rw_u, n + 1)
                    A(usb[:, :], ps[:, 4, :], ACT.Copy, scale=-1.0).then_inc(S.rw_u_kept, 1)
                    bg.to(f'out{c}')
                    if c == 0:
                        si = a['state_rw_wkv'][l].rearrange("b (p e) k v -> p (e k) b v", e=2)
                        so = o['s_wkv'][l].rearrange("b (p e) k v -> p (e k) b v", e=2)
                        for p in range(4):
                            act.dma_start(srw[:, p, :, :], si[p]).then_inc(S.rw_sample_loaded, 16)
                bg.to('sa')
                act.wait_ge(S.rw_chunk_done, NCH * (l + 1))
                act.dma_start(o['p_wkv'][l, 0].rearrange("(p e) k v -> (e k) p v", e=2), zst[:, :, :]).then_inc(S.rw_stored, 16)
                for name in ('sv', 'sy'):
                    bg.to(name)
                act.wait_ge(S.rw_sample_new, l + 1)
                for p in range(4):
                    act.dma_start(so[p], srw[:, p, :, :]).then_inc(S.rw_stored, 16)
                for name in ('gn', 'gnss'):
                    bg.to(name)
                act.wait_ge(S.rw_gn_c, l + 1)
                A(tmp[:, :, :], yt[:, :, :], ACT.Square).then_inc(S.rw_gn_in, 1)
                act.wait_ge(S.rw_gn_sum, 2 * l + 2)
                A(ln_s[0:RW_HEADS, :], ps[0:RW_HEADS, 4, 0:T], ACT.Sqrt, bias=eps[0:RW_HEADS, 2:3],
                  scale=1.0 / RW_HD).then_inc(S.rw_gn_std, 1)
                bg.to('end')
                act.wait_ge(S.rw_out, l + 1)
                A(oh[:, 0:4, :], yt[:, :, :], ACT.Copy).then_inc(S.rw_out_hi, 1)

                act.wait_ge(S.rw_done, l + 1)
                act.wait_ge(S.rw_stored, 80 * (l + 1))
                act.dma_start(rdec[:, :, :].rearrange("p a b -> p (a b)"), a['c_ret']).then_inc(S.rdec_loaded, 16)
                act.dma_start(rrot[:, :, :].rearrange("p a b -> p (a b)"), a['c_rot']).then_inc(S.rdec_loaded, 16)
                si = a['state_ret'][l].rearrange("b (p e) k v -> p (e k) b v", e=2)
                so = o['s_ret'][l].rearrange("b (p e) k v -> p (e k) b v", e=2)
                for p in range(AP_):
                    act.dma_start(rsam[:, p, :, :], si[p]).then_inc(S.a_sample_loaded, 16)
                bg = behind(l, 8, pml, 0, ret_plan)
                for name in ('swap', 'swap1', 'turn0'):
                    bg.to(name)
                attention(l, False, 2 * l, bg)
                act.dma_start(o['p_ret'][l, 0].rearrange("(p e) k v -> (e k) p v", e=2), st[:, 1, :, :]).then_inc(S.ret_stored, 16)
                for p in range(AP_):
                    act.dma_start(so[p], rsam[:, p, :, :]).then_inc(S.ret_stored, 16)

                act.wait_ge(S.a_done, 2 * l + 1)
                si = a['state_ml_c'][l].rearrange("b (p e) k v -> p (e k) b v", e=2)
                so = o['s_mlc'][l].rearrange("b (p e) k v -> p (e k) b v", e=2)
                ni = a['state_ml_n'][l].rearrange("b (p e) k -> p (e k) b", e=2)
                no = o['s_mln'][l].rearrange("b (p e) k -> p (e k) b", e=2)
                for p in range(AP_):
                    act.dma_start(msam[:, p, :, :], si[p]).then_inc(S.a_sample_loaded, 16)
                    act.dma_start(msn[:, p, :], ni[p], allow_slow_non_contiguous=True).then_inc(S.m_n_loaded, 16)
                act.dma_start(rows[:, 4, SEQ:T], a['state_ml_m'][l].rearrange("b h -> h b"), allow_slow_non_contiguous=True).then_inc(S.m_m_loaded, 16)
                act.wait_ge(S.m_gates_in, l + 1)
                own(A(rows[:, 0, :], rows[:, 0, :], ACT.Tanh, bias=mlb2[:, 0:1], scale=1.0 / CAP))
                own(A(rows[:, 1, :], rows[:, 1, :], ACT.Tanh, bias=mlb2[:, 1:2], scale=1.0 / CAP))
                own(A(rows[:, 1, :], rows[:, 1, :], ACT.Sigmoid, scale=CAP))
                A(rows[:, 1, :], rows[:, 1, :], ACT.Ln).then_inc(S.m_logf, 1)
                act.wait_ge(S.m_rows_x, l + 1)
                A(rows[:, 1, :], rows[:, 1, :], ACT.Exp)
                A(rows[:, 4, :], rows[:, 4, :], ACT.Exp)
                A(men[:, :], rows[:, 2, :], ACT.Exp, scale=-1.0).then_inc(S.m_rows_e, 1)
                act.wait_ge(S.m_exp_in, l + 1)
                for h in range(AH):
                    for c in range(NCH):
                        last = A(mexp[:, h, CH * c:CH * c + CH], mexp[:, h, CH * c:CH * c + CH], ACT.Exp,
                                 bias=mct[:, c, h:h + 1])
                last.then_inc(S.m_exp, 1)
                attention(l, True, 2 * l + 1, Parts(no_plan, None))
                act.dma_start(o['p_mlc'][l, 0].rearrange("(p e) k v -> (e k) p v", e=2), st[:, 1, :, :]).then_inc(S.ml_stored, 16)
                act.dma_start(o['p_mln'][l, 0].rearrange("(p e) k -> (e k) p", e=2), mnc[:, 1, :], allow_slow_non_contiguous=True).then_inc(S.ml_stored, 16)
                act.dma_start(o['p_mlm'][l, 0].rearrange("(h a) -> h a", a=1), mfin[:, NS:NS + 1]).then_inc(S.ml_stored, 16)
                act.dma_start(o['s_mlm'][l].rearrange("b h -> h b"), mfin[:, 0:NS], allow_slow_non_contiguous=True).then_inc(S.ml_stored, 16)
                for p in range(AP_):
                    act.dma_start(so[p], msam[:, p, :, :]).then_inc(S.ml_stored, 16)
                    act.dma_start(no[p], msn[:, p, :], allow_slow_non_contiguous=True).then_inc(S.ml_stored, 16)

                if l + 1 < DEPTH:
                    act.wait_ge(S.a_done, 2 * l + 2)
                    act.wait_ge(S.ml_stored, 160 * (l + 1))
                    early_loads(l + 1)
                his(slab0(l, 'out') + 4, 32)
                norm_parts(2 * l + 1, lambda b: col(l, 'ln1_g', b), lambda b: col(l, 'ln1_b', b))
                with act.Fori(0, FF_GROUPS) as it:
                    s = it * 16 + (slab0(l, 'up') + 4)
                    hi4(s)
                    hi4(s + 4)
                    act.wait_ge(S.slab_used, s + 4)
                    act.wait_ge(S.gated, it + (l * FF_GROUPS + 1))
                    A(sg[:, :, :], ps[:, 0:4, 0:T], ACT.Sigmoid).then_inc(S.gate_sig, 1)
                    hi4(s + 8)
                    hi4(s + 12)
                his(slab0(l, 'down') + 4, 4 * DOWN_SLABS - RING)
                if l + 1 < DEPTH:
                    hi4(slab0(l + 1, 'tail'), tail_pieces(l + 1, 0))
                norm_parts(2 * l + 2, lambda b: col(l, 'ln2_g', b), lambda b: col(l, 'ln2_b', b), last=l + 1 == DEPTH)
            for t in range(2):
                act.wait_ge(S.y_turned, t + 1)
                A(y_tok[:, t, :].rearrange("p (a b) -> p a b", a=4), ps[:, 4 * t:4 * t + 4, :], ACT.Copy).then_inc(S.y_rows, 1)
            act.wait_ge(S.y_turned, 3)
            A(y_tok[0:NS, 2, :].rearrange("p (a b) -> p a b", a=4), ps[0:NS, 0:4, :], ACT.Copy).then_inc(S.y_rows, 1)

        @block.vector
        def _(dve):
            v = nc.vector
            own = Own(dve, S.dve_steps)
            TT, TS, STT = v.tensor_tensor, v.tensor_scalar, v.scalar_tensor_tensor
            own(v.memset(eps[:, 0:1], LN_EPS))
            own(v.memset(eps[:, 1:2], NORM_EPS))
            own(v.memset(eps[:, 2:3], GN_EPS))
            dve.sem_inc(S.evacuated, 1)
            dve.sem_inc(S.gated, 1)
            v.memset(raw[:, :, :, :], 0.0).then_inc(S.raw_cleared, 1)

            def lo4(s0):
                for j in range(RING):
                    dve.wait_ge(S.hi_ready, s0 + (j + 1))
                    TT(wl[:, j, :, :], raw[:, j, :, :], wh[:, j, :, :].bitcast(F32), ALU.subtract).then_inc(S.lo_ready, 1)

            def evacuate(used, what):
                dve.wait_ge(S.slab_used, used)
                what().then_inc(S.evacuated, 1)

            def in_groups(l, first, dst, d0):
                with dve.Fori(0, 2) as it:
                    s = it * 16 + (slab0(l, 'in') + 8 * first)
                    lo4(s + 4)
                    lo4(s + 8)
                    evacuate(s + 8, lambda: v.tensor_copy(dst[:, ds(it * 8 + d0, 4), :], ps[:, 0:4, 0:TW]))
                    lo4(s + 12)
                    lo4(s + 16)
                    evacuate(s + 16, lambda: v.tensor_copy(dst[:, ds(it * 8 + (d0 + 4), 4), :], ps[:, 4:8, 0:TW]))

            def behind(l, first, plan_):
                def one(i):
                    s = slab0(l, 'in') + 8 * first + RING + i
                    dve.wait_ge(S.hi_ready, s + 1)
                    TT(wl[:, s % RING, :, :], raw[:, s % RING, :, :], wh[:, s % RING, :, :].bitcast(F32),
                       ALU.subtract).then_inc(S.lo_ready, 1)
                return Parts(plan_, one)

            def residual(blk, set_):
                STT(R[:, ds(blk, 4), :], xh[:, ds(blk, 4), 0:T].bitcast(F32), ALPHA, ps[:, set_:set_ + 4, 0:T],
                    ALU.mult, ALU.add).then_inc(S.resid_part, 1)
                return lambda: STT(R[:, ds(blk, 4), :], xl[:, ds(blk, 4), 0:T].bitcast(F32), ALPHA, R[:, ds(blk, 4), :],
                                   ALU.mult, ALU.add)

            def residual_group(used, blk, set_, count, g):
                dve.wait_ge(S.slab_used, used)
                second = residual(blk, set_)
                dve.wait_ge(S.resid_part, count + 1)
                second().then_inc(S.evacuated, 1)
                dve.wait_ge(S.evacuated, g)
                TT(gu[:, :, :], gu[:, :, :], R[:, ds(blk, 4), :], ALU.add).then_inc(S.resid_sum, 1)
                dve.wait_ge(S.resid_sum, count + 1)

            def norm(n, nxt=None, last=False):
                v.tensor_reduce(ln_s[:, :], gu[:, :, :].rearrange("p b t -> p t b"), AX.X, ALU.add).then_inc(S.ln_sum, 1)
                dve.wait_ge(S.ln_sum_all, n + 1)
                own(TS(ln_m[:, :], ps[:, 0, 0:T], 1.0 / D, None, ALU.mult))
                for q in range(4):
                    Rq = R[:, 4 * q:4 * q + 4, :]
                    TT(Rq, Rq, each(ln_m[:, :], 4), ALU.subtract).then_inc(S.ln_centered, 1)
                if nxt is not None:
                    dve.wait_ge(S.layer_turned, nxt + 1)
                    npr = PRM_ROWS if nxt else PRM_ROWS - 4
                    own(v.tensor_copy(prm2[:, nxt % 2, 0:npr], ps[:, 2, 0:npr]))
                    sh = ps[:, 3, 0:128].rearrange("p (b s) -> p b s", s=NS)
                    own(v.tensor_copy(xh[:, :, T:TW], sh))
                    TT(xl[:, :, T:TW], sh, xh[:, :, T:TW].bitcast(F32), ALU.subtract).then_inc(S.layer_taken, 1)
                dve.wait_ge(S.ln_std, n + 1)
                own(v.reciprocal(ln_m[:, :], ln_m[:, :]))
                dve.wait_ge(S.ln_centered, 4 * n + 4)
                for q in range(4):
                    Rq = R[:, 4 * q:4 * q + 4, :]
                    TT(Rq, Rq, each(ln_m[:, :], 4), ALU.mult).then_inc(S.ln_scaled, 1)
                for q in range(0 if last else 4):
                    qs_ = slice(4 * q, 4 * q + 4)
                    dve.wait_ge(S.x_hi_ready, 4 * n + q + 1)
                    TT(xl[:, qs_, 0:T], R[:, qs_, :], xh[:, qs_, 0:T].bitcast(F32), ALU.subtract).then_inc(S.x_ready, 1)

            def attention(l, ml, n, bg):
                def then(ins):
                    own(ins)
                    bg.step()
                src = pml if ml else pret
                bg.to('turn0')
                bg.to('turn1')
                bg.to('score')
                for c in range(NCH):
                    dve.wait_ge(S.a_scored, 2 * n + c + 1)
                    if ml:
                        dve.wait_ge(S.m_exp, l + 1)
                    w = mexp[:, :, CH * c:CH * c + CH] if ml else rdec[:, 0:AH, :]
                    TT(pairs(ssb[:, c, :, :]), halves_of(4 + 2 * c, CH, AH), pairs(w), ALU.mult).then_inc(S.a_weighted, 1)
                for c in range(NCH):
                    bg.to(f'num{c}')
                    dve.wait_ge(S.a_summed, 2 * n + c + 1)
                    if c == 0:
                        then(v.tensor_copy(st[:, 0, :, :], ps[:, 7, 0:384].rearrange("p (a b) -> p a b", a=AP_)))
                    else:
                        for p in range(AP_):
                            sc = mdc[:, p:p + 1] if ml else gam[:, AP_ + p:AP_ + p + 1]
                            then(STT(st[:, 1, p, :], st[:, 0, p, :], sc, ps[:, 7, 128 * p:128 * p + 128], ALU.mult, ALU.add))
                    dve.sem_inc(S.a_state_kept, 1)
                    y = v.tensor_copy(pairs(ay[:, :, CH * c:CH * c + CH]), halves_of(4, CH, AH))
                    y.then_inc(S.a_y_kept, 1)
                dve.wait_ge(S.a_y_kept, 2 * n + 2)
                dve.wait_ge(S.a_sample_loaded, 48 * (n + 1))
                sam, vd = (msam, mvd) if ml else (rsam, rvd)
                kv = ssb[:, :, :, :].rearrange("p c h i -> p (c h i)")[:, 0:NS * 128].rearrange("p (b v) -> p b v", v=128)
                for p in range(AP_):
                    for e in range(2):
                        h = 2 * p + e
                        if h:
                            dve.wait_ge(S.a_vspread, n * AH + h)
                        TT(vd[:, :, :], over(src[:, 2 * AP_ + h, SEQ:T], 128), each(ident, NS), ALU.mult).then_inc(S.a_vdiag, 1)
                    bg.to(f'v{p}')
                    dve.wait_ge(S.a_vspread, n * AH + 2 * p + 2)
                    k = kw[:, p, SEQ:T] if ml else src[:, AP_ + p, SEQ:T]
                    then(TT(kv, ps[:, 4:6, :].rearrange("p a (b v) -> p (a b) v", v=128), over(k, 128), ALU.mult))
                    if ml:
                        then(TT(sam[:, p, :, :], sam[:, p, :, :], over(msk[:, p, :], 128), ALU.mult))
                        TT(sam[:, p, :, :], sam[:, p, :, :], kv, ALU.add).then_inc(S.a_pair_done, 1)
                    else:
                        STT(sam[:, p, :, :], sam[:, p, :, :], gam[:, p:p + 1], kv, ALU.mult, ALU.add).then_inc(S.a_pair_done, 1)
                    dve.wait_ge(S.a_pair_done, n * AP_ + p + 1)
                if ml:
                    dve.wait_ge(S.m_n_loaded, 48 * (l + 1))
                    then(TT(msn[:, :, :], msn[:, :, :], msk[:, :, :], ALU.mult))
                    then(TT(msn[:, :, :], msn[:, :, :], kw[:, :, SEQ:T], ALU.add))
                    TT(mpd[:, :, :], msn[:, :, :], src[:, 0:AP_, SEQ:T], ALU.mult).then_inc(S.m_nprod, 1)
                bg.to('sy')
                dve.wait_ge(S.a_sample_y, n + 1)
                y = v.tensor_copy(pairs(ay[:, :, SEQ:T]), halves_of(4, NS, AH))
                y.then_inc(S.a_y_ready, 1)
                if ml:
                    dve.wait_ge(S.m_absden, l + 1)
                    TT(mdn[:, :], mdn[:, :], men[:, :], ALU.max).then_inc(S.m_guarded, 1)
                    dve.wait_ge(S.m_eps, l + 1)
                    dve.wait_ge(S.a_sumsq, n + 1)
                    then(STT(mdn[:, :], ps[0:AH, 7, 0:T], 1.0 / AV, mdn[:, :], ALU.mult, ALU.add))
                    TS(mdn[:, :], mdn[:, :], 1e-36, None, ALU.max).then_inc(S.m_var, 1)
                bg.to('sumsq')
                dve.wait_ge(S.a_std, n + 1)
                v.reciprocal(ln_s[0:AH, :], ln_s[0:AH, :]).then_inc(S.a_inv, 1)
                bg.to('spread')
                dve.wait_ge(S.a_spread, 2 * n + 1)
                TT(ay[:, 0:4, :], ay[:, 0:4, :], ps[:, 4:8, 0:T], ALU.mult).then_inc(S.a_normed, 1)
                bg.to('spread1')
                dve.wait_ge(S.a_spread, 2 * n + 2)
                then(TT(ay[:, 4:6, :], ay[:, 4:6, :], ps[:, 4:6, 0:T], ALU.mult))
                dve.wait_ge(S.a_normed, n + 1)
                bg.to('end')
                dve.wait_ge(S.a_gate, n + 1)
                if ml:
                    then(TT(ay[:, :, :], ay[:, :, :], over(cols(l, 'ml_norm', AH), T), ALU.mult))
                    TT(ay[:, :, :], ay[:, :, :], mgate[:, :, :], ALU.mult).then_inc(S.a_out, 1)
                else:
                    then(TT(ay[:, :, :], ay[:, :, :], rtmp[:, :, :], ALU.mult))
                    TT(ay[:, :, :], ay[:, :, :], pret[:, 12:18, 0:T], ALU.mult).then_inc(S.a_out, 1)
                a0 = 10 if ml else 4
                dve.wait_ge(S.a_out_hi, n + 1)
                TT(ol[:, a0:a0 + AH, :], ay[:, :, :], oh[:, a0:a0 + AH, :].bitcast(F32), ALU.subtract).then_inc(S.a_done, 1)

            for q in range(4):
                dve.wait_ge(S.x_turned, q + 1)
                v.tensor_copy(R[:, 4 * q:4 * q + 4, :], ps[:, 4 * (q % 2):4 * (q % 2) + 4, 0:T]).then_inc(S.x_taken, 1)
            dve.wait_ge(S.prm0_turned, 1)
            own(v.tensor_copy(prm0[:, :], ps[:, 4, 0:32]))
            dve.wait_ge(S.x_taken, 4)
            own(TT(gu[:, :, :], R[:, 0:4, :], R[:, 4:8, :], ALU.add))
            own(TT(gu[:, :, :], gu[:, :, :], R[:, 8:12, :], ALU.add))
            own(TT(gu[:, :, :], gu[:, :, :], R[:, 12:16, :], ALU.add))
            lo4(0)
            norm(0, 0)

            for l in range(DEPTH):
                dve.wait_ge(S.x_ready, 8 * l + 4)
                TT(rows9[:, :, :], xh[:, :, SEQ - 1:T].bitcast(F32), xl[:, :, SEQ - 1:T].bitcast(F32), ALU.add).then_inc(S.shift_cols, 1)
                dve.wait_ge(S.layer_taken, l + 1)
                own(TS(ka1[:, :], cols(l, 'rw_ka', 4), -1.0, 1.0, ALU.mult, ALU.add))
                lo4(slab0(l, 'tail') + 4)
                lo4(slab0(l, 'in'))
                evacuate(slab0(l, 'in'), lambda: v.tensor_copy(ptail[:, :, :], ps[:, 0:3, 0:TW]))
                in_groups(l, 0, praw, 0)

                dve.wait_ge(S.evacuated, group0(l, 'in') + 4)
                bg = behind(l, 4, rw_plan)
                then = (lambda ins: (own(ins), bg.step()))
                dve.wait_ge(S.shift_turned, l + 1)
                then(v.tensor_copy(pret[:, 0:2, :], praw[:, 14:16, :]))
                then(TT(mx[:, 0:RW_PB, 1:SEQ], praw[:, 0:RW_PB, 0:SEQ - 1], praw[:, 0:RW_PB, 1:SEQ], ALU.subtract))
                then(TS(mx[:, 0:RW_PB, 0:1], praw[:, 0:RW_PB, 0:1], -1.0, None, ALU.mult))
                then(TT(mx[:, 0:RW_PB, SEQ:T], praw[:, 0:RW_PB, T:TW], praw[:, 0:RW_PB, SEQ:T], ALU.subtract))
                then(TT(mx[:, 0:RW_PB, :], mx[:, 0:RW_PB, :], over(cols(l, 'rw_mu', RW_PB), T), ALU.mult))
                dve.wait_ge(S.lora_loaded, 48 if l == 0 else 48 + 80 * l)
                if l:
                    g = slice(64, 96)
                    then(TT(tmp[g, 0, 1:SEQ], ptail[g, 2, 0:SEQ - 1], ptail[g, 2, 1:SEQ], ALU.subtract))
                    then(TS(tmp[g, 0, 0:1], ptail[g, 2, 0:1], -1.0, None, ALU.mult))
                    then(TT(tmp[g, 0, SEQ:T], ptail[g, 2, T:TW], ptail[g, 2, SEQ:T], ALU.subtract))
                    then(STT(ptail[g, 2, 0:T], tmp[g, 0, :], vmu[g, :], ptail[g, 2, 0:T], ALU.mult, ALU.add))
                TT(mx[:, 0:RW_PB, :], mx[:, 0:RW_PB, :], praw[:, 0:RW_PB, 0:T], ALU.add).then_inc(S.rw_mix, 1)
                for name in ('in', 'a', 'g'):
                    bg.to(name)
                dve.wait_ge(S.rw_wa_taken, 2 * l + 2)
                if l == 0:
                    then(v.tensor_copy(vfirst[:, :, :], mx[:, 8:12, :]))
                else:
                    bg.to('v')
                    dve.wait_ge(S.rw_v_taken, l)
                    then(TT(ep[:, :, :], vfirst[:, :, :], mx[:, 8:12, :], ALU.subtract))
                    TT(ep[:, :, :], ep[:, :, :], tmp[:, :, :], ALU.mult).then_inc(S.rw_v_used, 1)
                    dve.wait_ge(S.rw_v_used, l)
                    then(TT(mx[:, 8:12, :], mx[:, 8:12, :], ep[:, :, :], ALU.add))
                TT(mx[:, 14:18, :], mx[:, 4:8, :], over(cols(l, 'rw_kk', 4), T), ALU.mult).then_inc(S.rw_kk_raw, 1)
                then(TS(lw[:, :, :], lw[:, :, :], -float(np.exp(-0.5)), None, ALU.mult))
                for b in range(4):
                    for c in range(NCH):
                        cs = slice(CH * c, CH * c + CH)
                        then(v.tensor_tensor_scan(lw[:, b, cs], ones, lw[:, b, cs], 0.0, ALU.mult, ALU.add))
                mid = lw[:, :, 0:SEQ].rearrange("p b (c i) -> p b c i", i=CH)[:, :, :, CH // 2 - 1]
                then(v.tensor_copy(amid[:, :, :], mid))
                TS(namid[:, :, :], mid, -1.0, None, ALU.mult).then_inc(S.rw_cum, 1)
                bg.to('kk')
                dve.wait_ge(S.rw_kk_sum, l + 1)
                dve.wait_ge(S.rw_kk_sq, l + 1)
                TS(ln_m[0:RW_HEADS, :], ps[0:RW_HEADS, 4, 0:T], 1e-24, None, ALU.max).then_inc(S.rw_kk_ss, 1)
                dve.wait_ge(S.rw_kk_norm, l + 1)
                v.reciprocal(ln_s[0:RW_HEADS, :], ln_s[0:RW_HEADS, :]).then_inc(S.rw_kk_inv, 1)
                dve.wait_ge(S.rw_kk_raw, l + 1)
                bg.to('kks')
                dve.wait_ge(S.rw_kk_spread, l + 1)
                then(TT(mx[:, 14:18, :], mx[:, 14:18, :], ps[:, 4:8, 0:T], ALU.mult))
                then(TT(tmp[:, :, :], mx[:, 18:22, :], over(cols(l, 'rw_ka', 4), T), ALU.mult))
                then(TT(tmp[:, :, :], tmp[:, :, :], over(ka1[:, :], T), ALU.add))
                then(TT(mx[:, 4:8, :], mx[:, 4:8, :], tmp[:, :, :], ALU.mult))
                then(TT(tmp[:, :, :], mx[:, 0:4, :], mx[:, 4:8, :], ALU.mult))
                TT(tmp[:, :, :], tmp[:, :, :], over(cols(l, 'rw_rk', 4), T), ALU.mult).then_inc(S.rw_bonus_in, 1)
                then(TT(mx[:, 18:22, :], mx[:, 18:22, :], mx[:, 14:18, :], ALU.mult))
                bg.to('bonus')
                dve.wait_ge(S.rw_bonus_sum, l + 1)
                then(TT(bonus[:, :, :], ps[:, 4:8, 0:T], mx[:, 8:12, :], ALU.mult))
                dve.wait_ge(S.rw_exps, l + 1)
                then(TT(mx[:, 4:8, 0:SEQ], mx[:, 4:8, 0:SEQ], em[:, :, 0:SEQ], ALU.mult))
                then(TT(mx[:, 18:22, 0:SEQ], mx[:, 18:22, 0:SEQ], em[:, :, 0:SEQ], ALU.mult))
                then(TT(mx[:, 0:4, 0:SEQ], mx[:, 0:4, 0:SEQ], ep[:, :, 0:SEQ], ALU.mult))
                kkv = mx[:, 14:18, 0:SEQ].rearrange("p b (c i) -> p b c i", i=CH)
                epv = ep[:, :, 0:SEQ].rearrange("p b (c i) -> p b c i", i=CH)
                then(TT(kkv[:, :, :, 1:CH], kkv[:, :, :, 1:CH], epv[:, :, :, 0:CH - 1], ALU.mult))
                then(TT(kkv[:, :, :, 0], kkv[:, :, :, 0], enam[:, :, :], ALU.mult))
                v.tensor_copy(eend[:, :, :], epv[:, :, :, CH - 1]).then_inc(S.rw_scaled, 1)
                dve.wait_ge(S.rw_scaled, l + 1)

                for c in range(NCH):
                    n = NCH * l + c
                    bg.to(f'tok{c}')
                    for q in range(2):
                        bg.to(f'more{c}' if q else f'pairs{c}')
                        hs = slice(4 * q, 4 * q + 4)
                        dve.wait_ge(S.rw_pairs, 4 * n + 2 * q + 1)
                        pv_ = halves_of(4, 2 * CH, 4)
                        then(TT(pairs(ym[:, hs, :]), pv_[:, :, :, 0:CH], each2(masks[:, 2, :], 2), ALU.mult))
                        TT(pairs(qb[:, hs, :]), pv_[:, :, :, CH:2 * CH], each2(masks[:, 3, :], 2), ALU.mult).then_inc(S.rw_pairs_taken, 1)
                        then(STT(ym[:, hs, :], ym[:, hs, :], -1.0, each(ident, 4), ALU.mult, ALU.add))
                        dve.wait_ge(S.rw_pairs, 4 * n + 2 * q + 2)
                        TT(pairs(mq[:, hs, :, :].rearrange("p h a i -> p h (a i)")), halves_of(6, 2 * CH, 4),
                           each2(masks[:, 0:2, :].rearrange("p a i -> p (a i)"), 2), ALU.mult).then_inc(S.rw_pairs_taken, 1)
                    bg.to(f'l{c}')
                    dve.wait_ge(S.rw_l, n + 1)
                    then(v.tensor_copy(pairs(lm[:, :, :]), halves_of(4, CH, RW_HEADS)))
                    then(TT(tm[:, :, :], lm[:, :, :], each(masks[:, 5, :], RW_HEADS), ALU.mult))
                    then(STT(tm[:, :, :], tm[:, :, :], -1.0, each(ident, RW_HEADS), ALU.mult, ALU.add))
                    for q in range(2):
                        hs = slice(4 * q, 4 * q + 4)
                        TT(lmk[:, hs, :], lm[:, hs, :], each(masks[:, 6, :], 4), ALU.mult).then_inc(S.rw_masked, 1)
                    for lev in range(6):
                        bg.to(f'x{c}.{lev}')
                        for q in range(2 if lev < 5 else 0):
                            hs = slice(4 * q, 4 * q + 4)
                            dve.wait_ge(S.rw_x, 12 * n + 2 * lev + q + 1)
                            TT(lmk[:, hs, :], lm[:, hs, :], each(masks[:, 7 + lev, :], 4), ALU.mult)
                        bg.to(f'y{c}.{lev}')
                        for q in range(2):
                            m = 12 * n + 2 * lev + q
                            hs = slice(4 * q, 4 * q + 4)
                            dve.wait_ge(S.rw_tx, m + 1)
                            yx = ps[:, 6 + q, :].rearrange("p (h i) -> p h i", i=CH)
                            TT(ym[:, hs, :], ym[:, hs, :], yx, ALU.subtract).then_inc(S.rw_masked if lev < 5 else S.rw_inverted, 1)
                    for name in ('w', 'u', 'out'):
                        bg.to(f'{name}{c}')
                    dve.wait_ge(S.rw_y, n + 1)
                    for e in range(2):
                        r = slice(64 * e, 64 * e + 64)
                        then(v.tensor_copy(yt[r, :, CH * c:CH * c + CH], ps[r, 5 + 2 * e, :].rearrange("p (b i) -> p b i", i=CH)))
                    upd = ps[:, 6, 0:256].rearrange("p (b i) -> p b i", i=64)
                    if c:
                        then(TT(zst[:, :, :], zst[:, :, :], upd, ALU.add))
                        TT(zst[:, :, :], zst[:, :, :], over(eend[:, :, c], 64), ALU.mult).then_inc(S.rw_chunk_done, 1)
                    else:
                        then(TT(zst[:, :, :], upd, over(eend[:, :, c], 64), ALU.mult))
                        TT(zst[:, :, :], zst[:, :, :], over(eamid[:, :, c + 1], 64), ALU.mult).then_inc(S.rw_chunk_done, 1)
                dve.wait_ge(S.rw_sample_loaded, 64 * (l + 1))

                def sam(b0):
                    return mx[:, b0:b0 + 4, SEQ:T].unsqueeze(3).to_broadcast([128, 4, NS, 64])
                id4 = ident2[:, :].unsqueeze(1).unsqueeze(1).to_broadcast([128, 4, NS, 64])
                TT(s1t[:, :, :, :], srw[:, :, :, :], sam(14), ALU.mult).then_inc(S.rw_sample_in, 1)
                TT(s2t[:, :, :, :], sam(8), id4, ALU.mult).then_inc(S.rw_sample_in, 1)
                then(TT(srw[:, :, :, :], srw[:, :, :, :], wsam[:, :, :].unsqueeze(3).to_broadcast([128, 4, NS, 64]), ALU.mult))
                bg.to('sa')
                dve.wait_ge(S.rw_sample_sum, 3 * l + 1)
                spread = ps[:, 4:8, :].rearrange("p a (b v) -> p a b v", v=64)
                TT(s1t[:, :, :, :], spread, sam(18), ALU.mult).then_inc(S.rw_sample_taken, 1)
                dve.wait_ge(S.rw_sample_taken, l + 1)
                then(TT(srw[:, :, :, :], srw[:, :, :, :], s1t[:, :, :, :], ALU.subtract))
                bg.to('sv')
                dve.wait_ge(S.rw_sample_sum, 3 * l + 2)
                then(TT(s1t[:, :, :, :], spread, sam(4), ALU.mult))
                TT(srw[:, :, :, :], srw[:, :, :, :], s1t[:, :, :, :], ALU.add).then_inc(S.rw_sample_new, 1)
                dve.wait_ge(S.rw_sample_new, l + 1)
                TT(s1t[:, :, :, :], srw[:, :, :, :], sam(0), ALU.mult).then_inc(S.rw_sample_in, 1)
                bg.to('sy')
                dve.wait_ge(S.rw_sample_sum, 3 * l + 3)
                then(TT(s2t[:, :, :, :], spread, id4, ALU.mult))
                v.tensor_reduce(yt[:, :, SEQ:T], s2t[:, :, :, :], AX.X, ALU.add).then_inc(S.rw_gn_in, 1)
                bg.to('gn')
                dve.wait_ge(S.rw_gn_sum, 2 * l + 1)
                STT(yt[:, :, :], ps[:, 4:8, 0:T], -1.0 / RW_HD, yt[:, :, :], ALU.mult, ALU.add).then_inc(S.rw_gn_c, 1)
                bg.to('gnss')
                dve.wait_ge(S.rw_gn_std, l + 1)
                v.reciprocal(ln_s[0:RW_HEADS, :], ln_s[0:RW_HEADS, :]).then_inc(S.rw_gn_inv, 1)
                bg.to('gnsp')
                dve.wait_ge(S.rw_gn_spread, l + 1)
                then(TT(yt[:, :, :], yt[:, :, :], ps[:, 4:8, 0:T], ALU.mult))
                then(TT(yt[:, :, :], yt[:, :, :], over(cols(l, 'rw_lnx_g', 4), T), ALU.mult))
                then(TT(yt[:, :, :], yt[:, :, :], over(cols(l, 'rw_lnx_b', 4), T), ALU.add))
                then(TT(yt[:, :, :], yt[:, :, :], bonus[:, :, :], ALU.add))
                TT(yt[:, :, :], yt[:, :, :], gate[:, :, :], ALU.mult).then_inc(S.rw_out, 1)
                dve.wait_ge(S.rw_out_hi, l + 1)
                TT(ol[:, 0:4, :], yt[:, :, :], oh[:, 0:4, :].bitcast(F32), ALU.subtract).then_inc(S.rw_done, 1)

                bg.to('end')

                bg = behind(l, 8, ret_plan)
                dve.wait_ge(S.evacuated, group0(l, 'in') + 8)
                dve.wait_ge(S.rdec_loaded, 32 * (l + 1))
                TT(kw[:, :, SEQ:T], pret[:, 0:AP_, SEQ:T], pret[:, 0:AP_, SEQ:T], ALU.add).then_inc(S.ret_in, 1)
                bg.to('swap')
                dve.wait_ge(S.ret_swapped, 2 * l + 1)
                TT(rtmp[:, 0:4, :], ps[:, 4:8, 0:T], each(rrot[:, 1, :], 4), ALU.mult).then_inc(S.ret_swap_taken, 1)
                bg.to('swap1')
                dve.wait_ge(S.ret_swapped, 2 * l + 2)
                dve.wait_ge(S.ret_swap_taken, l + 1)
                then(TT(rtmp[:, 4:6, :], ps[:, 4:6, 0:T], each(rrot[:, 1, :], 2), ALU.mult))
                then(TT(pret[:, 0:6, 0:T], pret[:, 0:6, 0:T], each(rrot[:, 0, :], AH), ALU.mult))
                then(TT(pret[:, 0:6, 0:T], pret[:, 0:6, 0:T], rtmp[:, :, :], ALU.add))
                then(TS(pret[:, 3:6, 0:T], pret[:, 3:6, 0:T], 0.125, None, ALU.mult))
                for dst, b0, t0 in ((qs, 0, AH), (kw, AP_, AH + AP_)):
                    for c in range(NCH):
                        cs = slice(CH * c, CH * c + CH)
                        last = TT(dst[:, :, cs], pret[:, b0:b0 + AP_, cs], rdec[:, t0:t0 + AP_, :], ALU.mult)
                last.then_inc(S.a_prepared, 1)
                attention(l, False, 2 * l, bg)

                dve.wait_ge(S.ret_stored, 64 * (l + 1))
                dve.wait_ge(S.evacuated, group0(l, 'in') + 12)
                dve.wait_ge(S.mlb_loaded, 32 * (l + 1))
                own(TS(mlb2[:, :], mlb[:, :], 1.0 / CAP, None, ALU.mult))
                own(v.tensor_copy(rows[:, 0, :], ptail[0:AH, 2, 0:T]))
                v.tensor_copy(rows[:, 1, :], ptail[32:32 + AH, 2, 0:T]).then_inc(S.m_gates_in, 1)
                own(TS(pml[:, AP_:2 * AP_, 0:T], pml[:, AP_:2 * AP_, 0:T], 0.125, None, ALU.mult))
                dve.wait_ge(S.m_logf, l + 1)
                for c in range(NCH):
                    cs = slice(CH * c, CH * c + CH)
                    own(v.tensor_tensor_scan(rows[:, 2, cs], ones[0:AH, :], rows[:, 1, cs], 0.0, ALU.mult, ALU.add))
                own(v.tensor_copy(rows[:, 2, SEQ:T], rows[:, 1, SEQ:T]))
                STT(rows[:, 0, :], rows[:, 0, :], CAP, rows[:, 2, :], ALU.mult, ALU.subtract).then_inc(S.m_rows_c, 1)
                dve.wait_ge(S.m_rows_c, l + 1)
                dve.wait_ge(S.m_m_loaded, 16 * (l + 1))
                own(v.memset(rows[:, 4, 0:CH], 0.0))
                for c in range(NCH):
                    cs = slice(CH * c, CH * c + CH)
                    own(v.tensor_tensor_scan(rows[:, 3, cs], rows[:, 0, cs], rows[:, 0, cs], mcol[:, :] if c else 0.0, ALU.max, ALU.max))
                    if c + 1 < NCH:
                        own(TT(mcol[:, :], rows[:, 2, CH * c + CH - 1:CH * c + CH], rows[:, 3, CH * c + CH - 1:CH * c + CH], ALU.add))
                        own(v.tensor_copy(rows[:, 4, CH * c + CH:CH * c + 2 * CH], mcol[:, :].to_broadcast([AH, CH])))
                TT(rows[:, 3, SEQ:T], rows[:, 0, SEQ:T], rows[:, 4, SEQ:T], ALU.max).then_inc(S.m_rows_m, 1)
                dve.wait_ge(S.m_rows_m, l + 1)
                own(TT(rows[:, 2, :], rows[:, 2, :], rows[:, 3, :], ALU.add))
                own(v.tensor_copy(mfin[:, 0:NS], rows[:, 2, SEQ:T]))
                own(v.tensor_copy(mfin[:, NS:NS + 1], rows[:, 2, SEQ - 1:SEQ]))
                for c in range(NCH):
                    cs = slice(CH * c, CH * c + CH)
                    own(TS(rows[:, 1, cs], rows[:, 0, cs], rows[:, 3, CH * c + CH - 1:CH * c + CH], None, ALU.subtract))
                own(TT(rows[:, 1, SEQ:T], rows[:, 0, SEQ:T], rows[:, 3, SEQ:T], ALU.subtract))
                TT(rows[:, 4, :], rows[:, 4, :], rows[:, 3, :], ALU.subtract).then_inc(S.m_rows_x, 1)
                dve.wait_ge(S.m_spread, 2 * l + 1)
                own(v.tensor_copy(mct[:, :, :], ps[:, 6, 0:16].rearrange("p (c h) -> p c h", h=8)[:, :, 0:AH]))
                negm = masks[:, 4, :].unsqueeze(1).unsqueeze(1).to_broadcast([128, AH, NCH, CH])
                TT(mexp[:, :, :].rearrange("p h (c i) -> p h c i", i=CH), negm,
                   ps[:, 0:AH, 0:SEQ].rearrange("p h (c i) -> p h c i", i=CH), ALU.subtract).then_inc(S.m_exp_in, 1)
                dve.wait_ge(S.m_spread, 2 * l + 2)
                own(TT(kw[:, :, :], pml[:, AP_:2 * AP_, 0:T], ps[:, 3:6, 0:T], ALU.mult))
                own(v.tensor_copy(msk[:, :, :], ps[:, 0:3, SEQ:T]))
                own(v.tensor_copy(mdc[:, :], ps[:, 0:3, SEQ - 1]))
                TT(qs[:, :, :], pml[:, 0:AP_, 0:T], ps[:, 0:3, 0:T], ALU.mult).then_inc(S.a_prepared, 1)
                own(v.tensor_reduce(mnc[:, :, :].rearrange("p c a -> p a c"),
                                    kw[:, :, 0:SEQ].rearrange("p a (c i) -> p a c i", i=CH), AX.X, ALU.add))
                dve.wait_ge(S.a_prepared, 2 * l + 2)
                TT(mnq[:, :, :], qs[:, :, CH:SEQ], over(mnc[:, 0, :], CH), ALU.mult).then_inc(S.m_nq, 1)
                own(TT(mnt[:, :], mnc[:, 0, :], mdc[:, :], ALU.mult))
                own(TT(mnc[:, 1, :], mnc[:, 1, :], mnt[:, :], ALU.add))
                attention(l, True, 2 * l + 1, Parts(no_plan, None))

                dve.wait_ge(S.ml_stored, 160 * (l + 1))
                dve.wait_ge(S.a_done, 2 * l + 2)
                own(v.memset(gu[:, :, :], 0.0))
                with dve.Fori(0, 2) as it:
                    s = it * 16 + slab0(l, 'out')
                    g = it * 2 + group0(l, 'out')
                    lo4(s + 4)
                    lo4(s + 8)
                    residual_group(s + 8, it * 8, 0, it * 2 + 8 * l, g + 1)
                    lo4(s + 12)
                    lo4(s + 16)
                    residual_group(s + 16, it * 8 + 4, 4, it * 2 + (8 * l + 1), g + 2)
                norm(2 * l + 1, l + 1 if l + 1 < DEPTH else None)
                dve.wait_ge(S.x_ready, 8 * l + 8)

                with dve.Fori(0, FF_GROUPS) as it:
                    s = it * 16 + slab0(l, 'up')
                    lo4(s + 4)
                    lo4(s + 8)
                    dve.wait_ge(S.gate_sig, it + (l * FF_GROUPS + 1))
                    TT(gu[:, :, :], sg[:, :, :], ps[:, 0:4, 0:T], ALU.mult).then_inc(S.evacuated, 1)
                    dve.wait_ge(S.evacuated, it * 2 + (group0(l, 'up') + 1))
                    dve.sem_inc(S.gated, 1)
                    lo4(s + 12)
                    lo4(s + 16)
                    dve.wait_ge(S.slab_used, s + 16)
                    TT(gu[:, :, :], gu[:, :, :], ps[:, 4:8, 0:T], ALU.mult).then_inc(S.evacuated, 1)
                    dve.wait_ge(S.evacuated, it * 2 + (group0(l, 'up') + 2))
                    v.tensor_copy(hh[:, ds(it * 4, 4), :], gu[:, :, :]).then_inc(S.hidden_hi, 1)
                    dve.wait_ge(S.hidden_hi, it + (l * FF_GROUPS + 1))
                    TT(hl[:, ds(it * 4, 4), :], gu[:, :, :], hh[:, ds(it * 4, 4), :].bitcast(F32), ALU.subtract).then_inc(S.hidden_ready, 1)

                def down(s, blk, before, g, more):
                    for k in range(4, 24, 4):
                        lo4(s + k)
                    residual_group(s + DOWN_SLABS, blk, 0, before, g + 1)
                    for k in range(24, 48 if more else 44, 4):
                        lo4(s + k)
                    residual_group(s + 2 * DOWN_SLABS, blk + 4, 4, before + 1, g + 2)
                g = group0(l, 'down')
                dve.wait_ge(S.hidden_ready, FF_GROUPS * (l + 1))
                own(v.memset(gu[:, :, :], 0.0))
                if l + 1 < DEPTH:
                    with dve.Fori(0, 2) as it:
                        down(it * (2 * DOWN_SLABS) + slab0(l, 'down'), it * 8, it * 2 + (8 * l + 4), it * 2 + g, True)
                else:
                    down(slab0(l, 'down'), 0, 8 * l + 4, g, True)
                    down(slab0(l, 'down') + 2 * DOWN_SLABS, 8, 8 * l + 6, g + 2, False)
                norm(2 * l + 2, last=l + 1 == DEPTH)


_NAMES = ['x_prompt', 'x_sample', 'state_rw_shift', 'state_rw_wkv', 'state_ret', 'state_ml_c', 'state_ml_n', 'state_ml_m',
          'ln0_g', 'ln0_b', 'w_in', 'rw_mu', 'rw_w0', 'rw_w2', 'rw_a0', 'rw_a2', 'rw_g2', 'rw_kk', 'rw_ka', 'rw_rk',
          'rw_lnx_g', 'rw_lnx_b', 'rw_v0', 'rw_v1', 'rw_vmu', 'rw_v2', 'ml_ib', 'ml_fb', 'ml_norm', 'w_out',
          'ln1_g', 'ln1_b', 'w_gate', 'w_up', 'w_down', 'ln2_g', 'ln2_b']
_OUTS = [('y_prompt', (1, SEQ, D)), ('y_sample', (NS, 1, D)),
         ('p_shift', (DEPTH, 1, D)), ('p_wkv', (DEPTH, 1, RW_HEADS, RW_HD, RW_HD)), ('p_ret', (DEPTH, 1, AH, 64, AV)),
         ('p_mlc', (DEPTH, 1, AH, 64, AV)), ('p_mln', (DEPTH, 1, AH, 64)), ('p_mlm', (DEPTH, 1, AH)),
         ('s_shift', (DEPTH, NS, D)), ('s_wkv', (DEPTH, NS, RW_HEADS, RW_HD, RW_HD)), ('s_ret', (DEPTH, NS, AH, 64, AV)),
         ('s_mlc', (DEPTH, NS, AH, 64, AV)), ('s_mln', (DEPTH, NS, AH, 64)), ('s_mlm', (DEPTH, NS, AH))]


def kernel(**inputs):
    from concourse import bacc
    from concourse.bass_utils import run_bass_kernel_spmd

    nc = bacc.Bacc("TRN2", target_bir_lowering=False, num_devices=1, dynamic_dma_scratch_size=64)
    arrays, a = {}, {}
    for name in _NAMES:
        arrays["in_" + name] = np.ascontiguousarray(inputs[name])
    for name, table in constants().items():
        arrays["in_" + name] = table
    for name, x in arrays.items():
        a[name[3:]] = nc.dram_tensor(name, x.shape, mybir.dt.from_np(x.dtype), kind="ExternalInput").ap()
    o = {name: nc.dram_tensor("out_" + name, shape, F32, kind="ExternalOutput").ap() for name, shape in _OUTS}
    build(nc, a, o)
    r = run_bass_kernel_spmd(nc, [arrays], core_ids=[0])
    return tuple(r.results[0]["out_" + name] for name, _ in _OUTS)
```

```python
import numpy as np
import concourse.bass as bass
from concourse import mybir

F32 = mybir.dt.float32
F32R = mybir.dt.float32r
ALU = mybir.AluOpType
ACT = mybir.ActivationFunctionType
AX = mybir.AxisListType

D = 2048
SEQ, NS = 256, 8
T = SEQ + NS
TW = T + NS
DEPTH = 2
KB = D // 128
CH = 128
NCH = SEQ // CH
RW_W, RW_HEADS, RW_HD = 512, 8, 64
RW_BLK = RW_W // 128
RW_P = 3 * RW_W + 64 + 64 + 128
RW_PB = RW_P // 128
AH, AP_, AV = 6, 3, 128
P_TOTAL = 6412
PAST = 2048
D_FF = 5632
FB = D_FF // 128
ALPHA = (2 * DEPTH) ** 0.25
LN_EPS, NORM_EPS, GN_EPS = 1e-5, 1e-6, 64e-5
CAP = 15.0
DECAY = float(np.exp(-0.5))
GC = 512
RING = 4

PRM = [('rw_mu', RW_PB), ('rw_w0', 4), ('rw_a0', 4), ('rw_kk', 4), ('rw_ka', 4), ('rw_rk', 4), ('rw_lnx_g', 4),
       ('rw_lnx_b', 4), ('ml_norm', AH), ('ln1_g', KB), ('ln1_b', KB), ('ln2_g', KB), ('ln2_b', KB), ('rw_v0', 4)]
PRM_AT, _n = {}, 0
for _name, _rows in PRM:
    PRM_AT[_name] = _n
    _n += _rows
PRM_ROWS = _n

TAIL_SLABS = KB // 2
GROUP_SLABS = KB // 2
IN_GROUPS = 12
DOWN_SLABS = FB // 2
FF_GROUPS = D_FF // GC
LAYER_SLABS = TAIL_SLABS + IN_GROUPS * GROUP_SLABS + 4 * GROUP_SLABS + 2 * FF_GROUPS * GROUP_SLABS + 4 * DOWN_SLABS
LAYER_GROUPS = 1 + IN_GROUPS + 8 + 2 * FF_GROUPS + 4
TOTAL_SLABS = DEPTH * LAYER_SLABS


def constants():
    f = np.float32
    p, q = np.arange(128)[:, None], np.arange(128)[None, :]
    ident = (p == q)
    half = (p // 64 == q // 64)
    swap = (q == (p ^ 32))
    base = np.concatenate([ident, half, swap, np.ones((128, 128))], 1).astype(f)
    ident2 = (p % 64 == np.arange(64)[None, :]).astype(f)
    strict, incl = (p < q), (p <= q)
    neg = np.where(incl, 0.0, -1e30)
    first = ((p // 2 == q // 2) & (p < q))
    levels = [((p // (2 * n) == q // (2 * n)) & (p % (2 * n) >= n) & (q % (2 * n) < n)) for n in (1, 2, 4, 8, 16, 32, 64)]
    masks = np.concatenate([strict, incl, first, incl, neg] + levels, 1).astype(f)
    inv = (f(10000.0) ** (-np.arange(32, dtype=f) / f(32))).astype(f)
    pos = np.concatenate([np.arange(SEQ), np.full(NS, PAST)]).astype(f)
    ang = (pos[None, :] * inv[:, None]).astype(f).astype(np.float64)
    cos = np.tile(np.cos(ang), (4, 1))
    sin = np.concatenate([-np.sin(ang), np.sin(ang)] * 2, 0)
    rot = np.concatenate([cos, sin], 1).astype(f)
    lg = np.log1p(-np.exp2(-5.0 - np.arange(AH)))
    idx = np.arange(CH)
    rel = idx[None, :] - idx[:, None]
    dmask = [np.where(rel >= 0, np.exp(np.maximum(rel, 0) * g), 0.0) for g in lg]
    ofhalf = lambda pr: lg[2 * pr + np.arange(128) // 64][:, None]
    qdec = [np.exp((idx + 1.0)[None, :] * ofhalf(pr)) for pr in range(AP_)]
    kend = [np.exp((CH - 1.0 - idx)[None, :] * ofhalf(pr)) for pr in range(AP_)]
    ret = np.concatenate(dmask + qdec + kend, 1).astype(f)
    gam = np.concatenate([np.exp(ofhalf(pr)) for pr in range(AP_)] + [np.exp(CH * ofhalf(pr)) for pr in range(AP_)], 1).astype(f)
    sel = np.zeros((RW_HEADS, AH + 4, 128), f)
    for h in range(RW_HEADS):
        if h < AH:
            sel[h, h, :] = 1
        sel[h, AH + h // 2, 64 * (h % 2):64 * (h % 2) + 64] = 1
    head = np.arange(128) // 64
    whole = np.concatenate([np.tile(np.arange(AH) == h, (128, 1)) for h in range(AH)], 1)
    pair6 = np.concatenate([2 * p + head[:, None] == np.arange(AH)[None] for p in range(AP_)], 1)
    pair8 = np.concatenate([2 * p + head[:, None] == np.arange(RW_HEADS)[None] for p in range(4)], 1)
    sums = np.concatenate([whole, pair6, pair8], 1).astype(f)
    same = np.zeros((128, NS), f)
    same[:AH * NS] = np.tile(np.eye(NS), (AH, 1))
    sums = np.concatenate([sums, same], 1).astype(f)
    return {'c_base': base, 'c_ident2': ident2, 'c_masks': masks, 'c_rot': rot, 'c_ret': ret, 'c_gam': gam,
            'c_sel': sel.reshape(RW_HEADS, -1), 'c_sums': sums}


def build(nc, a, o):
    mm, tr = nc.tensor.matmul, nc.tensor.transpose
    ds = bass.ds

    here = [-(-nc.sbuf_base // 32) * 32]

    def put(name, shape, dt=F32):
        n = int(np.prod(shape[1:])) * 4
        t = nc.alloc_sbuf_tensor_at(name, shape, dt, offset=here[0])
        here[0] += -(-n // 32) * 32
        return t

    xh = put("x_hi", [128, KB, TW], F32R)
    xl = put("x_lo", [128, KB, TW], F32R)
    raw = put("w_raw", [128, RING, 2, GC])
    wh = put("w_hi", [128, RING, 2, GC], F32R)
    wl = put("w_lo", [128, RING, 2, GC], F32R)
    vfirst = put("v_first", [128, RW_BLK, T])
    prm2 = put("params", [128, 2, 128])
    prm0 = put("params_ln0", [128, 32])
    base = put("base_tables", [128, 4, 128])
    ident2 = put("ident2", [128, 64])
    masks = put("masks", [128, 12, 128])
    gam = put("gammas", [128, 2 * AP_])
    sel = put("selectors", [RW_HEADS, AH + 4, 128])
    sums = put("sum_selectors", [128, AH * AH + AP_ * AH + 4 * RW_HEADS + NS])
    same = sums[0:AH * NS, AH * AH + AP_ * AH + 4 * RW_HEADS:]
    eps = put("eps", [128, 4])
    whole6 = lambda h: sums[:, AH * h:AH * h + AH]
    pair6 = lambda p: sums[:, AH * AH + AH * p:AH * AH + AH * p + AH]
    pair8 = lambda p: sums[:, AH * AH + AP_ * AH + 8 * p:AH * AH + AP_ * AH + 8 * p + 8]
    ident, halves, swap, ones = (base[:, i, :] for i in range(4))

    arena = here[0]

    def at(name, off, shape, dt=F32):
        assert arena + off + int(np.prod(shape[1:])) * 4 <= nc.sbuf_usable_end, name
        return nc.alloc_sbuf_tensor_at(name, shape, dt, offset=arena + off)

    BLK, BLW = T * 4, TW * 4
    O_H, O_L = 0, KB * BLK
    P_RET = 2 * KB * BLK
    P_MX = P_RET + 18 * BLW
    P_RAW = P_MX + 22 * BLK
    P_T = P_RAW + 16 * BLW
    P_END = P_T + 24 * BLK
    oh = at("o_hi", O_H, [128, KB, T], F32R)
    ol = at("o_lo", O_L, [128, KB, T], F32R)
    pret = at("p_ret", P_RET, [128, 18, TW])
    mx = at("rw_mixed", P_MX, [128, 22, T])
    praw = at("p_rw", P_RAW, [128, 16, TW])
    gate = at("rw_gate", P_T, [128, 4, T])
    bonus = at("rw_bonus", P_T + 4 * BLK, [128, 4, T])
    lw = at("rw_logw", P_T + 8 * BLK, [128, 4, T])
    ep = at("rw_ep", P_T + 12 * BLK, [128, 4, T])
    em = at("rw_em", P_T + 16 * BLK, [128, 4, T])
    tmp = at("rw_tmp", P_T + 20 * BLK, [128, 4, T])
    hh = at("h_hi", 0, [128, FB, T], F32R)
    hl = at("h_lo", FB * BLK, [128, FB, T], F32R)
    R = at("resid", 2 * FB * BLK, [128, KB, T])
    sg = at("sig_gate", (2 * FB + KB) * BLK, [128, 4, T])
    gu = at("gate_up", (2 * FB + KB + 4) * BLK, [128, 4, T])
    SQ = at("ln_squares", 0, [128, KB, T])
    R1 = [at(f"resid1_{q}", off, [128, 4, T]) for q, off in
          enumerate([P_RET + 12288] + [P_MX + 16 * BLW + 4 * BLK * i for i in range(3)])]
    small = [P_END]

    def little(name, shape, dt=F32):
        t = at(name, small[0], shape, dt)
        small[0] += -(-int(np.prod(shape[1:])) * 4 // 32) * 32
        return t

    ln_s = little("ln_sum", [128, T])
    ln_m = little("ln_stat", [128, T])
    ptail = little("p_tail", [128, 3, TW])
    prm_tok = at("params_rows", (2 * FB + KB) * BLK, [PRM_ROWS, 128])
    prm0_tok = at("params0_rows", (2 * FB + KB) * BLK + 512, [32, 128])
    mlb = little("ml_bias", [AH, 2])
    vmu = little("v_mu", [96, 1])
    ka1 = little("one_minus_ka", [128, 4])
    amid = little("rw_amid", [128, 4, NCH])
    namid = little("rw_namid", [128, 4, NCH])
    eamid = little("rw_eamid", [128, 4, NCH])
    wsam = little("rw_wsam", [128, 4, NS])
    enam = little("rw_enamid", [128, 4, NCH])
    eend = little("rw_eend", [128, 4, NCH])
    mlb2 = little("ml_bias_scaled", [AH, 2])
    mfin = little("m_final", [AH, NS + 1])
    mcol = little("m_carried", [AH, 1])
    rows9 = at("shift_cols", P_RET + 16384, [128, KB, 1 + NS])
    mq = at("rw_mq", P_RAW, [128, RW_HEADS, 2, CH])
    tok = at("rw_tok", P_RAW + 8192, [128, 3, RW_W])
    zst = at("rw_state", P_RAW + 8192 + 6144, [128, 4, 64])
    tm = at("rw_t", P_T + 8 * BLK, [128, RW_HEADS, CH])
    ym = at("rw_tT", P_T + 8 * BLK + 4096, [128, RW_HEADS, CH])
    xm = at("rw_x", P_T + 8 * BLK + 8192, [128, RW_HEADS, CH])
    lm = at("rw_l", P_T + 8 * BLK + 12288, [128, RW_HEADS, CH])
    qb = at("rw_qb", O_H + 4352, [128, RW_HEADS, CH])
    lmk = at("rw_lmask", O_H + 8448, [128, RW_HEADS, CH])
    wsb = at("rw_w", O_H + 12544, [128, RW_W])
    usb = at("rw_u", O_H + 14592, [128, RW_W])
    yt = at("rw_y", O_L + 4352, [128, 4, T])
    lora = at("rw_lora", O_L + 8576, [128, 3, RW_W])
    srw = at("rw_sample", O_L + 8576, [128, 4, NS, 64])
    s1t = at("rw_sample_t1", P_RAW, [128, 4, NS, 64])
    s2t = at("rw_sample_t2", P_T + 8 * BLK, [128, 4, NS, 64])
    shift_tok = at("shift_rows", P_RET, [NS, D])
    shift_out = at("shift_out", P_RET + 8192, [1 + NS, D])
    B0 = P_MX + 16 * BLW + 12 * BLK
    kw = at("a_kw", B0, [128, AP_, T])
    qs = at("a_qs", B0 + 3168, [128, AP_, T])
    ktok = at("a_ktok", B0 + 6336, [128, NCH, AP_ * 128])
    vtok = at("a_vtok", B0 + 9408, [128, NCH, AH * 128])
    ssb = at("a_scores", B0 + 15552, [128, 2, AH, CH])
    st = at("a_state", B0 + 21696, [128, 2, AP_, 128])
    men = at("m_guard", B0 + 24768, [AH, T])
    mdn = at("m_den", B0 + 24768 + 1056, [AH, T])
    ay = at("a_y", B0 + 27840, [128, AH, T])
    sq = at("a_squares", B0, [128, AH, T])
    assert B0 + 34176 <= P_END
    rtmp = at("r_tmp", B0 + 6336, [128, AH, T])
    rsam = at("r_sample", P_MX + 16 * BLW, [128, AP_, NS, 128])
    rdec = at("r_decays", O_H + 10 * BLK, [128, 12, 128])
    rrot = at("r_rotary", O_L + 10 * BLK, [128, 2, T])
    mgate = at("m_gate", B0 + 6336, [128, AH, T])
    pml = at("p_ml", P_MX, [128, 16, TW])
    kvs = at("a_kv_sample", B0 + 15552, [128, AP_ + 1, AH * NS])
    kst = at("a_k_turned", B0 + 15552 + 1024, [AH * NS, AP_, 128])
    vst = at("a_v_streams", B0 + 6336, [AH * NS, NS, 128])
    msam = at("m_sample", P_RET, [128, AP_, NS, 128])
    rows = at("m_rows", B0 + 27840, [AH, 6, T])
    mnq = at("m_nq", P_RET + 12288 + 4 * BLK, [128, AP_, CH])
    mnt = at("m_ntmp", B0 + 26880, [128, AP_])
    mnc = at("m_ncols", B0 + 26912, [128, 2, AP_])
    mct = at("m_ct", B0 + 26944, [128, NCH, AH])
    msn = at("m_nsample", B0 + 27008, [128, AP_, NS])
    msk = at("m_scol", B0 + 27104, [128, AP_, NS])
    mpd = at("m_nprod", B0 + 27200, [128, AP_, NS])
    mdc = at("m_cdecay", B0 + 27296, [128, AP_])
    x_tok = at("x_rows", 0, [128, 3, D])
    y_tok = at("y_rows", 0, [128, 3, D])

    ps = nc.alloc_psum_tensor("psum", [128, 8, 512], F32)

    made = {}

    class Names:
        def __getattr__(self, name):
            if name not in made:
                made[name] = nc.alloc_semaphore(name)
            return made[name]
    S = Names()
    raw_loaded = [nc.alloc_semaphore(f"raw_loaded{i}") for i in range(RING)]
    tail_loaded = [nc.alloc_semaphore(f"tail_loaded{i}") for i in range(RING)]

    class Own:
        def __init__(self, eng, sem):
            self.eng, self.sem, self.n = eng, sem, 0

        def __call__(self, ins):
            self.n += 1
            ins.then_inc(self.sem, 1)
            self.eng.wait_ge(self.sem, self.n)

    def cols(l, name, n):
        return prm2[:, l % 2, PRM_AT[name]:PRM_AT[name] + n]

    def col(l, name, i):
        return prm2[:, l % 2, PRM_AT[name] + i:PRM_AT[name] + i + 1]

    def quarter(n, q):
        return R1[q][:, :, :] if n % 2 else R[:, 4 * q:4 * q + 4, :]

    PIECES = ((0, 2), (2, 4), (4, 8), (8, 12), (12, 16))

    def piece(n, i):
        b0, b1 = PIECES[i]
        return quarter(n, b0 // 4)[:, b0 % 4:b0 % 4 + b1 - b0, :]

    def over(ap, n):
        return ap.unsqueeze(2).to_broadcast([ap.shape[0], ap.shape[1], n])

    def each(ap, m):
        return ap.unsqueeze(1).to_broadcast([ap.shape[0], m, ap.shape[1]])

    def hb(h, b0, w):
        return b0 + h % 2, slice(w * (h // 2), w * (h // 2) + w)

    def halves_of(b0, w, n):
        return ps[:, b0:b0 + 2, 0:w * (n // 2)].rearrange("p e (q i) -> p q e i", i=w)

    def pairs(ap):
        return ap.rearrange("p (q e) i -> p q e i", e=2)

    def each2(ap, m):
        return ap.unsqueeze(1).unsqueeze(1).to_broadcast([ap.shape[0], m, 2, ap.shape[1]])

    def slab0(l, part):
        n = l * LAYER_SLABS
        for name, slabs in (('tail', TAIL_SLABS), ('in', IN_GROUPS * 8), ('out', 32), ('up', 16 * FF_GROUPS),
                            ('down', 4 * DOWN_SLABS)):
            if name == part:
                return n
            n += slabs

    def group0(l, part):
        n = 1 + l * LAYER_GROUPS
        for name, groups in (('tail', 1), ('in', IN_GROUPS), ('out', 8), ('up', 2 * FF_GROUPS), ('down', 4)):
            if name == part:
                return n
            n += groups

    def plan(steps, blocks):
        at_, out = 0, {}
        for name, n in steps:
            at_ = min(at_ + n, blocks)
            out[name] = at_
        out['end'] = blocks
        return out

    rw_steps = [('in', 4), ('a', 0), ('g', 1), ('v', 1), ('kk', 4), ('kks', 1), ('bonus', 5), ('tok0', 4),
                ('pairs0', 0), ('more0', 1), ('l0', 1), ('x0.0', 1), ('y0.0', 0), ('x0.1', 1), ('y0.1', 0),
                ('x0.2', 1), ('y0.2', 0), ('x0.3', 0), ('y0.3', 0), ('x0.4', 2), ('y0.4', 0), ('x0.5', 2), ('y0.5', 0),
                ('w0', 1), ('u0', 1), ('out0', 1), ('tok1', 2), ('pairs1', 0), ('more1', 1), ('l1', 1), ('x1.0', 1),
                ('y1.0', 0), ('x1.1', 1), ('y1.1', 0), ('x1.2', 1), ('y1.2', 2), ('x1.3', 1), ('y1.3', 0), ('x1.4', 0),
                ('y1.4', 0), ('x1.5', 1), ('y1.5', 0), ('w1', 1), ('u1', 0), ('out1', 1), ('sa', 2), ('sv', 0),
                ('sy', 4), ('gn', 2), ('gnss', 3), ('gnsp', 2)]
    ret_steps = [('swap', 6), ('swap1', 7), ('turn0', 8), ('turn1', 2), ('score', 1), ('num0', 2), ('num1', 5),
                 ('vt', 3), ('v0', 4), ('v1', 2), ('v2', 0), ('sy', 2), ('sumsq', 2), ('spread', 6), ('spread1', 2)]
    ml_steps = [('rows', 9), ('spread_m', 4), ('spread_e', 2), ('turn0', 2), ('turn1', 1), ('score', 1), ('num0', 2),
                ('num1', 2), ('vt', 1), ('v0', 2), ('v1', 1), ('v2', 1), ('sy', 1), ('sumsq', 1), ('spread', 2),
                ('spread1', 1)]
    OUT_A = 20
    ml_plan = plan(ml_steps, 2 * OUT_A)
    BEHIND = 32
    rw_plan, ret_plan = plan(rw_steps, 2 * BEHIND), plan(ret_steps, 2 * BEHIND)

    class Parts:
        def __init__(self, plan_, one):
            self.i, self.one, self.goals, before = 0, one, {}, 0
            slabs = plan_['end'] // 8
            for name, n in plan_.items():
                self.goals[name] = max(before // 2, n // 2 - 2, (n - 1) // (2 * slabs) * slabs)
                before = n
            self.goals['end'] = plan_['end'] // 2
            self.names = list(self.goals)
            self.goal = self.goals[self.names[0]]

        def step(self):
            if self.i < self.goal:
                self.one(self.i)
                self.i += 1

        def to(self, name):
            self.goal = self.goals[name]
            while self.i < self.goal:
                self.step()
            following = self.names.index(name) + 1
            if following < len(self.names):
                self.goal = self.goals[self.names[following]]

    block = nc.Block()
    with block:
        @block.sync
        def _(sp):
            def free(s):
                if not (isinstance(s, int) and s < RING):
                    sp.wait_ge(S.hi_ready, s - RING + 1)
                    sp.wait_ge(S.lo_ready, s - RING + 1)

            def load(s, j, src, k0, c0):
                free(s)
                sp.dma_start(raw[:, j % RING, :, :], src[:, k0:k0 + 2, ds(c0, GC)]).then_inc(raw_loaded[j % RING], 16)

            sp.wait_ge(S.raw_cleared, 1)
            sp.wait_ge(S.start_loaded, 48)
            for l in range(DEPTH):
                win = a['w_in'][l].rearrange("(k p) n -> p k n", p=128)
                c0 = IN_GROUPS * GC
                for j in range(TAIL_SLABS):
                    s = slab0(l, 'tail') + j
                    free(s)
                    rj = raw[:, j % RING]
                    sp.dma_start(rj[:, :, 0:262], win[:, 2 * j:2 * j + 2, c0:c0 + 262]).then_inc(raw_loaded[j % RING], 16)
                    sp.dma_start(rj[:, :, 288:294], win[:, 2 * j:2 * j + 2, c0 + 262:c0 + 268]).then_inc(tail_loaded[j % RING], 16)
                    if l:
                        v1 = a['rw_v1'][l - 1].rearrange("(k p) n -> p k n", p=128)
                        sp.dma_start(rj[:, :, 320:352], v1[:, 2 * j:2 * j + 2, :]).then_inc(tail_loaded[j % RING], 16)

                def stream(src, s0, bodies, kblocks):
                    slabs = kblocks // 2
                    with sp.Fori(0, bodies) as it:
                        for j in range(2 * slabs):
                            load(it * (2 * slabs) + (s0 + j), j, src, 2 * (j % slabs), it * (2 * GC) + GC * (j // slabs))
                stream(win, slab0(l, 'in'), IN_GROUPS // 2, KB)
                wo = a['w_out'][l].rearrange("(k p) n -> p k n", p=128)
                s = slab0(l, 'out')
                for first, last in ((0, 5), (5, 8)):
                    for g in range(4):
                        for j in range(first, last):
                            load(s, s, wo, 2 * j, g * GC)
                            s += 1
                wg = a['w_gate'][l].rearrange("(k p) n -> p k n", p=128)
                wu = a['w_up'][l].rearrange("(k p) n -> p k n", p=128)
                with sp.Fori(0, FF_GROUPS) as it:
                    for j in range(16):
                        load(it * 16 + (slab0(l, 'up') + j), j, wg if j < 8 else wu, 2 * (j % 8), it * GC)
                stream(a['w_down'][l].rearrange("(k p) n -> p k n", p=128), slab0(l, 'down'), 2, FB)

            for t in range(2):
                sp.wait_ge(S.y_rows, t + 1)
                sp.dma_start(o['y_prompt'][0, 128 * t:128 * t + 128, :], y_tok[:, t, :]).then_inc(S.y_stored, 16)
            sp.wait_ge(S.y_rows, 3)
            sp.dma_start(o['y_sample'][:, 0, :], y_tok[0:NS, 2, :]).then_inc(S.y_stored, 16)
            sp.wait_ge(S.y_stored, 48)
            sp.wait_ge(S.shift_stored, 32 * DEPTH)
            sp.wait_ge(S.rw_stored, 16 * 5 * DEPTH)
            sp.wait_ge(S.ret_stored, 16 * 4 * DEPTH)
            sp.wait_ge(S.ml_stored, 16 * 10 * DEPTH)

        @block.tensor
        def _(pe):
            def product(s, j, g, k0, last_k, bh, bl, nt, blocks=4, ready=None, setat=None):
                pe.wait_ge(S.lo_ready, s + 1)
                if k0 == 0 and g is not None:
                    pe.wait_ge(S.evacuated, g - 1)
                if setat is None:
                    setat = 4 * ((j // ((last_k + 1) // 2)) % 2)
                if ready is not None:
                    pe.wait_ge(S.x_ready, ready + (k0 // 4 + 2 if k0 else 1))
                for k in (k0, k0 + 1):
                    for n in range(blocks):
                        w0 = wh[:, j % RING, k - k0, 128 * n:128 * n + 128]
                        w1 = wl[:, j % RING, k - k0, 128 * n:128 * n + 128]
                        out = ps[:, setat + n, 0:nt]
                        mm(out, w1, bh[:, k, 0:nt], start=(k == 0), stop=False)
                        mm(out, w0, bl[:, k, 0:nt], start=False, stop=False)
                        last = mm(out, w0, bh[:, k, 0:nt], start=False, stop=(k == last_k))
                last.then_inc(S.slab_used, 1)

            def groups(s0, g0, bodies, kblocks, bh, bl, nt, ready=None, hidden=None):
                slabs = kblocks // 2
                with pe.Fori(0, bodies) as it:
                    for j in range(2 * slabs):
                        if hidden and j == slabs - 2:
                            pe.wait_ge(S.hidden_ready, hidden)
                        product(it * (2 * slabs) + (s0 + j), j, it * 2 + (g0 + j // slabs), 2 * (j % slabs),
                                kblocks - 1, bh, bl, nt, ready=ready if j < slabs else None)

            def kblock(s, half, k, bank0, bh, bl, first, last_k):
                if not half:
                    pe.wait_ge(S.lo_ready, s + 1)
                for n in range(4):
                    w0 = wh[:, s % RING, half, 128 * n:128 * n + 128]
                    w1 = wl[:, s % RING, half, 128 * n:128 * n + 128]
                    out = ps[:, bank0 + n, 0:T]
                    mm(out, w1, bh[:, k, 0:T], start=(k == first), stop=False)
                    mm(out, w0, bl[:, k, 0:T], start=False, stop=False)
                    last = mm(out, w0, bh[:, k, 0:T], start=False, stop=(k == last_k))
                if half:
                    last.then_inc(S.slab_used, 1)

            class Behind:
                def __init__(self, s0, g0, plan_, kblocks, bh, bl, done=None):
                    self.s0, self.g0, self.plan, self.kblocks, self.b, self.i = s0, g0, plan_, kblocks, (bh, bl), 0
                    self.done = done

                def to(self, name):
                    while self.i < self.plan[name]:
                        k = self.i % self.kblocks
                        if k == 0:
                            pe.wait_ge(S.evacuated, self.g0 + self.i // self.kblocks)
                        if self.i == 4 and self.done:
                            pe.wait_ge(S.a_done, self.done)
                        kblock(self.s0 + self.i // 2, self.i % 2, k, 0, *self.b, 0, self.kblocks - 1)
                        self.i += 1

            def to_rows(src, n, w, bank0, sem):
                for b in range(n):
                    last = tr(ps[0:w, bank0 + b // 4, 128 * (b % 4):128 * (b % 4) + 128], src(b), ident)
                last.then_inc(sem, 1)

            def norm_sums(n, nxt=None):
                pe.wait_ge(S.ln_sum, n + 1)
                mm(ps[:, 0, 0:T], ones, ln_s[:, :], start=True, stop=True).then_inc(S.ln_sum_all, 1)
                if nxt is not None:
                    pe.wait_ge(S.prm_loaded, 16 * (13 * (nxt + 1) + nxt))
                    pr = PRM_ROWS if nxt else PRM_ROWS - 4
                    tr(ps[:, 2, 0:pr], prm_tok[0:pr, :], ident[0:pr, 0:pr])
                    pe.wait_ge(S.shift_loaded, 16 * (nxt + 1))
                    for b in range(KB):
                        last = tr(ps[:, 3, 8 * b:8 * b + 8], shift_tok[:, 128 * b:128 * b + 128], ident[0:NS, 0:NS])
                    last.then_inc(S.layer_turned, 1)
                for q in range(4):
                    pe.wait_ge(S.ln_squared, 4 * n + q + 1)
                    for b in range(4 * q, 4 * q + 4):
                        last = mm(ps[:, 1, 0:T], ones, SQ[:, b, :], start=(b == 0), stop=(b == KB - 1))
                last.then_inc(S.ln_sumsq_all, 1)

            pe.wait_ge(S.x_loaded, 48)
            for q in range(4):
                if q == 2:
                    pe.wait_ge(S.start_loaded, 48)
                if q >= 2:
                    pe.wait_ge(S.x_taken_odd if q % 2 else S.x_taken, 1)
                for b in range(4):
                    bank = ps[:, 4 * (q % 2) + b]
                    f = 128 * (4 * q + b)
                    for t in range(2):
                        tr(bank[:, 128 * t:128 * t + 128], x_tok[:, t, f:f + 128], ident)
                    last = tr(bank[:, SEQ:T], x_tok[0:NS, 2, f:f + 128], ident[0:NS, 0:NS])
                last.then_inc(S.x_turned, 1)
            pe.wait_ge(S.tables_loaded, 16 * 5)
            pe.wait_ge(S.x_taken_odd, 2)
            tr(ps[:, 4, 0:32], prm0_tok[:, :], ident[0:32, 0:32]).then_inc(S.prm0_turned, 1)
            norm_sums(0, 0)

            def attention(l, ml, n, bg):
                src = pml if ml else pret
                qT = (lambda p: src[:, p, :])
                kT = (lambda p: src[:, AP_ + p, :])
                vT = (lambda h: src[:, 2 * AP_ + h, :])
                for c in range(NCH):
                    bg.to(f'turn{c}')
                    if c:
                        pe.wait_ge(S.a_tok, 2 * n + 1)
                    else:
                        pe.wait_ge(S.a_prepared, n + 1)
                    for p in range(AP_):
                        tr(ps[:, 4, 128 * p:128 * p + 128], kw[:, p, CH * c:CH * c + CH], ident)
                    for h in range(AH):
                        last = tr(ps[:, 5 + h // 4, 128 * (h % 4):128 * (h % 4) + 128],
                                  vT(h)[:, CH * c:CH * c + CH], ident)
                    last.then_inc(S.a_turned, 1)
                bg.to('score')
                pe.wait_ge(S.a_tok, 2 * n + 2)
                for c in range(NCH):
                    for h in range(AH):
                        r = slice(64 * (h % 2), 64 * (h % 2) + 64)
                        bank, hc = hb(h, 4 + 2 * c, 128)
                        last = mm(ps[:, bank, hc],
                                  kT(h // 2)[r, CH * c:CH * c + CH], qT(h // 2)[r, CH * c:CH * c + CH], start=True, stop=True)
                    last.then_inc(S.a_scored, 1)
                for c in range(NCH):
                    bg.to(f'num{c}')
                    pe.wait_ge(S.a_weighted, 2 * n + 2)
                    if c:
                        pe.wait_ge(S.a_state_kept, 2 * n + 1)
                        pe.wait_ge(S.a_y_kept, 2 * n + 1)
                    for h in range(AH):
                        r = slice(64 * (h % 2), 64 * (h % 2) + 64)
                        bank, hc = hb(h, 4, 128)
                        mm(ps[:, bank, hc], vtok[:, c, 128 * h:128 * h + 128],
                           ssb[:, c, h, :], start=True, stop=(c == 0))
                        if c:
                            mm(ps[:, bank, hc], st[r, 0, h // 2, :],
                               qs[r, h // 2, CH * c:CH * c + CH], start=False, stop=True)
                    if ml:
                        dc = slice(CH * c, CH * c + CH)
                        for h in range(AH):
                            mm(ps[0:AH, 6, dc], whole6(h), ssb[:, c, h, :], start=(h == 0), stop=(c == 0 and h == AH - 1))
                        if c:
                            pe.wait_ge(S.m_nq, l + 1)
                            for p in range(AP_):
                                mm(ps[0:AH, 6, dc], pair6(p), mnq[:, p, :], start=False, stop=(p == AP_ - 1))
                    for h in range(AH):
                        r = slice(64 * (h % 2), 64 * (h % 2) + 64)
                        last = mm(ps[r, 7, 128 * (h // 2):128 * (h // 2) + 128], ktok[:, c, 64 * h:64 * h + 64],
                                  vtok[:, c, 128 * h:128 * h + 128], start=True, stop=True)
                    last.then_inc(S.a_summed, 1)
                bg.to('vt')
                pe.wait_ge(S.a_kv_sample, n + 1)
                for i in range(AP_ + 1):
                    last = tr(ps[0:AH * NS, 4 + i // AP_, 128 * (i % AP_):128 * (i % AP_) + 128], kvs[:, i, :], ident)
                last.then_inc(S.a_kv_turned, 1)
                for p in range(AP_):
                    bg.to(f'v{p}')
                    if p == 0:
                        pe.wait_ge(S.a_kv_ready, 2 * n + 2)
                    elif ml or p > 1:
                        pe.wait_ge(S.a_pair_done, n * AP_ + (p if ml else 1))
                    for b in range(2):
                        last = mm(ps[:, (4 if ml or p != 1 else 6) + b, :], kst[:, p, :],
                                  vst[:, 4 * b:4 * b + 4, :].rearrange("p b v -> p (b v)"), start=True, stop=True)
                    last.then_inc(S.a_vspread, 1)
                bg.to('sy')
                pe.wait_ge(S.a_pair_done, n * AP_ + AP_)
                sam = msam if ml else rsam
                for h in range(AH):
                    r = slice(64 * (h % 2), 64 * (h % 2) + 64)
                    for b in range(NS):
                        last = mm(ps[:, 4 + h % 2, 8 * (h // 2) + b:8 * (h // 2) + b + 1], sam[r, h // 2, b, :],
                                  qT(h // 2)[r, SEQ + b:SEQ + b + 1], start=True, stop=True)
                if ml:
                    pe.wait_ge(S.m_nprod, l + 1)
                    for p in range(AP_):
                        last = mm(ps[0:AH, 6, SEQ:T], pair6(p), mpd[:, p, :], start=(p == 0), stop=(p == AP_ - 1))
                last.then_inc(S.a_sample_y, 1)
                bg.to('sumsq')
                pe.wait_ge(S.a_squares, n + 1)
                pe.wait_ge(S.a_state_kept, 2 * n + 2)
                for h in range(AH):
                    last = mm(ps[0:AH, 7, 0:T], whole6(h), sq[:, h, :], start=(h == 0), stop=(h == AH - 1))
                last.then_inc(S.a_sumsq, 1)
                bg.to('spread')
                pe.wait_ge(S.a_inv, n + 1)
                for h in range(4):
                    last = mm(ps[:, 4 + h, 0:T], sel[0:AH, h, :], ln_s[0:AH, :], start=True, stop=True)
                last.then_inc(S.a_spread, 1)
                bg.to('spread1')
                pe.wait_ge(S.a_normed, n + 1)
                for h in range(4, AH):
                    last = mm(ps[:, h, 0:T], sel[0:AH, h, :], ln_s[0:AH, :], start=True, stop=True)
                last.then_inc(S.a_spread, 1)
                bg.to('end')

            for l in range(DEPTH):
                pe.wait_ge(S.layer_taken, l + 1)
                for j in range(TAIL_SLABS):
                    product(slab0(l, 'tail') + j, j, None, 2 * j, KB - 1, xh, xl, TW, blocks=3, ready=10 * l, setat=4)
                groups(slab0(l, 'in'), group0(l, 'in'), 2, KB, xh, xl, TW)

                pe.wait_ge(S.evacuated, group0(l, 'in') + 4)
                pe.wait_ge(S.shift_cols, l + 1)
                to_rows(lambda b: rows9[:, b, :], KB, 1 + NS, 4, S.shift_turned)
                bg = Behind(slab0(l, 'in') + 32, group0(l, 'in') + 4, rw_plan, KB, xh, xl)
                bg.to('in')
                pe.wait_ge(S.shift_rows, l + 1)

                pe.wait_ge(S.rw_in, l + 1)

                def four(lhs, rhs):
                    for b in range(4):
                        last = mm(ps[:, 4 + b, 0:T], lhs(slice(128 * b, 128 * b + 128)), rhs, start=True, stop=True)
                    return last
                four(lambda c: lora[0:64, 0, c], mx[0:64, 12, :]).then_inc(S.rw_wa, 1)
                bg.to('a')
                pe.wait_ge(S.rw_wa_taken, 2 * l + 1)
                four(lambda c: lora[64:128, 0, c], mx[64:128, 12, :]).then_inc(S.rw_wa, 1)
                bg.to('g')
                pe.wait_ge(S.rw_wa_taken, 2 * l + 2)
                four(lambda c: lora[:, 1, c], mx[:, 13, :]).then_inc(S.rw_g, 1)
                bg.to('v')
                pe.wait_ge(S.rw_g_taken, l + 1)
                if l:
                    four(lambda c: lora[64:96, 2, c], ptail[64:96, 2, 0:T]).then_inc(S.rw_v, 1)
                bg.to('kk')
                if l:
                    pe.wait_ge(S.rw_v_taken, l)
                pe.wait_ge(S.rw_kk_sq, l + 1)
                for b in range(4):
                    last = mm(ps[0:RW_HEADS, 4, 0:T], pair8(b), tmp[:, b, :], start=(b == 0), stop=(b == 3))
                last.then_inc(S.rw_kk_sum, 1)
                bg.to('kks')
                pe.wait_ge(S.rw_kk_inv, l + 1)
                for b in range(4):
                    last = mm(ps[:, 4 + b, 0:T], sel[:, AH + b, :], ln_s[0:RW_HEADS, :], start=True, stop=True)
                last.then_inc(S.rw_kk_spread, 1)
                bg.to('bonus')
                pe.wait_ge(S.rw_bonus_in, l + 1)
                for b in range(4):
                    last = mm(ps[:, 4 + b, 0:T], halves, tmp[:, b, :], start=True, stop=True)
                last.then_inc(S.rw_bonus_sum, 1)

                for c in range(NCH):
                    n = NCH * l + c
                    cs = slice(CH * c, CH * c + CH)
                    bg.to(f'tok{c}')
                    pe.wait_ge(S.rw_scaled, l + 1)
                    if c:
                        pe.wait_ge(S.rw_chunk_done, n)
                    for i, b0 in enumerate((8, 4, 18)):
                        for b in range(4):
                            last = tr(ps[:, 4 + i, 128 * b:128 * b + 128], mx[:, b0 + b, cs], ident)
                    last.then_inc(S.rw_turned, 1)
                    for q in range(2):
                        bg.to(f'more{c}' if q else f'pairs{c}')
                        if not q:
                            pe.wait_ge(S.rw_tok, n + 1)
                        for what, lhs0 in ((0, 18), (1, 4)):
                            if q:
                                pe.wait_ge(S.rw_pairs_taken, 4 * n + 1 + what)
                            for e in range(4):
                                h = 4 * q + e
                                r = slice(64 * (h % 2), 64 * (h % 2) + 64)
                                bank = 4 + 2 * what + e % 2
                                at_ = 256 * (e // 2)
                                mm(ps[:, bank, at_:at_ + 128], mx[r, lhs0 + h // 2, cs], mx[r, 14 + h // 2, cs],
                                   start=True, stop=True)
                                last = mm(ps[:, bank, at_ + 128:at_ + 256], mx[r, lhs0 + h // 2, cs], mx[r, h // 2, cs],
                                          start=True, stop=True)
                            last.then_inc(S.rw_pairs, 1)
                    bg.to(f'l{c}')
                    pe.wait_ge(S.rw_pairs_taken, 4 * n + 3)
                    for h in range(RW_HEADS):
                        r = slice(64 * (h % 2), 64 * (h % 2) + 64)
                        bank, hc = hb(h, 4, 128)
                        last = mm(ps[:, bank, hc], mx[r, 14 + h // 2, cs],
                                  mx[r, 18 + h // 2, cs], start=True, stop=True)
                    last.then_inc(S.rw_l, 1)
                    for lev in range(6):
                        bg.to(f'x{c}.{lev}')
                        for q in range(2):
                            m = 12 * n + 2 * lev + q
                            pe.wait_ge(S.rw_masked, m + 1)
                            for e in range(4):
                                h = 4 * q + e
                                last = mm(ps[:, 4 + q, 128 * e:128 * e + 128], lmk[:, h, :], ym[:, h, :], start=True, stop=True)
                            for e in range(4 if lev else 0):
                                last = tr(ps[:, 6 + q, 128 * e:128 * e + 128], ym[:, 4 * q + e, :], ident)
                            last.then_inc(S.rw_x, 1)
                        bg.to(f'y{c}.{lev}')
                        for q in range(2):
                            m = 12 * n + 2 * lev + q
                            pe.wait_ge(S.rw_x_kept, m + 1)
                            if not lev and not q:
                                pe.wait_ge(S.rw_t_first, n + 1)
                            for e in range(4):
                                h = 4 * q + e
                                last = mm(ps[:, 6 + q, 128 * e:128 * e + 128], tm[:, h, :], xm[:, h, :],
                                          start=True, stop=True)
                            last.then_inc(S.rw_tx, 1)
                    bg.to(f'w{c}')
                    pe.wait_ge(S.rw_inverted, 2 * n + 2)
                    for h in range(RW_HEADS):
                        r = slice(64 * (h % 2), 64 * (h % 2) + 64)
                        hc = slice(64 * h, 64 * h + 64)
                        bank, oc = hb(h, 6, 64)
                        last = mm(ps[:, bank, oc], mq[:, h, 0, :], tok[:, 0, hc], start=True, stop=(c == 0))
                        if c:
                            last = mm(ps[:, bank, oc], mx[r, 14 + h // 2, cs], zst[r, h // 2, :], start=False, stop=True)
                    last.then_inc(S.rw_w, 1)
                    bg.to(f'u{c}')
                    pe.wait_ge(S.rw_w_kept, n + 1)
                    for h in range(RW_HEADS):
                        hc = slice(64 * h, 64 * h + 64)
                        last = mm(ps[:, 4, hc], ym[:, h, :], wsb[:, hc], start=True, stop=True)
                    last.then_inc(S.rw_u, 1)
                    bg.to(f'out{c}')
                    pe.wait_ge(S.rw_u_kept, n + 1)
                    for h in range(RW_HEADS):
                        r = slice(64 * (h % 2), 64 * (h % 2) + 64)
                        hc = slice(64 * h, 64 * h + 64)
                        out = ps[r, 5 + 2 * (h % 2), 128 * (h // 2):128 * (h // 2) + 128]
                        if c:
                            mm(out, zst[r, h // 2, :], mx[r, h // 2, cs], start=True, stop=False)
                        mm(out, tok[:, 0, hc], mq[:, h, 1, :], start=(c == 0), stop=False)
                        mm(out, usb[:, hc], qb[:, h, :], start=False, stop=True)
                        out = ps[r, 6, 64 * (h // 2):64 * (h // 2) + 64]
                        mm(out, tok[:, 1, hc], tok[:, 0, hc], start=True, stop=False)
                        last = mm(out, tok[:, 2, hc], usb[:, hc], start=False, stop=True)
                    last.then_inc(S.rw_y, 1)
                for i, (src, name) in enumerate(((s1t, 'sa'), (s2t, 'sv'))):
                    bg.to(name)
                    pe.wait_ge(S.rw_sample_in, 2 * l + i + 1)
                    if i == 0:
                        pe.wait_ge(S.rw_chunk_done, NCH * (l + 1))
                    else:
                        pe.wait_ge(S.rw_sample_taken, l + 1)
                    for b in range(4):
                        last = mm(ps[:, 4 + b, :], halves, src[:, b, :, :].rearrange("p b v -> p (b v)"),
                                  start=True, stop=True)
                    last.then_inc(S.rw_sample_sum, 1)
                bg.to('sy')
                pe.wait_ge(S.rw_sample_new, l + 1)
                for h in range(RW_HEADS):
                    r = slice(64 * (h % 2), 64 * (h % 2) + 64)
                    for b in range(NS):
                        i = 8 * (h // 2) + b
                        last = mm(ps[r, 5 + 2 * (h % 2), i:i + 1], srw[r, h // 2, b, :], mx[r, h // 2, SEQ + b:SEQ + b + 1],
                                  start=True, stop=True)
                last.then_inc(S.rw_sample_y, 1)
                bg.to('gn')
                pe.wait_ge(S.rw_gn_in, 2 * l + 1)
                for b in range(4):
                    last = mm(ps[:, 4 + b, 0:T], halves, yt[:, b, :], start=True, stop=True)
                last.then_inc(S.rw_gn_sum, 1)
                bg.to('gnss')
                pe.wait_ge(S.rw_gn_in, 2 * l + 2)
                for b in range(4):
                    last = mm(ps[0:RW_HEADS, 4, 0:T], pair8(b), tmp[:, b, :], start=(b == 0), stop=(b == 3))
                last.then_inc(S.rw_gn_sum, 1)
                bg.to('gnsp')
                pe.wait_ge(S.rw_gn_inv, l + 1)
                for b in range(4):
                    last = mm(ps[:, 4 + b, 0:T], sel[:, AH + b, :], ln_s[0:RW_HEADS, :], start=True, stop=True)
                last.then_inc(S.rw_gn_spread, 1)
                bg.to('end')

                bg = Behind(slab0(l, 'in') + 64, group0(l, 'in') + 8, ret_plan, KB, xh, xl)
                bg.to('swap')
                pe.wait_ge(S.rw_done, l + 1)
                pe.wait_ge(S.ret_in, l + 1)
                for b in range(4):
                    last = mm(ps[:, 4 + b, 0:T], swap, pret[:, b, 0:T], start=True, stop=True)
                last.then_inc(S.ret_swapped, 1)
                bg.to('swap1')
                pe.wait_ge(S.ret_swap_taken, l + 1)
                for b in range(4, 6):
                    last = mm(ps[:, b, 0:T], swap, pret[:, b, 0:T], start=True, stop=True)
                last.then_inc(S.ret_swapped, 1)
                attention(l, False, 2 * l, bg)

                bg = Behind(slab0(l, 'out'), group0(l, 'out'), ml_plan, OUT_A // 2, oh, ol, done=2 * l + 1)
                bg.to('rows')
                pe.wait_ge(S.m_rows_c, l + 1)
                for c in range(NCH):
                    tr(ps[:, 7, 8 * c:8 * c + AH], rows[:, 0, CH * c:CH * c + CH], ident[0:AH, 0:AH])
                bg.to('spread_m')
                pe.wait_ge(S.m_rows_m, l + 1)
                for h in range(AH):
                    last = mm(ps[:, 4 + h // 2, SEQ * (h % 2):SEQ * (h % 2) + SEQ], sel[0:AH, h, :], rows[:, 3, 0:SEQ],
                              start=True, stop=True)
                last.then_inc(S.m_spread, 1)
                bg.to('spread_e')
                pe.wait_ge(S.m_exp_in, l + 1)
                pe.wait_ge(S.m_rows_e, l + 1)
                for p in range(AP_):
                    for i, row in enumerate((4, 1)):
                        mm(ps[:, 4 + p, SEQ * i:SEQ * i + SEQ], sel[0:AH, AH + p, :], rows[:, row, 0:SEQ], start=True, stop=True)
                        last = mm(ps[:, 7, 16 * p + 8 * i:16 * p + 8 * i + 8], sel[0:AH, AH + p, :], rows[:, row, SEQ:T],
                                  start=True, stop=True)
                last.then_inc(S.m_spread, 1)
                attention(l, True, 2 * l + 1, bg)
                pe.wait_ge(S.a_done, 2 * l + 2)

                for g in range(4):
                    s = slab0(l, 'out') + OUT_A + 3 * g
                    if g:
                        pe.wait_ge(S.evacuated, group0(l, 'out') + 3 + g)
                    for i in range(6):
                        kblock(s + i // 2, i % 2, 10 + i, 4 * ((g + 1) % 2), oh, ol, 10, KB - 1)
                norm_sums(2 * l + 1, l + 1 if l + 1 < DEPTH else None)
                groups(slab0(l, 'up'), group0(l, 'up'), FF_GROUPS, KB, xh, xl, T, ready=10 * l + 5)
                pe.wait_ge(S.hidden_ready, FF_GROUPS * (l + 1) - 1)
                groups(slab0(l, 'down'), group0(l, 'down'), 2, FB, hh, hl, T, hidden=FF_GROUPS * (l + 1))
                norm_sums(2 * l + 2)

            pe.wait_ge(S.x_ready, 10 * DEPTH + 5)
            to_rows(lambda b: R[:, b, 0:128], KB, 128, 0, S.y_turned)
            to_rows(lambda b: R[:, b, 128:256], KB, 128, 4, S.y_turned)
            pe.wait_ge(S.y_rows, 1)
            to_rows(lambda b: R[:, b, SEQ:T], KB, NS, 0, S.y_turned)

        @block.scalar
        def _(act):
            own = Own(act, S.act_steps)
            A = nc.scalar.activation

            def hi4(s0, pieces=None):
                for j in range(RING):
                    act.wait_ge(raw_loaded[j], s0 * 4 + 16)
                    if pieces:
                        act.wait_ge(tail_loaded[j], pieces)
                    if not (isinstance(s0, int) and s0 < RING):
                        act.wait_ge(S.slab_used, s0 + (j - RING + 1))
                    A(wh[:, j, :, :], raw[:, j, :, :], ACT.Copy).then_inc(S.hi_ready, 1)

            def his(s0, n):
                with act.Fori(0, n // RING) as it:
                    hi4(it * RING + s0)

            def hi1(s):
                act.wait_ge(raw_loaded[s % RING], 16 * (s // RING + 1))
                act.wait_ge(S.slab_used, s - RING + 1)
                A(wh[:, s % RING, :, :], raw[:, s % RING, :, :], ACT.Copy).then_inc(S.hi_ready, 1)

            def behind(l, first, dst, d0, plan_):
                base_ = slab0(l, 'in') + 8 * first

                def one(i):
                    if i % 8 == 7:
                        act.wait_ge(S.slab_used, base_ + i + 1)
                        if first == 4 and i == 7:
                            act.wait_ge(S.shift_stored, 32 * (l + 1))
                        b = 4 * (i // 8) + d0
                        A(dst[:, b:b + 4, 0:T], ps[:, 0:4, 0:T], ACT.Copy).then_inc(S.evacuated, 1)
                    hi1(base_ + RING + i)
                return Parts(plan_, one)

            def tail_pieces(l, turn):
                return 16 * (turn + 1) if l == 0 else 32 + 64 * (l - 1) + 32 * (turn + 1)

            act.dma_start(base[:, :, :].rearrange("p a b -> p (a b)"), a['c_base']).then_inc(S.x_loaded, 16)
            xp = a['x_prompt'][0].rearrange("(t p) d -> p t d", p=128)
            act.dma_start(x_tok[:, 0:2, 0:D // 2], xp[:, :, 0:D // 2]).then_inc(S.x_loaded, 16)
            act.dma_start(x_tok[0:NS, 2, :], a['x_sample'][:, 0, :]).then_inc(S.x_loaded, 16)
            act.dma_start(x_tok[:, 0:2, D // 2:D], xp[:, :, D // 2:D]).then_inc(S.start_loaded, 16)
            act.dma_start(prm0_tok[0:16, :], a['ln0_g'].rearrange("(b c) -> b c", c=128)).then_inc(S.start_loaded, 16)
            act.dma_start(prm0_tok[16:32, :], a['ln0_b'].rearrange("(b c) -> b c", c=128)).then_inc(S.start_loaded, 16)
            act.dma_start(ident2[:, :], a['c_ident2']).then_inc(S.tables_loaded, 16)
            act.dma_start(masks[:, :, :].rearrange("p a b -> p (a b)"), a['c_masks']).then_inc(S.tables_loaded, 16)
            act.dma_start(gam[:, :], a['c_gam']).then_inc(S.tables_loaded, 16)
            act.dma_start(sel[:, :, :].rearrange("p a b -> p (a b)"), a['c_sel']).then_inc(S.tables_loaded, 16)
            act.dma_start(sums[:, :], a['c_sums']).then_inc(S.tables_loaded, 16)

            def hi_tail(l, i):
                act.wait_ge(tail_loaded[i % RING], tail_pieces(l, i // RING))
                hi1(slab0(l, 'tail') + i)

            def norm_parts(n, gam_, bet_, last=False, ahead=None):
                for q in range(4):
                    qs_, Rq = slice(4 * q, 4 * q + 4), quarter(n, q)
                    act.wait_ge(S.ln_centered, 4 * n + q + 1)
                    A(SQ[:, qs_, :], Rq, ACT.Square).then_inc(S.ln_squared, 1)
                act.wait_ge(S.ln_sumsq_all, n + 1)
                A(ln_m[:, :], ps[:, 1, 0:T], ACT.Sqrt, bias=eps[:, 0:1], scale=1.0 / D).then_inc(S.ln_std, 1)
                for i, (b0, b1) in enumerate(PIECES):
                    act.wait_ge(S.ln_scaled, 5 * n + i + 1)
                    Rp = piece(n, i)
                    for b in range(b1 - b0):
                        ins = A(Rp[:, b, :], Rp[:, b, :], ACT.Identity, scale=gam_(b0 + b), bias=bet_(b0 + b))
                    if last:
                        ins.then_inc(S.x_ready, 1)
                    else:
                        own(ins)
                        A(xh[:, b0:b1, 0:T], Rp, ACT.Copy).then_inc(S.x_hi_ready, 1)
                    if ahead is not None and i == 3:
                        hi_tail(ahead, RING)
                        hi_tail(ahead, RING + 1)

            def early_loads(l):
                for name, n in PRM:
                    if name == 'rw_v0' and l == 0:
                        continue
                    src = a[name][l - 1 if name == 'rw_v0' else l].rearrange("(b c) -> b c", c=128)
                    act.dma_start(prm_tok[PRM_AT[name]:PRM_AT[name] + n, :], src).then_inc(S.prm_loaded, 16)
                act.dma_start(shift_tok[:, :], a['state_rw_shift'][l]).then_inc(S.shift_loaded, 16)

            def layer_loads(l):
                act.wait_ge(S.x_ready, 10 * l + 5)
                act.dma_start(mlb[:, 0:1], a['ml_ib'][l].rearrange("(h a) -> h a", a=1)).then_inc(S.mlb_loaded, 16)
                act.dma_start(mlb[:, 1:2], a['ml_fb'][l].rearrange("(h a) -> h a", a=1)).then_inc(S.mlb_loaded, 16)
                act.dma_start(lora[0:64, 0, :], a['rw_w2'][l]).then_inc(S.lora_loaded, 16)
                act.dma_start(lora[64:128, 0, :], a['rw_a2'][l]).then_inc(S.lora_loaded, 16)
                act.dma_start(lora[:, 1, :], a['rw_g2'][l]).then_inc(S.lora_loaded, 16)
                if l:
                    act.dma_start(lora[64:96, 2, :], a['rw_v2'][l - 1]).then_inc(S.lora_loaded, 16)
                    act.dma_start(vmu[64:96, :], a['rw_vmu'][l - 1].rearrange("(h a) -> h a", a=1)).then_inc(S.lora_loaded, 16)

            def attention(l, ml, n, bg):
                for c in range(NCH):
                    bg.to(f'turn{c}')
                    act.wait_ge(S.a_turned, 2 * n + c + 1)
                    A(ktok[:, c, :], ps[:, 4, 0:384], ACT.Copy)
                    A(vtok[:, c, 0:512], ps[:, 5, :], ACT.Copy)
                    A(vtok[:, c, 512:768], ps[:, 6, 0:256], ACT.Copy).then_inc(S.a_tok, 1)
                for name in ('score', 'num0', 'num1', 'vt'):
                    bg.to(name)
                act.wait_ge(S.a_kv_turned, n + 1)
                A(kst[:, :, :].rearrange("p a k -> p (a k)"), ps[0:AH * NS, 4, 0:128 * AP_], ACT.Copy).then_inc(S.a_kv_ready, 1)
                for name in tuple(f'v{p}' for p in range(AP_)) + ('sy', 'sumsq'):
                    bg.to(name)
                act.wait_ge(S.a_y_ready, n + 1)
                if ml:
                    A(sq[:, :, :], ay[:, :, :], ACT.Square).then_inc(S.a_squares, 1)
                    own(A(mdn[:, :], ps[0:AH, 6, 0:T], ACT.Abs))
                    act.sem_inc(S.m_absden, 1)
                    act.wait_ge(S.m_guarded, l + 1)
                    A(mdn[:, :], mdn[:, :], ACT.Square, scale=float(np.sqrt(NORM_EPS))).then_inc(S.m_eps, 1)
                    act.wait_ge(S.m_var, l + 1)
                    A(ln_s[0:AH, :], mdn[:, :], ACT.Sqrt).then_inc(S.a_std, 1)
                else:
                    A(sq[:, :, :], ay[:, :, :], ACT.Square).then_inc(S.a_squares, 1)
                    act.wait_ge(S.a_sumsq, n + 1)
                    A(ln_s[0:AH, :], ps[0:AH, 7, 0:T], ACT.Sqrt, bias=eps[0:AH, 1:2], scale=1.0 / AV).then_inc(S.a_std, 1)
                if ml:
                    A(mgate[:, 0:4, :], pml[:, 12:16, 0:T], ACT.Sigmoid)
                    A(mgate[:, 4:6, :], ptail[:, 0:2, 0:T], ACT.Sigmoid).then_inc(S.a_gate, 1)
                else:
                    A(rtmp[:, :, :], pret[:, 12:18, 0:T], ACT.Sigmoid).then_inc(S.a_gate, 1)
                bg.to('spread')
                bg.to('spread1')
                a0 = 10 if ml else 4
                act.wait_ge(S.a_out, n + 1)
                A(oh[:, a0:a0 + AH, :], ay[:, :, :], ACT.Copy).then_inc(S.a_out_hi, 1)
                bg.to('end')

            early_loads(0)
            for q in (1, 3):
                act.wait_ge(S.x_turned, q + 1)
                A(R[:, 4 * q:4 * q + 4, :], ps[:, 4:8, 0:T], ACT.Copy).then_inc(S.x_taken_odd, 1)
            hi4(0, tail_pieces(0, 0))
            norm_parts(0, lambda b: prm0[:, b:b + 1], lambda b: prm0[:, 16 + b:17 + b], ahead=0)
            for l in range(DEPTH):
                hi_tail(l, RING + 2)
                hi_tail(l, RING + 3)
                layer_loads(l)
                his(slab0(l, 'in'), 36)
                act.wait_ge(S.shift_turned, l + 1)
                A(shift_out[:, :].rearrange("p (a b) -> p a b", a=4), ps[0:1 + NS, 4:8, :], ACT.Copy).then_inc(S.shift_rows, 1)
                act.wait_ge(S.shift_rows, l + 1)
                act.dma_start(o['p_shift'][l], shift_out[0:1, :]).then_inc(S.shift_stored, 16)
                act.dma_start(o['s_shift'][l], shift_out[1:1 + NS, :]).then_inc(S.shift_stored, 16)

                bg = behind(l, 4, pret, 2, rw_plan)
                bg.to('in')
                act.wait_ge(S.rw_mix, l + 1)
                A(mx[0:64, 12, :], mx[0:64, 12, :], ACT.Tanh)
                A(mx[:, 13, :], mx[:, 13, :], ACT.Sigmoid).then_inc(S.rw_in, 1)
                act.wait_ge(S.rw_wa, 2 * l + 1)
                for b in range(4):
                    last = A(lw[:, b, :], ps[:, 4 + b, 0:T], ACT.Sigmoid, bias=col(l, 'rw_w0', b))
                last.then_inc(S.rw_wa_taken, 1)
                bg.to('a')
                act.wait_ge(S.rw_wa, 2 * l + 2)
                for b in range(4):
                    last = A(mx[:, 18 + b, :], ps[:, 4 + b, 0:T], ACT.Sigmoid, bias=col(l, 'rw_a0', b))
                last.then_inc(S.rw_wa_taken, 1)
                bg.to('g')
                act.wait_ge(S.rw_g, l + 1)
                A(gate[:, :, :], ps[:, 4:8, 0:T], ACT.Copy).then_inc(S.rw_g_taken, 1)
                if l == 0:
                    A(vfirst[:, :, :], mx[:, 8:12, :], ACT.Copy).then_inc(S.rw_v_first, 1)
                if l:
                    bg.to('v')
                    act.wait_ge(S.rw_v, l)
                    for b in range(4):
                        last = A(tmp[:, b, :], ps[:, 4 + b, 0:T], ACT.Sigmoid, bias=col(l, 'rw_v0', b))
                    last.then_inc(S.rw_v_taken, 1)
                bg.to('kk')
                act.wait_ge(S.rw_kk_raw, l + 1)
                if l:
                    act.wait_ge(S.rw_v_used, l)
                A(tmp[:, :, :], mx[:, 14:18, :], ACT.Square).then_inc(S.rw_kk_sq, 1)
                bg.to('kks')
                act.wait_ge(S.rw_kk_ss, l + 1)
                A(ln_s[0:RW_HEADS, :], ln_m[0:RW_HEADS, :], ACT.Sqrt).then_inc(S.rw_kk_norm, 1)
                for b in range(4):
                    last = A(tmp[:, b, :], mx[:, 18 + b, :], ACT.Identity, scale=col(l, 'rw_ka', b), bias=ka1[:, b:b + 1])
                last.then_inc(S.rw_ka_done, 1)
                bg.to('bonus')
                act.wait_ge(S.rw_cum, l + 1)
                for b in range(4):
                    for c in range(NCH):
                        cs = slice(CH * c, CH * c + CH)
                        A(ep[:, b, cs], lw[:, b, cs], ACT.Exp, bias=namid[:, b, c:c + 1], scale=-DECAY)
                        A(em[:, b, cs], lw[:, b, cs], ACT.Exp, bias=amid[:, b, c:c + 1], scale=DECAY)
                A(wsam[:, :, :], lw[:, :, SEQ:T], ACT.Exp, scale=-DECAY)
                A(eamid[:, :, :], amid[:, :, :], ACT.Exp)
                A(enam[:, :, :], namid[:, :, :], ACT.Exp).then_inc(S.rw_exps, 1)
                for c in range(NCH):
                    n = NCH * l + c
                    bg.to(f'tok{c}')
                    act.wait_ge(S.rw_turned, n + 1)
                    A(tok[:, :, :], ps[:, 4:7, :], ACT.Copy).then_inc(S.rw_tok, 1)
                    for name in ('pairs', 'more', 'l'):
                        bg.to(f'{name}{c}')
                    act.wait_ge(S.rw_l, n + 1)
                    A(pairs(lm[:, :, :]), halves_of(4, CH, RW_HEADS), ACT.Copy).then_inc(S.rw_l_kept, 1)
                    for lev in range(6):
                        bg.to(f'x{c}.{lev}')
                        for q in range(2):
                            m = 12 * n + 2 * lev + q
                            hs = slice(4 * q, 4 * q + 4)
                            act.wait_ge(S.rw_x, m + 1)
                            last = A(xm[:, hs, :], ps[:, 4 + q, :].rearrange("p (h i) -> p h i", i=CH), ACT.Copy)
                            if lev:
                                last = A(tm[:, hs, :], ps[:, 6 + q, :].rearrange("p (h i) -> p h i", i=CH), ACT.Copy)
                            last.then_inc(S.rw_x_kept, 1)
                        bg.to(f'y{c}.{lev}')
                    bg.to(f'w{c}')
                    act.wait_ge(S.rw_w, n + 1)
                    A(pairs(wsb[:, :].rearrange("p (h v) -> p h v", v=64)), halves_of(6, 64, RW_HEADS), ACT.Copy).then_inc(S.rw_w_kept, 1)
                    bg.to(f'u{c}')
                    act.wait_ge(S.rw_u, n + 1)
                    A(usb[:, :], ps[:, 4, :], ACT.Copy, scale=-1.0).then_inc(S.rw_u_kept, 1)
                    bg.to(f'out{c}')
                    if c == 0:
                        si = a['state_rw_wkv'][l].rearrange("b (p e) k v -> p (e k) b v", e=2)
                        so = o['s_wkv'][l].rearrange("b (p e) k v -> p (e k) b v", e=2)
                        for p in range(4):
                            act.dma_start(srw[:, p, :, :], si[p]).then_inc(S.rw_sample_loaded, 16)
                bg.to('sa')
                act.wait_ge(S.rw_chunk_done, NCH * (l + 1))
                act.dma_start(o['p_wkv'][l, 0].rearrange("(p e) k v -> (e k) p v", e=2), zst[:, :, :]).then_inc(S.rw_stored, 16)
                for name in ('sv', 'sy'):
                    bg.to(name)
                act.wait_ge(S.rw_sample_new, l + 1)
                for p in range(4):
                    act.dma_start(so[p], srw[:, p, :, :]).then_inc(S.rw_stored, 16)
                for name in ('gn', 'gnss'):
                    bg.to(name)
                act.wait_ge(S.rw_gn_c, l + 1)
                A(tmp[:, :, :], yt[:, :, :], ACT.Square).then_inc(S.rw_gn_in, 1)
                act.wait_ge(S.rw_gn_sum, 2 * l + 2)
                A(ln_s[0:RW_HEADS, :], ps[0:RW_HEADS, 4, 0:T], ACT.Sqrt, bias=eps[0:RW_HEADS, 2:3],
                  scale=1.0 / RW_HD).then_inc(S.rw_gn_std, 1)
                bg.to('gnsp')
                act.wait_ge(S.rw_out, l + 1)
                A(oh[:, 0:4, :], yt[:, :, :], ACT.Copy).then_inc(S.rw_out_hi, 1)
                bg.to('end')

                act.wait_ge(S.rw_done, l + 1)
                act.wait_ge(S.rw_stored, 80 * (l + 1))
                act.dma_start(rdec[:, :, :].rearrange("p a b -> p (a b)"), a['c_ret']).then_inc(S.rdec_loaded, 16)
                act.dma_start(rrot[:, :, :].rearrange("p a b -> p (a b)"), a['c_rot']).then_inc(S.rdec_loaded, 16)
                si = a['state_ret'][l].rearrange("b (p e) k v -> p (e k) b v", e=2)
                so = o['s_ret'][l].rearrange("b (p e) k v -> p (e k) b v", e=2)
                for p in range(AP_):
                    act.dma_start(rsam[:, p, :, :], si[p]).then_inc(S.a_sample_loaded, 16)
                bg = behind(l, 8, pml, 0, ret_plan)
                for name in ('swap', 'swap1', 'turn0'):
                    bg.to(name)
                attention(l, False, 2 * l, bg)
                act.dma_start(o['p_ret'][l, 0].rearrange("(p e) k v -> (e k) p v", e=2), st[:, 1, :, :]).then_inc(S.ret_stored, 16)
                for p in range(AP_):
                    act.dma_start(so[p], rsam[:, p, :, :]).then_inc(S.ret_stored, 16)

                act.wait_ge(S.a_done, 2 * l + 1)
                si = a['state_ml_c'][l].rearrange("b (p e) k v -> p (e k) b v", e=2)
                so = o['s_mlc'][l].rearrange("b (p e) k v -> p (e k) b v", e=2)
                ni = a['state_ml_n'][l].rearrange("b (p e) k -> p (e k) b", e=2)
                no = o['s_mln'][l].rearrange("b (p e) k -> p (e k) b", e=2)
                for p in range(AP_):
                    act.dma_start(msam[:, p, :, :], si[p]).then_inc(S.a_sample_loaded, 16)
                    act.dma_start(msn[:, p, :], ni[p], allow_slow_non_contiguous=True).then_inc(S.m_n_loaded, 16)
                act.dma_start(rows[:, 4, SEQ:T], a['state_ml_m'][l].rearrange("b h -> h b"), allow_slow_non_contiguous=True).then_inc(S.m_m_loaded, 16)
                bg = Parts(ml_plan, lambda i: hi1(slab0(l, 'out') + RING + i))
                bg.to('rows')
                act.wait_ge(S.m_gates_in, l + 1)
                own(A(rows[:, 0, :], rows[:, 0, :], ACT.Tanh, bias=mlb2[:, 0:1], scale=1.0 / CAP))
                own(A(rows[:, 1, :], rows[:, 1, :], ACT.Tanh, bias=mlb2[:, 1:2], scale=1.0 / CAP))
                own(A(rows[:, 1, :], rows[:, 1, :], ACT.Sigmoid, scale=CAP))
                A(rows[:, 1, :], rows[:, 1, :], ACT.Ln).then_inc(S.m_logf, 1)
                bg.to('spread_m')
                bg.to('spread_e')
                act.wait_ge(S.m_rows_x, l + 1)
                A(rows[:, 1, :], rows[:, 1, :], ACT.Exp)
                A(rows[:, 4, :], rows[:, 4, :], ACT.Exp)
                A(men[:, :], rows[:, 2, :], ACT.Exp, scale=-1.0).then_inc(S.m_rows_e, 1)
                act.wait_ge(S.m_exp_in, l + 1)
                for h in range(AH):
                    for c in range(NCH):
                        last = A(ssb[:, c, h, :], ssb[:, c, h, :], ACT.Exp, bias=mct[:, c, h:h + 1])
                last.then_inc(S.m_exp, 1)
                attention(l, True, 2 * l + 1, bg)
                act.dma_start(o['p_mlc'][l, 0].rearrange("(p e) k v -> (e k) p v", e=2), st[:, 1, :, :]).then_inc(S.ml_stored, 16)
                act.dma_start(o['p_mln'][l, 0].rearrange("(p e) k -> (e k) p", e=2), mnc[:, 1, :], allow_slow_non_contiguous=True).then_inc(S.ml_stored, 16)
                act.dma_start(o['p_mlm'][l, 0].rearrange("(h a) -> h a", a=1), mfin[:, NS:NS + 1]).then_inc(S.ml_stored, 16)
                act.dma_start(o['s_mlm'][l].rearrange("b h -> h b"), mfin[:, 0:NS], allow_slow_non_contiguous=True).then_inc(S.ml_stored, 16)
                for p in range(AP_):
                    act.dma_start(so[p], msam[:, p, :, :]).then_inc(S.ml_stored, 16)
                    act.dma_start(no[p], msn[:, p, :], allow_slow_non_contiguous=True).then_inc(S.ml_stored, 16)

                his(slab0(l, 'out') + OUT_A + 4, 4)
                act.wait_ge(S.a_done, 2 * l + 2)
                act.wait_ge(S.ml_stored, 160 * (l + 1))
                if l + 1 < DEPTH:
                    early_loads(l + 1)
                his(slab0(l, 'out') + OUT_A + 8, 8)
                norm_parts(2 * l + 1, lambda b: col(l, 'ln1_g', b), lambda b: col(l, 'ln1_b', b))
                with act.Fori(0, FF_GROUPS) as it:
                    s = it * 16 + (slab0(l, 'up') + 4)
                    hi4(s)
                    hi4(s + 4)
                    act.wait_ge(S.slab_used, s + 4)
                    act.wait_ge(S.gated, it + (l * FF_GROUPS + 1))
                    A(sg[:, :, :], ps[:, 0:4, 0:T], ACT.Sigmoid).then_inc(S.gate_sig, 1)
                    hi4(s + 8)
                    hi4(s + 12)
                his(slab0(l, 'down') + 4, 4 * DOWN_SLABS - RING)
                if l + 1 < DEPTH:
                    hi4(slab0(l + 1, 'tail'), tail_pieces(l + 1, 0))
                norm_parts(2 * l + 2, lambda b: col(l, 'ln2_g', b), lambda b: col(l, 'ln2_b', b), last=l + 1 == DEPTH,
                           ahead=l + 1 if l + 1 < DEPTH else None)
            for t in range(2):
                act.wait_ge(S.y_turned, t + 1)
                A(y_tok[:, t, :].rearrange("p (a b) -> p a b", a=4), ps[:, 4 * t:4 * t + 4, :], ACT.Copy).then_inc(S.y_rows, 1)
            act.wait_ge(S.y_turned, 3)
            A(y_tok[0:NS, 2, :].rearrange("p (a b) -> p a b", a=4), ps[0:NS, 0:4, :], ACT.Copy).then_inc(S.y_rows, 1)

        @block.vector
        def _(dve):
            v = nc.vector
            own = Own(dve, S.dve_steps)
            TT, TS, STT = v.tensor_tensor, v.tensor_scalar, v.scalar_tensor_tensor
            own(v.memset(eps[:, 0:1], LN_EPS))
            own(v.memset(eps[:, 1:2], NORM_EPS))
            own(v.memset(eps[:, 2:3], GN_EPS))
            dve.sem_inc(S.evacuated, 1)
            dve.sem_inc(S.gated, 1)
            v.memset(raw[:, :, :, :], 0.0).then_inc(S.raw_cleared, 1)

            def lo4(s0, slots=range(RING)):
                for j in slots:
                    dve.wait_ge(S.hi_ready, s0 + (j + 1))
                    TT(wl[:, j, :, :], raw[:, j, :, :], wh[:, j, :, :].bitcast(F32), ALU.subtract).then_inc(S.lo_ready, 1)

            def evacuate(used, what):
                dve.wait_ge(S.slab_used, used)
                what().then_inc(S.evacuated, 1)

            def lo1(s):
                dve.wait_ge(S.hi_ready, s + 1)
                TT(wl[:, s % RING, :, :], raw[:, s % RING, :, :], wh[:, s % RING, :, :].bitcast(F32),
                   ALU.subtract).then_inc(S.lo_ready, 1)

            def out_part(l, i):
                s0, g0 = slab0(l, 'out'), group0(l, 'out')
                if i < OUT_A and i % 5 == 4:
                    q = i // 5
                    dve.wait_ge(S.slab_used, s0 + i + 1)
                    qs_ = slice(4 * q, 4 * q + 4)
                    STT(R1[q][:, :, :], xh[:, qs_, 0:T].bitcast(F32), ALPHA, ps[:, 0:4, 0:T],
                        ALU.mult, ALU.add).then_inc(S.evacuated, 1)
                    dve.wait_ge(S.evacuated, g0 + q + 1)
                    own(STT(R1[q][:, :, :], xl[:, qs_, 0:T].bitcast(F32), ALPHA, R1[q][:, :, :], ALU.mult, ALU.add))
                if i >= OUT_A and (i - OUT_A) % 3 == 2:
                    q = (i - OUT_A) // 3
                    dve.wait_ge(S.slab_used, s0 + i + 1)
                    b0 = 4 * ((q + 1) % 2)
                    TT(R1[q][:, :, :], R1[q][:, :, :], ps[:, b0:b0 + 4, 0:T], ALU.add).then_inc(S.evacuated, 1)
                    dve.wait_ge(S.evacuated, g0 + 4 + q + 1)
                    if q == 1:
                        own(TT(gu[:, :, :], R1[0][:, :, :], R1[1][:, :, :], ALU.add))
                    if q > 1:
                        own(TT(gu[:, :, :], gu[:, :, :], R1[q][:, :, :], ALU.add))
                lo1(s0 + RING + i)

            def behind(l, first, plan_):
                return Parts(plan_, lambda i: lo1(slab0(l, 'in') + 8 * first + RING + i))

            def residual_x(blk, count):
                Rb = R[:, ds(blk, 4), :]
                TS(Rb, xh[:, ds(blk, 4), 0:T].bitcast(F32), ALPHA, None, ALU.mult).then_inc(S.resid_part, 1)
                dve.wait_ge(S.resid_part, count * 2 + 1)
                STT(Rb, xl[:, ds(blk, 4), 0:T].bitcast(F32), ALPHA, Rb, ALU.mult, ALU.add).then_inc(S.resid_part, 1)
                dve.wait_ge(S.resid_part, count * 2 + 2)

            def residual_group(used, blk, set_, count, g):
                Rb = R[:, ds(blk, 4), :]
                dve.wait_ge(S.slab_used, used)
                TT(Rb, Rb, ps[:, set_:set_ + 4, 0:T], ALU.add).then_inc(S.evacuated, 1)
                dve.wait_ge(S.evacuated, g)
                TT(gu[:, :, :], gu[:, :, :], R[:, ds(blk, 4), :], ALU.add).then_inc(S.resid_sum, 1)
                dve.wait_ge(S.resid_sum, count + 1)

            def norm(n, nxt=None, last=False, first=None, ahead=None):
                v.tensor_reduce(ln_s[:, :], gu[:, :, :].rearrange("p b t -> p t b"), AX.X, ALU.add).then_inc(S.ln_sum, 1)
                dve.wait_ge(S.ln_sum_all, n + 1)
                own(TS(ln_m[:, :], ps[:, 0, 0:T], 1.0 / D, None, ALU.mult))
                for q in range(4):
                    Rq = quarter(n, q)
                    TT(Rq, Rq, each(ln_m[:, :], 4), ALU.subtract).then_inc(S.ln_centered, 1)
                if first is not None:
                    lo4(first)
                if nxt is not None:
                    dve.wait_ge(S.layer_turned, nxt + 1)
                    npr = PRM_ROWS if nxt else PRM_ROWS - 4
                    own(v.tensor_copy(prm2[:, nxt % 2, 0:npr], ps[:, 2, 0:npr]))
                    sh = ps[:, 3, 0:128].rearrange("p (b s) -> p b s", s=NS)
                    own(v.tensor_copy(xh[:, :, T:TW], sh))
                    TT(xl[:, :, T:TW], sh, xh[:, :, T:TW].bitcast(F32), ALU.subtract).then_inc(S.layer_taken, 1)
                dve.wait_ge(S.ln_std, n + 1)
                own(v.reciprocal(ln_m[:, :], ln_m[:, :]))
                dve.wait_ge(S.ln_centered, 4 * n + 4)

                def scale(i):
                    Rp = piece(n, i)
                    TT(Rp, Rp, each(ln_m[:, :], Rp.shape[1]), ALU.mult).then_inc(S.ln_scaled, 1)

                def low(i):
                    b0, b1 = PIECES[i]
                    dve.wait_ge(S.x_hi_ready, 5 * n + i + 1)
                    TT(xl[:, b0:b1, 0:T], piece(n, i), xh[:, b0:b1, 0:T].bitcast(F32), ALU.subtract).then_inc(S.x_ready, 1)
                for i in range(3):
                    scale(i)
                for i in range(5):
                    if not last:
                        low(i)
                    if i < 2:
                        scale(i + 3)
                    if ahead is not None and i == 3:
                        lo1(ahead)
                        lo1(ahead + 1)

            def attention(l, ml, n, bg):
                def then(ins):
                    own(ins)
                    bg.step()
                src = pml if ml else pret
                bg.to('turn0')
                bg.to('turn1')
                bg.to('score')
                for c in range(NCH):
                    dve.wait_ge(S.a_scored, 2 * n + c + 1)
                    if ml:
                        dve.wait_ge(S.m_exp, l + 1)
                    w = ssb[:, c, :, :] if ml else rdec[:, 0:AH, :]
                    TT(pairs(ssb[:, c, :, :]), halves_of(4 + 2 * c, CH, AH), pairs(w), ALU.mult).then_inc(S.a_weighted, 1)
                for c in range(NCH):
                    bg.to(f'num{c}')
                    dve.wait_ge(S.a_summed, 2 * n + c + 1)
                    if c == 0:
                        then(v.tensor_copy(st[:, 0, :, :], ps[:, 7, 0:384].rearrange("p (a b) -> p a b", a=AP_)))
                    else:
                        for p in range(AP_):
                            sc = mdc[:, p:p + 1] if ml else gam[:, AP_ + p:AP_ + p + 1]
                            then(STT(st[:, 1, p, :], st[:, 0, p, :], sc, ps[:, 7, 128 * p:128 * p + 128], ALU.mult, ALU.add))
                    dve.sem_inc(S.a_state_kept, 1)
                    y = v.tensor_copy(pairs(ay[:, :, CH * c:CH * c + CH]), halves_of(4, CH, AH))
                    y.then_inc(S.a_y_kept, 1)
                dve.wait_ge(S.a_y_kept, 2 * n + 2)
                dve.wait_ge(S.a_sample_loaded, 48 * (n + 1))
                sam = msam if ml else rsam
                k = kw[:, :, SEQ:T] if ml else src[:, AP_:2 * AP_, SEQ:T]
                by_head = sums[:, AH * AH:AH * AH + AP_ * AH].rearrange("p (a h) -> p a h", h=AH)
                own(TT(kvs[:, 0:AP_, :].rearrange("p a (h b) -> p a h b", b=NS),
                       by_head.unsqueeze(3).to_broadcast([128, AP_, AH, NS]),
                       k.unsqueeze(2).to_broadcast([128, AP_, AH, NS]), ALU.mult))
                v.tensor_copy(kvs[:, AP_, :].rearrange("p (h b) -> p h b", b=NS),
                              src[:, 2 * AP_:2 * AP_ + AH, SEQ:T]).then_inc(S.a_kv_sample, 1)
                if ml:
                    for p in range(AP_):
                        then(TT(sam[:, p, :, :], sam[:, p, :, :], over(msk[:, p, :], 128), ALU.mult))
                bg.to('vt')
                dve.wait_ge(S.a_kv_turned, n + 1)
                TT(vst[:, :, :], each(ps[0:AH * NS, 5, 0:128], NS), over(same, 128),
                   ALU.mult).then_inc(S.a_kv_ready, 1)
                for p in range(AP_):
                    bg.to(f'v{p}')
                    dve.wait_ge(S.a_vspread, n * AP_ + p + 1)
                    b0 = 4 if ml or p != 1 else 6
                    kv = ps[:, b0:b0 + 2, :].rearrange("p a (b v) -> p (a b) v", v=128)
                    if ml:
                        TT(sam[:, p, :, :], sam[:, p, :, :], kv, ALU.add).then_inc(S.a_pair_done, 1)
                    else:
                        STT(sam[:, p, :, :], sam[:, p, :, :], gam[:, p:p + 1], kv, ALU.mult, ALU.add).then_inc(S.a_pair_done, 1)
                    dve.wait_ge(S.a_pair_done, n * AP_ + p + 1)
                if ml:
                    dve.wait_ge(S.m_n_loaded, 48 * (l + 1))
                    then(TT(msn[:, :, :], msn[:, :, :], msk[:, :, :], ALU.mult))
                    then(TT(msn[:, :, :], msn[:, :, :], kw[:, :, SEQ:T], ALU.add))
                    TT(mpd[:, :, :], msn[:, :, :], src[:, 0:AP_, SEQ:T], ALU.mult).then_inc(S.m_nprod, 1)
                bg.to('sy')
                dve.wait_ge(S.a_sample_y, n + 1)
                y = v.tensor_copy(pairs(ay[:, :, SEQ:T]), halves_of(4, NS, AH))
                y.then_inc(S.a_y_ready, 1)
                if ml:
                    dve.wait_ge(S.m_absden, l + 1)
                    TT(mdn[:, :], mdn[:, :], men[:, :], ALU.max).then_inc(S.m_guarded, 1)
                    dve.wait_ge(S.m_eps, l + 1)
                    dve.wait_ge(S.a_sumsq, n + 1)
                    then(STT(mdn[:, :], ps[0:AH, 7, 0:T], 1.0 / AV, mdn[:, :], ALU.mult, ALU.add))
                    TS(mdn[:, :], mdn[:, :], 1e-36, None, ALU.max).then_inc(S.m_var, 1)
                bg.to('sumsq')
                dve.wait_ge(S.a_std, n + 1)
                v.reciprocal(ln_s[0:AH, :], ln_s[0:AH, :]).then_inc(S.a_inv, 1)
                bg.to('spread')
                dve.wait_ge(S.a_spread, 2 * n + 1)
                TT(ay[:, 0:4, :], ay[:, 0:4, :], ps[:, 4:8, 0:T], ALU.mult).then_inc(S.a_normed, 1)
                bg.to('spread1')
                dve.wait_ge(S.a_spread, 2 * n + 2)
                own(TT(ay[:, 4:6, :], ay[:, 4:6, :], ps[:, 4:6, 0:T], ALU.mult))
                dve.wait_ge(S.a_normed, n + 1)
                dve.wait_ge(S.a_gate, n + 1)
                if ml:
                    own(TT(ay[:, :, :], ay[:, :, :], over(cols(l, 'ml_norm', AH), T), ALU.mult))
                    TT(ay[:, :, :], ay[:, :, :], mgate[:, :, :], ALU.mult).then_inc(S.a_out, 1)
                else:
                    own(TT(ay[:, :, :], ay[:, :, :], rtmp[:, :, :], ALU.mult))
                    TT(ay[:, :, :], ay[:, :, :], pret[:, 12:18, 0:T], ALU.mult).then_inc(S.a_out, 1)
                a0 = 10 if ml else 4
                dve.wait_ge(S.a_out_hi, n + 1)
                TT(ol[:, a0:a0 + AH, :], ay[:, :, :], oh[:, a0:a0 + AH, :].bitcast(F32), ALU.subtract).then_inc(S.a_done, 1)
                bg.to('end')

            for q in (0, 2):
                dve.wait_ge(S.x_turned, q + 1)
                v.tensor_copy(R[:, 4 * q:4 * q + 4, :], ps[:, 0:4, 0:T]).then_inc(S.x_taken, 1)
                if q:
                    dve.wait_ge(S.x_taken, 2)
                    dve.wait_ge(S.x_taken_odd, 1)
                    own(TT(gu[:, :, :], R[:, 0:4, :], R[:, 4:8, :], ALU.add))
                    own(TT(gu[:, :, :], gu[:, :, :], R[:, 8:12, :], ALU.add))
            dve.wait_ge(S.x_taken_odd, 2)
            own(TT(gu[:, :, :], gu[:, :, :], R[:, 12:16, :], ALU.add))
            dve.wait_ge(S.prm0_turned, 1)
            own(v.tensor_copy(prm0[:, :], ps[:, 4, 0:32]))
            norm(0, 0, first=0, ahead=RING)

            for l in range(DEPTH):
                dve.wait_ge(S.x_ready, 10 * l + 5)
                TT(rows9[:, :, :], xh[:, :, SEQ - 1:T].bitcast(F32), xl[:, :, SEQ - 1:T].bitcast(F32), ALU.add).then_inc(S.shift_cols, 1)
                dve.wait_ge(S.layer_taken, l + 1)
                own(TS(ka1[:, :], cols(l, 'rw_ka', 4), -1.0, 1.0, ALU.mult, ALU.add))
                for i in range(6, 12):
                    lo1(slab0(l, 'tail') + i)
                evacuate(slab0(l, 'in'), lambda: v.tensor_copy(ptail[:, :, :], ps[:, 4:7, 0:TW]))
                def mix(g, i):
                    b0, n = 4 * g, min(4, RW_PB - 4 * g)
                    pr, m = praw[:, b0:b0 + n, :], mx[:, b0:b0 + n, :]
                    if i == 0:
                        own(TT(m[:, :, 1:SEQ], pr[:, :, 0:SEQ - 1], pr[:, :, 1:SEQ], ALU.subtract))
                    if i == 1:
                        own(TS(m[:, :, 0:1], pr[:, :, 0:1], -1.0, None, ALU.mult))
                    if i == 2:
                        own(TT(m[:, :, SEQ:T], pr[:, :, T:TW], pr[:, :, SEQ:T], ALU.subtract))
                    if i == 3:
                        own(TT(m, m, over(cols(l, 'rw_mu', RW_PB)[:, b0:b0 + n], T), ALU.mult))
                    if i == 4:
                        own(TT(m, m, pr[:, :, 0:T], ALU.add))
                for g in range(4):
                    for i in range(8):
                        if i == 7:
                            dve.wait_ge(S.slab_used, slab0(l, 'in') + 8 * g + 8)
                            b0 = 4 * (g % 2)
                            v.tensor_copy(praw[:, 4 * g:4 * g + 4, :], ps[:, b0:b0 + 4, 0:TW]).then_inc(S.evacuated, 1)
                        lo1(slab0(l, 'in') + 8 * g + RING + i)
                        if g and i < 5:
                            mix(g - 1, i)
                        if g == 3 and i == 5:
                            dve.wait_ge(S.lora_loaded, 48 if l == 0 else 48 + 80 * l)
                        if l and g == 3 and i == 5:
                            r = slice(64, 96)
                            own(TT(tmp[r, 0, 1:SEQ], ptail[r, 2, 0:SEQ - 1], ptail[r, 2, 1:SEQ], ALU.subtract))
                            own(TS(tmp[r, 0, 0:1], ptail[r, 2, 0:1], -1.0, None, ALU.mult))
                            own(TT(tmp[r, 0, SEQ:T], ptail[r, 2, T:TW], ptail[r, 2, SEQ:T], ALU.subtract))
                            own(STT(ptail[r, 2, 0:T], tmp[r, 0, :], vmu[r, :], ptail[r, 2, 0:T], ALU.mult, ALU.add))
                    dve.wait_ge(S.evacuated, group0(l, 'in') + g + 1)

                bg = behind(l, 4, rw_plan)
                then = (lambda ins: (own(ins), bg.step()))
                for i in range(5):
                    mix(3, i)
                dve.sem_inc(S.rw_mix, 1)
                dve.wait_ge(S.shift_turned, l + 1)
                then(v.tensor_copy(pret[:, 0:2, :], praw[:, 14:16, :]))
                for name in ('in', 'a', 'g'):
                    bg.to(name)
                dve.wait_ge(S.rw_wa_taken, 2 * l + 2)
                if l:
                    dve.wait_ge(S.rw_v_first, 1)
                    bg.to('v')
                    dve.wait_ge(S.rw_v_taken, l)
                    then(TT(ep[:, :, :], vfirst[:, :, :], mx[:, 8:12, :], ALU.subtract))
                    TT(ep[:, :, :], ep[:, :, :], tmp[:, :, :], ALU.mult).then_inc(S.rw_v_used, 1)
                    dve.wait_ge(S.rw_v_used, l)
                    then(TT(mx[:, 8:12, :], mx[:, 8:12, :], ep[:, :, :], ALU.add))
                TT(mx[:, 14:18, :], mx[:, 4:8, :], over(cols(l, 'rw_kk', 4), T), ALU.mult).then_inc(S.rw_kk_raw, 1)
                for b in range(4):
                    for c in range(NCH):
                        cs = slice(CH * c, CH * c + CH)
                        then(v.tensor_tensor_scan(lw[:, b, cs], ones, lw[:, b, cs], 0.0, ALU.mult, ALU.add))
                mid = lw[:, :, 0:SEQ].rearrange("p b (c i) -> p b c i", i=CH)[:, :, :, CH // 2 - 1]
                own(TS(amid[:, :, :], mid, -DECAY, None, ALU.mult))
                TS(namid[:, :, :], mid, DECAY, None, ALU.mult).then_inc(S.rw_cum, 1)
                bg.to('kk')
                dve.wait_ge(S.rw_kk_sum, l + 1)
                dve.wait_ge(S.rw_kk_sq, l + 1)
                TS(ln_m[0:RW_HEADS, :], ps[0:RW_HEADS, 4, 0:T], 1e-24, None, ALU.max).then_inc(S.rw_kk_ss, 1)
                dve.wait_ge(S.rw_kk_norm, l + 1)
                v.reciprocal(ln_s[0:RW_HEADS, :], ln_s[0:RW_HEADS, :]).then_inc(S.rw_kk_inv, 1)
                dve.wait_ge(S.rw_kk_raw, l + 1)
                bg.to('kks')
                dve.wait_ge(S.rw_kk_spread, l + 1)
                then(TT(mx[:, 14:18, :], mx[:, 14:18, :], ps[:, 4:8, 0:T], ALU.mult))
                dve.wait_ge(S.rw_ka_done, l + 1)
                then(TT(mx[:, 4:8, :], mx[:, 4:8, :], tmp[:, :, :], ALU.mult))
                then(TT(tmp[:, :, :], mx[:, 0:4, :], mx[:, 4:8, :], ALU.mult))
                TT(tmp[:, :, :], tmp[:, :, :], over(cols(l, 'rw_rk', 4), T), ALU.mult).then_inc(S.rw_bonus_in, 1)
                then(TT(mx[:, 18:22, :], mx[:, 18:22, :], mx[:, 14:18, :], ALU.mult))
                bg.to('bonus')
                dve.wait_ge(S.rw_bonus_sum, l + 1)
                then(TT(bonus[:, :, :], ps[:, 4:8, 0:T], mx[:, 8:12, :], ALU.mult))
                dve.wait_ge(S.rw_exps, l + 1)
                then(TT(mx[:, 4:8, 0:SEQ], mx[:, 4:8, 0:SEQ], em[:, :, 0:SEQ], ALU.mult))
                then(TT(mx[:, 18:22, 0:SEQ], mx[:, 18:22, 0:SEQ], em[:, :, 0:SEQ], ALU.mult))
                then(TT(mx[:, 0:4, 0:SEQ], mx[:, 0:4, 0:SEQ], ep[:, :, 0:SEQ], ALU.mult))
                kkv = mx[:, 14:18, 0:SEQ].rearrange("p b (c i) -> p b c i", i=CH)
                epv = ep[:, :, 0:SEQ].rearrange("p b (c i) -> p b c i", i=CH)
                then(TT(kkv[:, :, :, 1:CH], kkv[:, :, :, 1:CH], epv[:, :, :, 0:CH - 1], ALU.mult))
                then(TT(kkv[:, :, :, 0], kkv[:, :, :, 0], enam[:, :, :], ALU.mult))
                v.tensor_copy(eend[:, :, :], epv[:, :, :, CH - 1]).then_inc(S.rw_scaled, 1)
                dve.wait_ge(S.rw_scaled, l + 1)

                for c in range(NCH):
                    n = NCH * l + c
                    bg.to(f'tok{c}')
                    for q in range(2):
                        bg.to(f'more{c}' if q else f'pairs{c}')
                        hs = slice(4 * q, 4 * q + 4)
                        dve.wait_ge(S.rw_pairs, 4 * n + 2 * q + 1)
                        pv_ = halves_of(4, 2 * CH, 4)
                        then(TT(pairs(ym[:, hs, :]), pv_[:, :, :, 0:CH], each2(masks[:, 2, :], 2), ALU.mult))
                        TT(pairs(qb[:, hs, :]), pv_[:, :, :, CH:2 * CH], each2(masks[:, 3, :], 2), ALU.mult).then_inc(S.rw_pairs_taken, 1)
                        then(STT(ym[:, hs, :], ym[:, hs, :], -1.0, each(ident, 4), ALU.mult, ALU.add))
                        dve.wait_ge(S.rw_pairs, 4 * n + 2 * q + 2)
                        TT(pairs(mq[:, hs, :, :].rearrange("p h a i -> p h (a i)")), halves_of(6, 2 * CH, 4),
                           each2(masks[:, 0:2, :].rearrange("p a i -> p (a i)"), 2), ALU.mult).then_inc(S.rw_pairs_taken, 1)
                    bg.to(f'l{c}')
                    dve.wait_ge(S.rw_l_kept, n + 1)
                    for q in range(2):
                        hs = slice(4 * q, 4 * q + 4)
                        TT(lmk[:, hs, :], lm[:, hs, :], each(masks[:, 6, :], 4), ALU.mult).then_inc(S.rw_masked, 1)
                    own(TT(tm[:, :, :], lm[:, :, :], each(masks[:, 5, :], RW_HEADS), ALU.mult))
                    STT(tm[:, :, :], tm[:, :, :], -1.0, each(ident, RW_HEADS), ALU.mult, ALU.add).then_inc(S.rw_t_first, 1)
                    for lev in range(6):
                        bg.to(f'x{c}.{lev}')
                        for q in range(2 if lev < 5 else 0):
                            hs = slice(4 * q, 4 * q + 4)
                            dve.wait_ge(S.rw_x, 12 * n + 2 * lev + q + 1)
                            TT(lmk[:, hs, :], lm[:, hs, :], each(masks[:, 7 + lev, :], 4), ALU.mult)
                        bg.to(f'y{c}.{lev}')
                        for q in range(2):
                            m = 12 * n + 2 * lev + q
                            hs = slice(4 * q, 4 * q + 4)
                            dve.wait_ge(S.rw_tx, m + 1)
                            yx = ps[:, 6 + q, :].rearrange("p (h i) -> p h i", i=CH)
                            TT(ym[:, hs, :], ym[:, hs, :], yx, ALU.subtract).then_inc(S.rw_masked if lev < 5 else S.rw_inverted, 1)
                    for name in ('w', 'u', 'out'):
                        bg.to(f'{name}{c}')
                    dve.wait_ge(S.rw_y, n + 1)
                    for e in range(2):
                        r = slice(64 * e, 64 * e + 64)
                        then(v.tensor_copy(yt[r, :, CH * c:CH * c + CH], ps[r, 5 + 2 * e, :].rearrange("p (b i) -> p b i", i=CH)))
                    upd = ps[:, 6, 0:256].rearrange("p (b i) -> p b i", i=64)
                    if c:
                        then(TT(zst[:, :, :], zst[:, :, :], upd, ALU.add))
                        TT(zst[:, :, :], zst[:, :, :], over(eend[:, :, c], 64), ALU.mult).then_inc(S.rw_chunk_done, 1)
                    else:
                        then(TT(zst[:, :, :], upd, over(eend[:, :, c], 64), ALU.mult))
                        TT(zst[:, :, :], zst[:, :, :], over(eamid[:, :, c + 1], 64), ALU.mult).then_inc(S.rw_chunk_done, 1)
                dve.wait_ge(S.rw_sample_loaded, 64 * (l + 1))

                def sam(b0):
                    return mx[:, b0:b0 + 4, SEQ:T].unsqueeze(3).to_broadcast([128, 4, NS, 64])
                id4 = ident2[:, :].unsqueeze(1).unsqueeze(1).to_broadcast([128, 4, NS, 64])
                TT(s1t[:, :, :, :], srw[:, :, :, :], sam(14), ALU.mult).then_inc(S.rw_sample_in, 1)
                TT(s2t[:, :, :, :], sam(8), id4, ALU.mult).then_inc(S.rw_sample_in, 1)
                then(TT(srw[:, :, :, :], srw[:, :, :, :], wsam[:, :, :].unsqueeze(3).to_broadcast([128, 4, NS, 64]), ALU.mult))
                bg.to('sa')
                dve.wait_ge(S.rw_sample_sum, 2 * l + 1)
                spread = ps[:, 4:8, :].rearrange("p a (b v) -> p a b v", v=64)
                TT(s1t[:, :, :, :], spread, sam(18), ALU.mult).then_inc(S.rw_sample_taken, 1)
                dve.wait_ge(S.rw_sample_taken, l + 1)
                then(TT(srw[:, :, :, :], srw[:, :, :, :], s1t[:, :, :, :], ALU.subtract))
                bg.to('sv')
                dve.wait_ge(S.rw_sample_sum, 2 * l + 2)
                then(TT(s1t[:, :, :, :], spread, sam(4), ALU.mult))
                TT(srw[:, :, :, :], srw[:, :, :, :], s1t[:, :, :, :], ALU.add).then_inc(S.rw_sample_new, 1)
                dve.wait_ge(S.rw_sample_new, l + 1)
                then(TT(bonus[:, :, :], bonus[:, :, :], over(cols(l, 'rw_lnx_b', 4), T), ALU.add))
                bg.to('sy')
                dve.wait_ge(S.rw_sample_y, l + 1)
                for e in range(2):
                    r = slice(64 * e, 64 * e + 64)
                    last = v.tensor_copy(yt[r, :, SEQ:T], ps[r, 5 + 2 * e, 0:4 * NS].rearrange("p (b i) -> p b i", i=NS))
                    if e == 0:
                        own(last)
                last.then_inc(S.rw_gn_in, 1)
                bg.to('gn')
                dve.wait_ge(S.rw_gn_sum, 2 * l + 1)
                STT(yt[:, :, :], ps[:, 4:8, 0:T], -1.0 / RW_HD, yt[:, :, :], ALU.mult, ALU.add).then_inc(S.rw_gn_c, 1)
                bg.to('gnss')
                dve.wait_ge(S.rw_gn_std, l + 1)
                v.reciprocal(ln_s[0:RW_HEADS, :], ln_s[0:RW_HEADS, :]).then_inc(S.rw_gn_inv, 1)
                bg.to('gnsp')
                dve.wait_ge(S.rw_gn_spread, l + 1)
                own(TT(yt[:, :, :], yt[:, :, :], ps[:, 4:8, 0:T], ALU.mult))
                for b in range(4):
                    last = STT(yt[:, b, :], yt[:, b, :], col(l, 'rw_lnx_g', b), bonus[:, b, :], ALU.mult, ALU.add)
                own(last)
                TT(yt[:, :, :], yt[:, :, :], gate[:, :, :], ALU.mult).then_inc(S.rw_out, 1)
                dve.wait_ge(S.rw_out_hi, l + 1)
                TT(ol[:, 0:4, :], yt[:, :, :], oh[:, 0:4, :].bitcast(F32), ALU.subtract).then_inc(S.rw_done, 1)

                bg.to('end')

                bg = behind(l, 8, ret_plan)
                dve.wait_ge(S.evacuated, group0(l, 'in') + 8)
                dve.wait_ge(S.rdec_loaded, 32 * (l + 1))
                TT(kw[:, :, SEQ:T], pret[:, 0:AP_, SEQ:T], pret[:, 0:AP_, SEQ:T], ALU.add).then_inc(S.ret_in, 1)
                bg.to('swap')
                dve.wait_ge(S.ret_swapped, 2 * l + 1)
                TT(rtmp[:, 0:4, :], ps[:, 4:8, 0:T], each(rrot[:, 1, :], 4), ALU.mult).then_inc(S.ret_swap_taken, 1)
                bg.to('swap1')
                dve.wait_ge(S.ret_swapped, 2 * l + 2)
                dve.wait_ge(S.ret_swap_taken, l + 1)
                then(TT(rtmp[:, 4:6, :], ps[:, 4:6, 0:T], each(rrot[:, 1, :], 2), ALU.mult))
                then(TT(pret[:, 0:6, 0:T], pret[:, 0:6, 0:T], each(rrot[:, 0, :], AH), ALU.mult))
                then(TT(pret[:, 0:6, 0:T], pret[:, 0:6, 0:T], rtmp[:, :, :], ALU.add))
                then(TS(pret[:, 3:6, 0:T], pret[:, 3:6, 0:T], 0.125, None, ALU.mult))
                for dst, b0, t0 in ((qs, 0, AH), (kw, AP_, AH + AP_)):
                    for c in range(NCH):
                        cs = slice(CH * c, CH * c + CH)
                        last = TT(dst[:, :, cs], pret[:, b0:b0 + AP_, cs], rdec[:, t0:t0 + AP_, :], ALU.mult)
                last.then_inc(S.a_prepared, 1)
                attention(l, False, 2 * l, bg)

                dve.wait_ge(S.ret_stored, 64 * (l + 1))
                dve.wait_ge(S.evacuated, group0(l, 'in') + 12)
                bg = Parts(ml_plan, lambda i: out_part(l, i))
                then = (lambda ins: (own(ins), bg.step()))
                dve.wait_ge(S.mlb_loaded, 32 * (l + 1))
                own(TS(mlb2[:, :], mlb[:, :], 1.0 / CAP, None, ALU.mult))
                own(v.tensor_copy(rows[:, 0, :], ptail[0:AH, 2, 0:T]))
                v.tensor_copy(rows[:, 1, :], ptail[32:32 + AH, 2, 0:T]).then_inc(S.m_gates_in, 1)
                own(TS(pml[:, AP_:2 * AP_, 0:T], pml[:, AP_:2 * AP_, 0:T], 0.125, None, ALU.mult))
                dve.wait_ge(S.m_logf, l + 1)
                for c in range(NCH):
                    cs = slice(CH * c, CH * c + CH)
                    own(v.tensor_tensor_scan(rows[:, 2, cs], ones[0:AH, :], rows[:, 1, cs], 0.0, ALU.mult, ALU.add))
                own(v.tensor_copy(rows[:, 2, SEQ:T], rows[:, 1, SEQ:T]))
                STT(rows[:, 0, :], rows[:, 0, :], CAP, rows[:, 2, :], ALU.mult, ALU.subtract).then_inc(S.m_rows_c, 1)
                bg.to('rows')
                dve.wait_ge(S.m_rows_c, l + 1)
                dve.wait_ge(S.m_m_loaded, 16 * (l + 1))
                then(v.memset(rows[:, 4, 0:CH], 0.0))
                for c in range(NCH):
                    cs = slice(CH * c, CH * c + CH)
                    then(v.tensor_tensor_scan(rows[:, 3, cs], rows[:, 0, cs], rows[:, 0, cs], mcol[:, :] if c else 0.0, ALU.max, ALU.max))
                    if c + 1 < NCH:
                        then(TT(mcol[:, :], rows[:, 2, CH * c + CH - 1:CH * c + CH], rows[:, 3, CH * c + CH - 1:CH * c + CH], ALU.add))
                        then(v.tensor_copy(rows[:, 4, CH * c + CH:CH * c + 2 * CH], mcol[:, :].to_broadcast([AH, CH])))
                TT(rows[:, 3, SEQ:T], rows[:, 0, SEQ:T], rows[:, 4, SEQ:T], ALU.max).then_inc(S.m_rows_m, 1)
                dve.wait_ge(S.m_rows_m, l + 1)
                then(TT(rows[:, 2, :], rows[:, 2, :], rows[:, 3, :], ALU.add))
                then(v.tensor_copy(mfin[:, 0:NS], rows[:, 2, SEQ:T]))
                then(v.tensor_copy(mfin[:, NS:NS + 1], rows[:, 2, SEQ - 1:SEQ]))
                for c in range(NCH):
                    cs = slice(CH * c, CH * c + CH)
                    then(TS(rows[:, 1, cs], rows[:, 0, cs], rows[:, 3, CH * c + CH - 1:CH * c + CH], None, ALU.subtract))
                then(TT(rows[:, 1, SEQ:T], rows[:, 0, SEQ:T], rows[:, 3, SEQ:T], ALU.subtract))
                TT(rows[:, 4, :], rows[:, 4, :], rows[:, 3, :], ALU.subtract).then_inc(S.m_rows_x, 1)
                bg.to('spread_m')
                dve.wait_ge(S.m_spread, 2 * l + 1)
                then(v.tensor_copy(mct[:, :, :], ps[:, 7, 0:16].rearrange("p (c h) -> p c h", h=8)[:, :, 0:AH]))
                negm = masks[:, 4, :].unsqueeze(1).unsqueeze(1).to_broadcast([128, AH, NCH, CH])
                TT(ssb[:, :, :, :].rearrange("p c h i -> p h c i"), negm,
                   ps[:, 4:7, :].rearrange("p a (e c i) -> p (a e) c i", c=NCH, i=CH), ALU.subtract).then_inc(S.m_exp_in, 1)
                bg.to('spread_e')
                dve.wait_ge(S.m_spread, 2 * l + 2)
                sampled = ps[:, 7, 0:16 * AP_].rearrange("p (a w s) -> p a w s", w=2, s=NS)
                then(TT(kw[:, :, 0:SEQ], pml[:, AP_:2 * AP_, 0:SEQ], ps[:, 4:7, SEQ:2 * SEQ], ALU.mult))
                own(TT(kw[:, :, SEQ:T], pml[:, AP_:2 * AP_, SEQ:T], sampled[:, :, 1, :], ALU.mult))
                own(v.tensor_copy(msk[:, :, :], sampled[:, :, 0, :]))
                own(v.tensor_copy(mdc[:, :], ps[:, 4:7, SEQ - 1]))
                TT(qs[:, :, 0:SEQ], pml[:, 0:AP_, 0:SEQ], ps[:, 4:7, 0:SEQ], ALU.mult).then_inc(S.a_prepared, 1)
                then(v.tensor_reduce(mnc[:, :, :].rearrange("p c a -> p a c"),
                                    kw[:, :, 0:SEQ].rearrange("p a (c i) -> p a c i", i=CH), AX.X, ALU.add))
                dve.wait_ge(S.a_prepared, 2 * l + 2)
                TT(mnq[:, :, :], qs[:, :, CH:SEQ], over(mnc[:, 0, :], CH), ALU.mult).then_inc(S.m_nq, 1)
                then(TT(mnt[:, :], mnc[:, 0, :], mdc[:, :], ALU.mult))
                then(TT(mnc[:, 1, :], mnc[:, 1, :], mnt[:, :], ALU.add))
                attention(l, True, 2 * l + 1, bg)

                dve.wait_ge(S.a_done, 2 * l + 2)
                for i in range(OUT_A, 32):
                    out_part(l, i)
                norm(2 * l + 1, l + 1 if l + 1 < DEPTH else None)
                dve.wait_ge(S.x_ready, 10 * l + 10)
                dve.wait_ge(S.ml_stored, 160 * (l + 1))

                with dve.Fori(0, FF_GROUPS) as it:
                    s = it * 16 + slab0(l, 'up')
                    lo4(s + 4)
                    lo4(s + 8)
                    dve.wait_ge(S.gate_sig, it + (l * FF_GROUPS + 1))
                    TT(gu[:, :, :], sg[:, :, :], ps[:, 0:4, 0:T], ALU.mult).then_inc(S.evacuated, 1)
                    dve.wait_ge(S.evacuated, it * 2 + (group0(l, 'up') + 1))
                    dve.sem_inc(S.gated, 1)
                    lo4(s + 12)
                    lo4(s + 16)
                    dve.wait_ge(S.slab_used, s + 16)
                    TT(gu[:, :, :], gu[:, :, :], ps[:, 4:8, 0:T], ALU.mult).then_inc(S.evacuated, 1)
                    dve.wait_ge(S.evacuated, it * 2 + (group0(l, 'up') + 2))
                    v.tensor_copy(hh[:, ds(it * 4, 4), :], gu[:, :, :]).then_inc(S.hidden_hi, 1)
                    dve.wait_ge(S.hidden_hi, it + (l * FF_GROUPS + 1))
                    TT(hl[:, ds(it * 4, 4), :], gu[:, :, :], hh[:, ds(it * 4, 4), :].bitcast(F32), ALU.subtract).then_inc(S.hidden_ready, 1)

                def down(s, blk, before, g, more):
                    for k in range(4, 24, 4):
                        lo4(s + k)
                    residual_x(blk, before)
                    residual_group(s + DOWN_SLABS, blk, 0, before, g + 1)
                    for k in range(24, 44, 4):
                        lo4(s + k)
                    residual_x(blk + 4, before + 1)
                    if more:
                        lo4(s + 44, range(3))
                    residual_group(s + 2 * DOWN_SLABS, blk + 4, 4, before + 1, g + 2)
                    if more:
                        lo4(s + 44, (3,))
                g = group0(l, 'down')
                dve.wait_ge(S.hidden_ready, FF_GROUPS * (l + 1))
                own(v.memset(gu[:, :, :], 0.0))
                if l + 1 < DEPTH:
                    with dve.Fori(0, 2) as it:
                        down(it * (2 * DOWN_SLABS) + slab0(l, 'down'), it * 8, it * 2 + 4 * l, it * 2 + g, True)
                else:
                    down(slab0(l, 'down'), 0, 4 * l, g, True)
                    down(slab0(l, 'down') + 2 * DOWN_SLABS, 8, 4 * l + 2, g + 2, False)
                norm(2 * l + 2, last=l + 1 == DEPTH, ahead=slab0(l + 1, 'tail') + RING if l + 1 < DEPTH else None)


_NAMES = ['x_prompt', 'x_sample', 'state_rw_shift', 'state_rw_wkv', 'state_ret', 'state_ml_c', 'state_ml_n', 'state_ml_m',
          'ln0_g', 'ln0_b', 'w_in', 'rw_mu', 'rw_w0', 'rw_w2', 'rw_a0', 'rw_a2', 'rw_g2', 'rw_kk', 'rw_ka', 'rw_rk',
          'rw_lnx_g', 'rw_lnx_b', 'rw_v0', 'rw_v1', 'rw_vmu', 'rw_v2', 'ml_ib', 'ml_fb', 'ml_norm', 'w_out',
          'ln1_g', 'ln1_b', 'w_gate', 'w_up', 'w_down', 'ln2_g', 'ln2_b']
_OUTS = [('y_prompt', (1, SEQ, D)), ('y_sample', (NS, 1, D)),
         ('p_shift', (DEPTH, 1, D)), ('p_wkv', (DEPTH, 1, RW_HEADS, RW_HD, RW_HD)), ('p_ret', (DEPTH, 1, AH, 64, AV)),
         ('p_mlc', (DEPTH, 1, AH, 64, AV)), ('p_mln', (DEPTH, 1, AH, 64)), ('p_mlm', (DEPTH, 1, AH)),
         ('s_shift', (DEPTH, NS, D)), ('s_wkv', (DEPTH, NS, RW_HEADS, RW_HD, RW_HD)), ('s_ret', (DEPTH, NS, AH, 64, AV)),
         ('s_mlc', (DEPTH, NS, AH, 64, AV)), ('s_mln', (DEPTH, NS, AH, 64)), ('s_mlm', (DEPTH, NS, AH))]


def kernel(**inputs):
    from concourse import bacc
    from concourse.bass_utils import run_bass_kernel_spmd

    nc = bacc.Bacc("TRN2", target_bir_lowering=False, num_devices=1, dynamic_dma_scratch_size=64)
    arrays, a = {}, {}
    for name in _NAMES:
        arrays["in_" + name] = np.ascontiguousarray(inputs[name])
    for name, table in constants().items():
        arrays["in_" + name] = table
    for name, x in arrays.items():
        a[name[3:]] = nc.dram_tensor(name, x.shape, mybir.dt.from_np(x.dtype), kind="ExternalInput").ap()
    o = {name: nc.dram_tensor("out_" + name, shape, F32, kind="ExternalOutput").ap() for name, shape in _OUTS}
    build(nc, a, o)
    r = run_bass_kernel_spmd(nc, [arrays], core_ids=[0])
    return tuple(r.results[0]["out_" + name] for name, _ in _OUTS)
```
